# Optimizing a Trainium2 kernel written in Bass

```python
import math
import jax, jax.numpy as jnp
from jax import lax
import numpy as np

D_MODEL = 1024
BATCH = 1
SEQ = 1024
DEPTH = 1

HEAD_DIM = 64
MIX_WIDTH = D_MODEL
NSA_HEADS = (MIX_WIDTH // 2) // HEAD_DIM
NSA_KV_GROUPS = 2
NSA_GROUP_SIZE = NSA_HEADS // NSA_KV_GROUPS
NSA_WIDTH = NSA_HEADS * HEAD_DIM
NSA_KV_WIDTH = NSA_KV_GROUPS * HEAD_DIM
CMP_BLOCK = 32
CMP_STRIDE = 16
CMP_HIDDEN = 256
SEL_BLOCK = 64
SEL_TOPK = 16
SEL_FORCE = 1e4
WINDOW = 512
Q_BLOCK = 128
RWKV_HEADS = (MIX_WIDTH - NSA_WIDTH) // HEAD_DIM
RWKV_WIDTH = RWKV_HEADS * HEAD_DIM
DECAY_LORA = 64
AAA_LORA = 64
GATE_LORA = 128
RWKV_GN_EPS = 64e-5
D_FF = 2816
MEM_TOKENS = 256
MEM_HEADS = 4
MEM_HEAD_DIM = D_MODEL // MEM_HEADS
ROPE_THETA = 10000.0
NORM_EPS = 1e-6
NEG_INF = -1e30

NSA_SPLITS = (NSA_WIDTH,) + (NSA_KV_WIDTH,) * 6 + (3 * NSA_HEADS,)
RWKV_SPLITS = (RWKV_WIDTH,) * 3 + (DECAY_LORA, AAA_LORA, GATE_LORA)
NSA_COLS = sum(NSA_SPLITS)
RWKV_COLS = sum(RWKV_SPLITS)
IN_COLS = NSA_COLS + RWKV_COLS

kernel_name = 'hybrid_nsa_rwkv7_macaron_block'

def rms_norm(x, g):
    xf = x.astype(jnp.float32)
    y = xf * lax.rsqrt(jnp.mean(xf * xf, -1, keepdims=True) + NORM_EPS)
    return (y * g.astype(jnp.float32)).astype(x.dtype)

def swiglu(x, w_gate, w_up, w_down):
    return (jax.nn.silu(x @ w_gate) * (x @ w_up)) @ w_down

def rope(x, pos):
    half = x.shape[-1] // 2
    inv = ROPE_THETA ** (-jnp.arange(half, dtype=jnp.float32) / half)
    ang = pos.astype(jnp.float32)[:, None] * inv[None, :]
    cos, sin = jnp.cos(ang).astype(x.dtype), jnp.sin(ang).astype(x.dtype)
    x1, x2 = x[..., :half], x[..., half:]
    return jnp.concatenate([x1 * cos - x2 * sin, x1 * sin + x2 * cos], -1)

def masked_softmax(s, mask):
    s = jnp.where(mask, s.astype(jnp.float32), NEG_INF)
    m = jnp.max(s, -1, keepdims=True)
    e = jnp.where(mask, jnp.exp(s - m), 0.0)
    return e / jnp.maximum(jnp.sum(e, -1, keepdims=True), 1e-30)

def split_cols(z, sizes):
    return jnp.split(z, np.cumsum(sizes)[:-1].tolist(), axis=-1)

def compress_blocks(kv, pe, w1, w2):
    T = kv.shape[2]
    n_cmp = (T - CMP_BLOCK) // CMP_STRIDE + 1
    idx = np.arange(n_cmp)[:, None] * CMP_STRIDE + np.arange(CMP_BLOCK)[None, :]
    blocks = kv[:, :, idx, :] + pe
    flat = blocks.reshape(blocks.shape[:3] + (CMP_BLOCK * HEAD_DIM,))
    return jax.nn.silu(flat @ w1) @ w2

def nsa_mixer(q, k_cmp, v_cmp, k_slc, v_slc, k_win, v_win, gate_logits,
              pe_k, w1_k, w2_k, pe_v, w1_v, w2_v):
    B, T, _ = q.shape
    G, R, dh = NSA_KV_GROUPS, NSA_GROUP_SIZE, HEAD_DIM
    pos = jnp.arange(T)
    qh = rope(q.reshape(B, T, G, R, dh).transpose(0, 2, 3, 1, 4), pos)

    def kv_heads(z):
        return z.reshape(B, T, G, dh).transpose(0, 2, 1, 3)

    n_cmp = (T - CMP_BLOCK) // CMP_STRIDE + 1
    cmp_start = np.arange(n_cmp) * CMP_STRIDE
    cmp_end = jnp.asarray(cmp_start + CMP_BLOCK - 1)
    kc = rope(compress_blocks(kv_heads(k_cmp), pe_k, w1_k, w2_k), cmp_end)
    vc = compress_blocks(kv_heads(v_cmp), pe_v, w1_v, w2_v)

    n_sel = T // SEL_BLOCK
    n_top = min(SEL_TOPK, n_sel)
    sel_start = np.arange(n_sel) * SEL_BLOCK
    overlap = jnp.asarray(((cmp_start[:, None] < sel_start[None, :] + SEL_BLOCK)
                           & (cmp_start[:, None] + CMP_BLOCK > sel_start[None, :])).astype(np.float32))
    ks_blocks = rope(kv_heads(k_slc), pos).reshape(B, G, n_sel, SEL_BLOCK, dh)
    vs_blocks = kv_heads(v_slc).reshape(B, G, n_sel, SEL_BLOCK, dh)
    pad = ((0, 0), (0, 0), (WINDOW, 0), (0, 0))
    kw_pad = jnp.pad(rope(kv_heads(k_win), pos), pad)
    vw_pad = jnp.pad(kv_heads(v_win), pad)
    gates = jax.nn.sigmoid(gate_logits).reshape(B, T, G, R, 3).transpose(0, 2, 3, 1, 4)
    scale = HEAD_DIM ** -0.5
    gather_blocks = jax.vmap(jax.vmap(lambda blocks, ids: blocks[ids]))
    sel_ids = jnp.arange(n_sel)

    def query_block(i):
        q0 = i * Q_BLOCK
        t = q0 + jnp.arange(Q_BLOCK)
        qb = lax.dynamic_slice_in_dim(qh, q0, Q_BLOCK, axis=3)
        gb = lax.dynamic_slice_in_dim(gates, q0, Q_BLOCK, axis=3)
        s_c = jnp.einsum('bgrqd,bgcd->bgrqc', qb, kc) * scale
        p_c = masked_softmax(s_c, cmp_end[None, :] <= t[:, None])
        o_c = jnp.einsum('bgrqc,bgcd->bgrqd', p_c.astype(vc.dtype), vc)
        imp = jnp.einsum('bgrqc,cs->bgqs', p_c, overlap)
        cur = (t // SEL_BLOCK)[:, None]
        forced = (sel_ids == 0) | (sel_ids == cur) | (sel_ids == cur - 1)
        score = jnp.where(forced, SEL_FORCE, jnp.where(sel_ids <= cur, imp, -SEL_FORCE))
        _, top = lax.top_k(score, n_top)
        ks = gather_blocks(ks_blocks, top).reshape(B, G, Q_BLOCK, n_top * SEL_BLOCK, dh)
        vs = gather_blocks(vs_blocks, top).reshape(B, G, Q_BLOCK, n_top * SEL_BLOCK, dh)
        pos_s = (top[..., None] * SEL_BLOCK + jnp.arange(SEL_BLOCK)).reshape(B, G, 1, Q_BLOCK, n_top * SEL_BLOCK)
        s_s = jnp.einsum('bgrqd,bgqkd->bgrqk', qb, ks) * scale
        p_s = masked_softmax(s_s, pos_s <= t[:, None])
        o_s = jnp.einsum('bgrqk,bgqkd->bgrqd', p_s.astype(vs.dtype), vs)
        kw = lax.dynamic_slice_in_dim(kw_pad, q0, Q_BLOCK + WINDOW, axis=2)
        vw = lax.dynamic_slice_in_dim(vw_pad, q0, Q_BLOCK + WINDOW, axis=2)
        pos_w = q0 - WINDOW + jnp.arange(Q_BLOCK + WINDOW)
        rel = t[:, None] - pos_w[None, :]
        s_w = jnp.einsum('bgrqd,bgkd->bgrqk', qb, kw) * scale
        p_w = masked_softmax(s_w, (pos_w[None, :] >= 0) & (rel >= 0) & (rel < WINDOW))
        o_w = jnp.einsum('bgrqk,bgkd->bgrqd', p_w.astype(vw.dtype), vw)
        return gb[..., 0:1] * o_c + gb[..., 1:2] * o_s + gb[..., 2:3] * o_w

    out = lax.map(query_block, jnp.arange(T // Q_BLOCK))
    return out.transpose(1, 0, 4, 2, 3, 5).reshape(B, T, NSA_WIDTH)

def rwkv7_mixer(r, k, v, w_lo, a_lo, g_lo, w0, w2, a0, a2, g2, k_k, k_a, r_k, gn_g, gn_b):
    B, T, C = r.shape
    H, N = RWKV_HEADS, HEAD_DIM
    f32 = jnp.float32
    w = -jax.nn.softplus(-(w0 + jnp.tanh(w_lo) @ w2)) - 0.5
    decay = jnp.exp(-jnp.exp(w.astype(f32)))
    a = jax.nn.sigmoid(a0 + a_lo @ a2)
    g = jax.nn.sigmoid(g_lo) @ g2
    kk = (k * k_k).astype(f32).reshape(B, T, H, N)
    kk = kk / jnp.maximum(jnp.sqrt(jnp.sum(kk * kk, -1, keepdims=True)), 1e-12)
    k = k * (1 + (a - 1) * k_a)

    def heads(z):
        return z.astype(f32).reshape(B, T, H, N).transpose(1, 0, 2, 3)

    def step(state, inp):
        r_t, w_t, k_t, v_t, kk_t, a_t = inp
        sa = jnp.einsum('bhvk,bhk->bhv', state, -kk_t)
        state = (state * w_t[:, :, None, :] + sa[..., None] * (kk_t * a_t)[:, :, None, :]
                 + v_t[..., None] * k_t[:, :, None, :])
        return state, jnp.einsum('bhvk,bhk->bhv', state, r_t)

    state0 = jnp.zeros((B, H, N, N), f32)
    _, y = lax.scan(step, state0, (heads(r), heads(decay), heads(k), heads(v),
                                   kk.transpose(1, 0, 2, 3), heads(a)))
    y = y.transpose(1, 0, 2, 3)
    mu = jnp.mean(y, -1, keepdims=True)
    var = jnp.mean(jnp.square(y - mu), -1, keepdims=True)
    y = ((y - mu) * lax.rsqrt(var + RWKV_GN_EPS)).reshape(B, T, C)
    y = y * gn_g.astype(f32) + gn_b.astype(f32)
    bonus = (jnp.sum((r * k * r_k).astype(f32).reshape(B, T, H, N), -1, keepdims=True)
             * v.astype(f32).reshape(B, T, H, N)).reshape(B, T, C)
    return (y + bonus).astype(r.dtype) * g

def memory_cross_attention(h, m, wq, wk, wv, wo):
    B, T, _ = h.shape
    M = m.shape[1]
    q = (h @ wq).reshape(B, T, MEM_HEADS, MEM_HEAD_DIM)
    k = (m @ wk).reshape(B, M, MEM_HEADS, MEM_HEAD_DIM)
    v = (m @ wv).reshape(B, M, MEM_HEADS, MEM_HEAD_DIM)
    s = jnp.einsum('bqhd,bkhd->bhqk', q, k) * (MEM_HEAD_DIM ** -0.5)
    p = jax.nn.softmax(s.astype(jnp.float32), axis=-1).astype(v.dtype)
    o = jnp.einsum('bhqk,bkhd->bqhd', p, v).reshape(B, T, D_MODEL)
    return o @ wo

def setup_inputs(seed: int = 0) -> dict:
    key = jax.random.key(seed)
    L = DEPTH
    specs = [
        ('x', (BATCH, SEQ, D_MODEL), 'normal', 1.0),
        ('mem', (BATCH, MEM_TOKENS, D_MODEL), 'normal', 1.0),
        ('ffn1_pre_g', (L, D_MODEL), 'gain', 0.02),
        ('ffn1_w_gate', (L, D_MODEL, D_FF), 'normal', D_MODEL ** -0.5),
        ('ffn1_w_up', (L, D_MODEL, D_FF), 'normal', D_MODEL ** -0.5),
        ('ffn1_w_down', (L, D_FF, D_MODEL), 'normal', D_FF ** -0.5),
        ('ffn1_post_g', (L, D_MODEL), 'gain', 0.02),
        ('mix_pre_g', (L, D_MODEL), 'gain', 0.02),
        ('w_in', (L, D_MODEL, IN_COLS), 'normal', D_MODEL ** -0.5),
        ('cmp_pe_k', (L, CMP_BLOCK, HEAD_DIM), 'normal', 0.1),
        ('cmp_w1_k', (L, CMP_BLOCK * HEAD_DIM, CMP_HIDDEN), 'normal', (CMP_BLOCK * HEAD_DIM) ** -0.5),
        ('cmp_w2_k', (L, CMP_HIDDEN, HEAD_DIM), 'normal', CMP_HIDDEN ** -0.5),
        ('cmp_pe_v', (L, CMP_BLOCK, HEAD_DIM), 'normal', 0.1),
        ('cmp_w1_v', (L, CMP_BLOCK * HEAD_DIM, CMP_HIDDEN), 'normal', (CMP_BLOCK * HEAD_DIM) ** -0.5),
        ('cmp_w2_v', (L, CMP_HIDDEN, HEAD_DIM), 'normal', CMP_HIDDEN ** -0.5),
        ('nsa_out_g', (L, NSA_WIDTH), 'gain', 0.02),
        ('rwkv_mu', (L, RWKV_COLS), 'uniform', (0.0, 1.0)),
        ('rwkv_w0', (L, RWKV_WIDTH), 'uniform', (-5.0, 1.0)),
        ('rwkv_w2', (L, DECAY_LORA, RWKV_WIDTH), 'normal', DECAY_LORA ** -0.5),
        ('rwkv_a0', (L, RWKV_WIDTH), 'normal', 0.1),
        ('rwkv_a2', (L, AAA_LORA, RWKV_WIDTH), 'normal', AAA_LORA ** -0.5),
        ('rwkv_g2', (L, GATE_LORA, RWKV_WIDTH), 'normal', GATE_LORA ** -0.5),
        ('rwkv_k_k', (L, RWKV_WIDTH), 'uniform', (0.7, 1.0)),
        ('rwkv_k_a', (L, RWKV_WIDTH), 'uniform', (0.8, 1.2)),
        ('rwkv_r_k', (L, RWKV_WIDTH), 'normal', 0.1),
        ('rwkv_gn_g', (L, RWKV_WIDTH), 'gain', 0.02),
        ('rwkv_gn_b', (L, RWKV_WIDTH), 'normal', 0.02),
        ('w_out', (L, MIX_WIDTH, D_MODEL), 'normal', MIX_WIDTH ** -0.5),
        ('mix_post_g', (L, D_MODEL), 'gain', 0.02),
        ('mem_pre_g', (L, D_MODEL), 'gain', 0.02),
        ('mem_kv_g', (L, D_MODEL), 'gain', 0.02),
        ('mem_wq', (L, D_MODEL, D_MODEL), 'normal', D_MODEL ** -0.5),
        ('mem_wk', (L, D_MODEL, D_MODEL), 'normal', D_MODEL ** -0.5),
        ('mem_wv', (L, D_MODEL, D_MODEL), 'normal', D_MODEL ** -0.5),
        ('mem_wo', (L, D_MODEL, D_MODEL), 'normal', D_MODEL ** -0.5),
        ('mem_post_g', (L, D_MODEL), 'gain', 0.02),
        ('ffn2_pre_g', (L, D_MODEL), 'gain', 0.02),
        ('ffn2_w_gate', (L, D_MODEL, D_FF), 'normal', D_MODEL ** -0.5),
        ('ffn2_w_up', (L, D_MODEL, D_FF), 'normal', D_MODEL ** -0.5),
        ('ffn2_w_down', (L, D_FF, D_MODEL), 'normal', D_FF ** -0.5),
        ('ffn2_post_g', (L, D_MODEL), 'gain', 0.02),
    ]
    keys = jax.random.split(key, len(specs))
    out = {}
    for kk, (name, shape, kind, p) in zip(keys, specs):
        if kind == 'normal':
            out[name] = p * jax.random.normal(kk, shape, jnp.float32)
        elif kind == 'gain':
            out[name] = 1.0 + p * jax.random.normal(kk, shape, jnp.float32)
        else:
            out[name] = jax.random.uniform(kk, shape, jnp.float32, p[0], p[1])
    return out

def reference(x, mem,
              ffn1_pre_g, ffn1_w_gate, ffn1_w_up, ffn1_w_down, ffn1_post_g,
              mix_pre_g, w_in, cmp_pe_k, cmp_w1_k, cmp_w2_k, cmp_pe_v, cmp_w1_v, cmp_w2_v, nsa_out_g,
              rwkv_mu, rwkv_w0, rwkv_w2, rwkv_a0, rwkv_a2, rwkv_g2, rwkv_k_k, rwkv_k_a, rwkv_r_k,
              rwkv_gn_g, rwkv_gn_b, w_out, mix_post_g,
              mem_pre_g, mem_kv_g, mem_wq, mem_wk, mem_wv, mem_wo, mem_post_g,
              ffn2_pre_g, ffn2_w_gate, ffn2_w_up, ffn2_w_down, ffn2_post_g):
    for l in range(DEPTH):
        h = rms_norm(x, ffn1_pre_g[l])
        x = x + 0.5 * rms_norm(swiglu(h, ffn1_w_gate[l], ffn1_w_up[l], ffn1_w_down[l]), ffn1_post_g[l])
        h = rms_norm(x, mix_pre_g[l])
        proj = h @ w_in[l]
        nsa_cols, rwkv_cols = proj[..., :NSA_COLS], proj[..., NSA_COLS:]
        prev = jnp.pad(rwkv_cols, ((0, 0), (1, 0), (0, 0)))[:, :-1]
        rwkv_cols = rwkv_cols + (prev - rwkv_cols) * rwkv_mu[l]
        q, k_c, v_c, k_s, v_s, k_w, v_w, gate_logits = split_cols(nsa_cols, NSA_SPLITS)
        r, k, v, w_lo, a_lo, g_lo = split_cols(rwkv_cols, RWKV_SPLITS)
        o_nsa = nsa_mixer(q, k_c, v_c, k_s, v_s, k_w, v_w, gate_logits,
                          cmp_pe_k[l], cmp_w1_k[l], cmp_w2_k[l], cmp_pe_v[l], cmp_w1_v[l], cmp_w2_v[l])
        o_rwkv = rwkv7_mixer(r, k, v, w_lo, a_lo, g_lo, rwkv_w0[l], rwkv_w2[l], rwkv_a0[l], rwkv_a2[l],
                             rwkv_g2[l], rwkv_k_k[l], rwkv_k_a[l], rwkv_r_k[l], rwkv_gn_g[l], rwkv_gn_b[l])
        mixed = jnp.concatenate([rms_norm(o_nsa, nsa_out_g[l]), o_rwkv], -1) @ w_out[l]
        x = x + rms_norm(mixed, mix_post_g[l])
        h = rms_norm(x, mem_pre_g[l])
        m = rms_norm(mem, mem_kv_g[l])
        x = x + rms_norm(memory_cross_attention(h, m, mem_wq[l], mem_wk[l], mem_wv[l], mem_wo[l]), mem_post_g[l])
        h = rms_norm(x, ffn2_pre_g[l])
        x = x + 0.5 * rms_norm(swiglu(h, ffn2_w_gate[l], ffn2_w_up[l], ffn2_w_down[l]), ffn2_post_g[l])
    return x


_drawn_inputs = setup_inputs


def setup_inputs(seed=0):
    import zlib

    import numpy as np

    out = dict(_drawn_inputs(seed))
    spreads = {}
    factors = {'ffn1_pre_g': 3.627,
     'ffn1_post_g': 5.139,
     'mix_pre_g': 3.119,
     'cmp_pe_k': 3.732,
     'nsa_out_g': 4.887,
     'rwkv_w2': 2.702,
     'rwkv_a0': 4.892,
     'rwkv_k_k': 2.914,
     'rwkv_gn_g': 8.0,
     'rwkv_gn_b': 8.0,
     'mix_post_g': 3.987,
     'mem_pre_g': 5.169,
     'mem_kv_g': 3.334,
     'mem_post_g': 18.787,
     'ffn2_pre_g': 27.816,
     'ffn2_post_g': 42.2}
    for name, (base, spread) in spreads.items():
        noise = np.random.default_rng([zlib.crc32(name.encode()), seed]).standard_normal(out[name].shape)
        drawn = base * np.exp(spread * noise) if base else spread * noise
        out[name] = __import__('jax').numpy.asarray(drawn.astype(out[name].dtype))
    for name, factor in factors.items():
        out[name] = (out[name] * factor).astype(out[name].dtype)
    return out
```

```python
from contextlib import ExitStack

import numpy as np

import concourse.bass as bass
from concourse import mybir

P = 128
F32 = mybir.dt.float32
F32R = mybir.dt.float32r
BF16 = mybir.dt.bfloat16
ALU = mybir.AluOpType
ACT = mybir.ActivationFunctionType
AX_X = mybir.AxisListType.X

D = 1024
T = 1024
KD = D // P
TT = T // P
HALF = 512
NORM_EPS = 1e-6
GROUP_EPS = 64e-5


class Core:

    def __init__(self, nc):
        self.nc, self.taken = nc, []

    def sem(self, name):
        self.taken.append(self.nc.alloc_semaphore(name=name))
        return self.taken[-1]

    def sems(self, name, n):
        return [self.sem(f"{name}{i}") for i in range(n)]

    def pool_dma_sems(self, name, n):
        return [self.nc.alloc_semaphore(name=f"{name}{i}") for i in range(n)]

    def clear(self):
        nc = self.nc
        with nc.Block() as block:
            @block.sync
            def _(sp):
                for s in self.taken:
                    sp.sem_clear(s)
        for s in self.taken:
            nc.release_semaphore(s)
        self.taken = []


def sbuf(nc, ctx, name, shape, dt=F32):
    return ctx.enter_context(nc.sbuf_tensor(name, shape, dt))


def psum(nc, ctx, name, shape, dt=F32):
    return ctx.enter_context(nc.psum_tensor(name, shape, dt))


def norm_transpose(core, tag, src, gain, tiles, consts, hi, lo):
    nc = core.nc
    ident, eps = consts["ident"], consts["eps"]
    with ExitStack() as ctx:
        x = sbuf(nc, ctx, f"{tag}_x", [P, 2, D])
        xn = sbuf(nc, ctx, f"{tag}_xn", [P, 2, D])
        sq = sbuf(nc, ctx, f"{tag}_sq", [P, 2, D])
        g = sbuf(nc, ctx, f"{tag}_g", [P, KD])
        ssum = sbuf(nc, ctx, f"{tag}_ssum", [P, 2])
        root = sbuf(nc, ctx, f"{tag}_root", [P, 2])
        rstd = sbuf(nc, ctx, f"{tag}_rstd", [P, 2])
        tp = psum(nc, ctx, f"{tag}_tp", [P, 4, 4, P])
        g_loaded = core.sem(f"{tag}_g_loaded")
        x_loaded = core.sems(f"{tag}_x_loaded", 2)
        squared = core.sems(f"{tag}_squared", 2)
        rooted = core.sems(f"{tag}_rooted", 2)
        inverted = core.sems(f"{tag}_inverted", 2)
        scaled = core.sems(f"{tag}_scaled", 2)
        turned = core.sems(f"{tag}_turned", 2)
        hi_done = core.sems(f"{tag}_hi_done", 2)
        lo_done = core.sems(f"{tag}_lo_done", 2)
        block = ctx.enter_context(nc.Block())

        @block.sync
        def _(sp):
            with nc.allow_non_contiguous_dma("gain per feature"):
                sp.dma_start(g[:], gain.rearrange("(k p) -> p k", p=P)).then_inc(g_loaded, 16)
            with sp.Fori(0, tiles // 2) as i:
                for b in range(2):
                    sp.wait_ge(scaled[b], i)
                    sp.dma_start(x[:, b, :], src[bass.ds((i * 2 + b) * P, P), :]).then_inc(x_loaded[b], 16)

        @block.scalar
        def _(act):
            act.wait_ge(g_loaded, 16)
            with act.Fori(0, tiles // 2) as i:
                for b in range(2):
                    act.wait_ge(x_loaded[b], i * 16 + 16)
                    nc.scalar.activation(sq[:, b, :], x[:, b, :], ACT.Square,
                                         accum_out=ssum[:, b:b + 1]).then_inc(squared[b], 1)
                    act.wait_ge(squared[b], i + 1)
                    act.wait_ge(inverted[b], i)
                    nc.scalar.activation(root[:, b:b + 1], ssum[:, b:b + 1], ACT.Sqrt, bias=eps[:, 0:1],
                                         scale=1.0 / D).then_inc(rooted[b], 1)
                for b in range(2):
                    act.wait_ge(turned[b], i + 1)
                    for k in range(KD):
                        nc.scalar.activation(hi[:, k, bass.ds((i * 2 + b) * P, P)], tp[:, 2 * b + k // 4, k % 4, :],
                                             ACT.Copy, scale=g[:, k:k + 1]).then_inc(hi_done[b], 1)

        @block.vector
        def _(dve):
            dve.wait_ge(g_loaded, 16)
            with dve.Fori(0, tiles // 2) as i:
                for b in range(2):
                    dve.wait_ge(rooted[b], i + 1)
                    nc.vector.reciprocal(rstd[:, b:b + 1], root[:, b:b + 1]).then_inc(inverted[b], 1)
                    dve.wait_ge(inverted[b], i + 1)
                    dve.wait_ge(turned[b], i)
                    nc.vector.tensor_scalar(xn[:, b, :], x[:, b, :], rstd[:, b:b + 1], None,
                                            ALU.mult).then_inc(scaled[b], 1)
                for b in range(2):
                    dve.wait_ge(turned[b], i + 1)
                    for k in range(KD):
                        dve.wait_ge(hi_done[b], i * KD + k // 4 * 4 + 4)
                        at = (slice(None), k, bass.ds((i * 2 + b) * P, P))
                        nc.vector.scalar_tensor_tensor(
                            out=lo[at], in0=tp[:, 2 * b + k // 4, k % 4, :], scalar=g[:, k:k + 1],
                            in1=hi[at].bitcast(F32), op0=ALU.mult, op1=ALU.subtract).then_inc(lo_done[b], 1)

        @block.tensor
        def _(pe):
            with pe.Fori(0, tiles // 2) as i:
                for b in range(2):
                    pe.wait_ge(scaled[b], i + 1)
                    pe.wait_ge(lo_done[b], i * KD)
                    for k in range(KD):
                        last = nc.tensor.transpose(tp[:, 2 * b + k // 4, k % 4, :],
                                                   xn[:, b, k * P:(k + 1) * P], ident[:])
                    last.then_inc(turned[b], 1)


def ffn_products(core, tag, w_gate, w_up, w_down, hi, lo, y):
    nc = core.nc
    F = w_gate.shape[1]
    PAIRS = F // (2 * P)
    with ExitStack() as ctx:
        raw = [sbuf(nc, ctx, f"{tag}_raw{n}", [P, KD, 2 * P]) for n in "gu"]
        raw_d = sbuf(nc, ctx, f"{tag}_rawd", [P, 2, D])
        w_hi = [[sbuf(nc, ctx, f"{tag}_{n}{j}h", [P, KD, P], F32R) for n in "gu"] for j in range(2)]
        w_lo = [[sbuf(nc, ctx, f"{tag}_{n}{j}l", [P, KD, P], F32R) for n in "gu"] for j in range(2)]
        d_hi = [sbuf(nc, ctx, f"{tag}_d{j}h", [P, D], F32R) for j in range(2)]
        d_lo = [sbuf(nc, ctx, f"{tag}_d{j}l", [P, D], F32R) for j in range(2)]
        a_hi = [sbuf(nc, ctx, f"{tag}_a{j}h", [P, T], F32R) for j in range(2)]
        a_lo = [sbuf(nc, ctx, f"{tag}_a{j}l", [P, T], F32R) for j in range(2)]
        silu = sbuf(nc, ctx, f"{tag}_silu", [P, 2, HALF])
        prod = sbuf(nc, ctx, f"{tag}_prod", [P, 2, HALF])
        gate_ps = psum(nc, ctx, f"{tag}_gate_ps", [P, 2, HALF])
        up_ps = psum(nc, ctx, f"{tag}_up_ps", [P, 2, HALF])
        down_ps = psum(nc, ctx, f"{tag}_down_ps", [P, 4, HALF])
        gu_loaded = core.sem(f"{tag}_gu_loaded")
        d_loaded = core.sem(f"{tag}_d_loaded")
        gu_hi = core.sem(f"{tag}_gu_hi")
        gu_lo = core.sem(f"{tag}_gu_lo")
        dn_hi = core.sem(f"{tag}_dn_hi")
        dn_lo = core.sem(f"{tag}_dn_lo")
        gu_mm = core.sems(f"{tag}_gu_mm", 2)
        silu_done = core.sems(f"{tag}_silu_done", 2)
        prod_done = core.sems(f"{tag}_prod_done", 2)
        a_hi_done = core.sems(f"{tag}_a_hi_done", 2)
        a_ready = core.sems(f"{tag}_a_ready", 2)
        dn_mm = core.sems(f"{tag}_dn_mm", 4)
        added = core.sems(f"{tag}_added", 4)
        y_zeroed = core.sem(f"{tag}_y_zeroed")
        block = ctx.enter_context(nc.Block())

        gu_dram = [w.rearrange("(k p) n -> p k n", p=P) for w in (w_gate, w_up)]
        d_dram = w_down.rearrange("(c p) n -> p c n", p=P)

        @block.gpsimd
        def _(pool):
            nc.gpsimd.memset(y[:], 0.0).then_inc(y_zeroed, 1)

        @block.sync
        def _(sp):
            with sp.Fori(0, PAIRS) as i:
                sp.wait_ge(gu_lo, i * 4)
                for n in range(2):
                    sp.dma_start(raw[n][:], gu_dram[n][:, :, bass.ds(i * 2 * P, 2 * P)]).then_inc(gu_loaded, 16)
                sp.wait_ge(dn_lo, i * 2)
                sp.dma_start(raw_d[:], d_dram[:, bass.ds(i * 2, 2), :]).then_inc(d_loaded, 16)

        @block.scalar
        def _(act):
            def body(i, last):
                for j in range(2):
                    for h in range(2):
                        act.wait_ge(gu_mm[h], i * 2 + j + 1)
                        act.wait_ge(prod_done[h], i * 2 + j)
                        nc.scalar.activation(silu[:, h, :], gate_ps[:, h, :], ACT.Silu).then_inc(silu_done[h], 1)
                        act.wait_ge(prod_done[h], i * 2 + j + 1)
                        nc.scalar.copy(a_hi[j][:, h * HALF:(h + 1) * HALF], prod[:, h, :]).then_inc(a_hi_done[h], 1)
                        if j == 0 and h == 0:
                            act.wait_ge(d_loaded, i * 16 + 16)
                            for c in range(2):
                                nc.scalar.copy(d_hi[c][:], raw_d[:, c, :]).then_inc(dn_hi, 1)
                    if not last:
                        if j == 0:
                            act.wait_ge(gu_loaded, i * 32 + 64)
                        for n in range(2):
                            nc.scalar.copy(w_hi[j][n][:], raw[n][:, :, j * P:(j + 1) * P]).then_inc(gu_hi, 1)

            act.wait_ge(gu_loaded, 32)
            for j in range(2):
                for n in range(2):
                    nc.scalar.copy(w_hi[j][n][:], raw[n][:, :, j * P:(j + 1) * P]).then_inc(gu_hi, 1)
            with act.Fori(0, PAIRS - 1) as i:
                body(i, False)
            body(PAIRS - 1, True)

        @block.vector
        def _(dve):
            def split_lo(pair, j):
                for n in range(2):
                    dve.wait_ge(gu_hi, pair * 4 + 2 * j + n + 1)
                    nc.vector.tensor_tensor(w_lo[j][n][:], raw[n][:, :, j * P:(j + 1) * P],
                                            w_hi[j][n][:].bitcast(F32), ALU.subtract).then_inc(gu_lo, 1)

            def body(i, last):
                for j in range(2):
                    for h in range(2):
                        dve.wait_ge(silu_done[h], i * 2 + j + 1)
                        dve.wait_ge(a_ready[h], i * 2 + j)
                        nc.vector.tensor_tensor(prod[:, h, :], up_ps[:, h, :], silu[:, h, :],
                                                ALU.mult).then_inc(prod_done[h], 1)
                        dve.wait_ge(a_hi_done[h], i * 2 + j + 1)
                        at = slice(h * HALF, (h + 1) * HALF)
                        nc.vector.tensor_tensor(a_lo[j][:, at], prod[:, h, :], a_hi[j][:, at].bitcast(F32),
                                                ALU.subtract).then_inc(a_ready[h], 1)
                        if j == 0 and h == 0:
                            for c in range(2):
                                dve.wait_ge(dn_hi, i * 2 + c + 1)
                                nc.vector.tensor_tensor(d_lo[c][:], raw_d[:, c, :], d_hi[c][:].bitcast(F32),
                                                        ALU.subtract).then_inc(dn_lo, 1)
                for m in range(16):
                    t, h = m // 2, m % 2
                    at = (slice(None), t, slice(h * HALF, (h + 1) * HALF))
                    dve.wait_ge(dn_mm[m % 4], i * 4 + m // 4 + 1)
                    nc.vector.tensor_tensor(y[at], down_ps[:, m % 4, :], y[at], ALU.add).then_inc(added[m % 4], 1)
                    if m in (1, 5) and not last:
                        split_lo(i + 1, m // 4)

            split_lo(0, 0)
            split_lo(0, 1)
            dve.wait_ge(y_zeroed, 1)
            with dve.Fori(0, PAIRS - 1) as i:
                body(i, False)
            body(PAIRS - 1, True)

        @block.tensor
        def _(pe):
            def hidden(i, j, h):
                pe.wait_ge(gu_lo, i * 4 + 2 * j + 2)
                pe.wait_ge(prod_done[h], i * 2 + j)
                at = slice(h * HALF, (h + 1) * HALF)
                for k in range(KD):
                    for ps, n in ((gate_ps, 0), (up_ps, 1)):
                        nc.tensor.matmul(ps[:, h, :], w_hi[j][n][:, k, :], hi[:, k, at], start=(k == 0), stop=False)
                        nc.tensor.matmul(ps[:, h, :], w_hi[j][n][:, k, :], lo[:, k, at], start=False, stop=False)
                        mm = nc.tensor.matmul(ps[:, h, :], w_lo[j][n][:, k, :], hi[:, k, at],
                                              start=False, stop=(k == KD - 1))
                mm.then_inc(gu_mm[h], 1)

            def down(i, m):
                t, h = m // 2, m % 2
                if m == 0:
                    pe.wait_ge(dn_lo, i * 2 + 2)
                if m % 8 == 0:
                    pe.wait_ge(a_ready[m // 8], i * 2 + 2)
                pe.wait_ge(added[m % 4], i * 4 + m // 4)
                rows, cols = slice(t * P, (t + 1) * P), slice(h * HALF, (h + 1) * HALF)
                for c in range(2):
                    nc.tensor.matmul(down_ps[:, m % 4, :], a_hi[c][:, rows], d_hi[c][:, cols], start=(c == 0), stop=False)
                    nc.tensor.matmul(down_ps[:, m % 4, :], a_hi[c][:, rows], d_lo[c][:, cols], start=False, stop=False)
                    mm = nc.tensor.matmul(down_ps[:, m % 4, :], a_lo[c][:, rows], d_hi[c][:, cols],
                                          start=False, stop=(c == 1))
                mm.then_inc(dn_mm[m % 4], 1)

            with pe.Fori(0, PAIRS) as i:
                for j in range(2):
                    for h in range(2):
                        hidden(i, j, h)
                for m in range(16):
                    down(i, m)


def residual(core, tag, x_in, y, gain, factor, consts, x_out):
    nc = core.nc
    eps = consts["eps"]
    with ExitStack() as ctx:
        x = sbuf(nc, ctx, f"{tag}_x", [P, 2, D])
        sq = sbuf(nc, ctx, f"{tag}_sq", [P, 2, D])
        g = sbuf(nc, ctx, f"{tag}_g", [P, D])
        ssum = sbuf(nc, ctx, f"{tag}_ssum", [P, TT])
        root = sbuf(nc, ctx, f"{tag}_root", [P, TT])
        rstd = sbuf(nc, ctx, f"{tag}_rstd", [P, TT])
        g_loaded = core.sem(f"{tag}_g_loaded")
        x_loaded = core.sems(f"{tag}_x_loaded", 2)
        squared = core.sem(f"{tag}_squared")
        rooted = core.sem(f"{tag}_rooted")
        inverted = core.sem(f"{tag}_inverted")
        scaled = core.sem(f"{tag}_scaled")
        summed = core.sems(f"{tag}_summed", 2)
        stored = core.sems(f"{tag}_stored", 2)
        block = ctx.enter_context(nc.Block())

        @block.sync
        def _(sp):
            sp.dma_start(g[:], gain.rearrange("(o n) -> o n", o=1).broadcast_to([P, D])).then_inc(g_loaded, 16)
            with sp.Fori(0, TT // 2) as i:
                for b in range(2):
                    sp.wait_ge(stored[b], i * 16)
                    sp.dma_start(x[:, b, :], x_in[bass.ds((i * 2 + b) * P, P), :]).then_inc(x_loaded[b], 16)

        @block.scalar
        def _(act):
            for t in range(TT):
                if t >= 2:
                    act.wait_ge(squared, t - 1)
                nc.scalar.activation(sq[:, t % 2, :], y[:, t, :], ACT.Square,
                                     accum_out=ssum[:, t:t + 1]).then_inc(squared, 1)
            act.wait_ge(squared, TT)
            nc.scalar.activation(root[:], ssum[:], ACT.Sqrt, bias=eps[:, 0:1], scale=1.0 / D).then_inc(rooted, 1)
            with act.Fori(0, TT // 2) as i:
                for b in range(2):
                    act.wait_ge(summed[b], i + 1)
                    act.dma_start(x_out[bass.ds((i * 2 + b) * P, P), :], x[:, b, :]).then_inc(stored[b], 16)
            for b in range(2):
                act.wait_ge(stored[b], TT // 2 * 16)

        @block.vector
        def _(dve):
            dve.wait_ge(rooted, 1)
            dve.wait_ge(g_loaded, 16)
            nc.vector.reciprocal(rstd[:], root[:]).then_inc(inverted, 1)
            dve.wait_ge(inverted, 1)
            if factor != 1.0:
                nc.vector.tensor_scalar(rstd[:], rstd[:], factor, None, ALU.mult).then_inc(inverted, 1)
                dve.wait_ge(inverted, 2)
            for t in range(TT):
                b = t % 2
                nc.vector.scalar_tensor_tensor(out=y[:, t, :], in0=y[:, t, :], scalar=rstd[:, t:t + 1], in1=g[:],
                                               op0=ALU.mult, op1=ALU.mult).then_inc(scaled, 1)
                dve.wait_ge(scaled, t + 1)
                dve.wait_ge(x_loaded[b], 16 * (t // 2 + 1))
                nc.vector.tensor_tensor(x[:, b, :], x[:, b, :], y[:, t, :], ALU.add).then_inc(summed[b], 1)


def make_consts(core, ctx, ident_dram):
    nc = core.nc
    ident = sbuf(nc, ctx, "ident", [P, P])
    eps = sbuf(nc, ctx, "eps", [P, 2])
    loaded, set_ = core.sem("ident_loaded"), core.sem("eps_set")
    with nc.Block() as block:
        @block.sync
        def _(sp):
            sp.dma_start(ident[:], ident_dram).then_inc(loaded, 16)
            sp.wait_ge(loaded, 16)

        @block.vector
        def _(dve):
            nc.vector.memset(eps[:, 0:1], NORM_EPS).then_inc(set_, 1)
            nc.vector.memset(eps[:, 1:2], GROUP_EPS).then_inc(set_, 1)
            dve.wait_ge(set_, 2)
    return {"ident": ident, "eps": eps}


def feature_product(core, tag, w, col0, chunks, hi, lo, n, dst, row0, mix=None):
    nc = core.nc
    half = min(n, HALF)
    halves = n // half
    with ExitStack() as ctx:
        raw = sbuf(nc, ctx, f"{tag}_raw", [P, KD, 2 * P])
        w_hi = [sbuf(nc, ctx, f"{tag}_w{j}h", [P, KD, P], F32R) for j in range(2)]
        w_lo = [sbuf(nc, ctx, f"{tag}_w{j}l", [P, KD, P], F32R) for j in range(2)]
        z = [sbuf(nc, ctx, f"{tag}_z{j}", [P, n + 1]) for j in range(2)]
        if mix is not None:
            res = [sbuf(nc, ctx, f"{tag}_res{j}", [P, n]) for j in range(2)]
            dif = [sbuf(nc, ctx, f"{tag}_dif{j}", [P, n]) for j in range(2)]
            mu = sbuf(nc, ctx, f"{tag}_mu", [P, chunks])
        ps = psum(nc, ctx, f"{tag}_ps", [P, 2, 2, HALF])
        loaded = core.sem(f"{tag}_loaded")
        mu_loaded = core.sem(f"{tag}_mu_loaded")
        w_hi_done = core.sem(f"{tag}_w_hi_done")
        w_lo_done = core.sem(f"{tag}_w_lo_done")
        multiplied = core.sems(f"{tag}_multiplied", 2)
        copied = core.sems(f"{tag}_copied", 2)
        differed = core.sems(f"{tag}_differed", 2)
        mixed = core.sems(f"{tag}_mixed", 2)
        stored = core.sems(f"{tag}_stored", 2)
        zeroed = core.sem(f"{tag}_zeroed")
        block = ctx.enter_context(nc.Block())
        w_dram = w.rearrange("(k p) n -> p k n", p=P)
        pairs = chunks // 2
        done = mixed if mix is not None else copied
        out = res if mix is not None else [t[:, 1:n + 1] for t in z]

        @block.sync
        def _(sp):
            def load(i):
                sp.dma_start(raw[:], w_dram[:, :, bass.ds(i * (2 * P) + col0, 2 * P)]).then_inc(loaded, 16)

            def store(i):
                for j in range(2):
                    sp.wait_ge(done[j], i + 1)
                    sp.dma_start(dst[bass.ds(i * (2 * P) + (row0 + j * P), P), :], out[j][:] if mix is not None else out[j]
                                 ).then_inc(stored[j], 16)

            if mix is not None:
                with nc.allow_non_contiguous_dma("blend per feature"):
                    sp.dma_start(mu[:], mix.rearrange("(c p) -> p c", p=P)).then_inc(mu_loaded, 16)
            load(0)
            with sp.Fori(0, pairs - 1) as i:
                sp.wait_ge(w_lo_done, i * 2 + 2)
                load(i + 1)
                store(i)
            store(pairs - 1)
            for j in range(2):
                sp.wait_ge(stored[j], 16 * pairs)

        @block.scalar
        def _(act):
            def split_hi(j):
                nc.scalar.copy(w_hi[j][:], raw[:, :, j * P:(j + 1) * P]).then_inc(w_hi_done, 1)

            def body(i, last):
                for j in range(2):
                    act.wait_ge(multiplied[j], i + 1)
                    if mix is not None:
                        act.wait_ge(mixed[j], i)
                    else:
                        act.wait_ge(stored[j], i * 16)
                    nc.scalar.copy(z[j][:, 1:n + 1], ps[:, j, 0:halves, 0:half]).then_inc(copied[j], 1)
                    if not last:
                        if j == 0:
                            act.wait_ge(loaded, i * 16 + 32)
                        split_hi(j)

            act.wait_ge(loaded, 16)
            split_hi(0)
            split_hi(1)
            with act.Fori(0, pairs - 1) as i:
                body(i, False)
            body(pairs - 1, True)

        @block.vector
        def _(dve):
            def split_lo(i, j):
                dve.wait_ge(w_hi_done, i * 2 + j + 1)
                nc.vector.tensor_tensor(w_lo[j][:], raw[:, :, j * P:(j + 1) * P], w_hi[j][:].bitcast(F32),
                                        ALU.subtract).then_inc(w_lo_done, 1)

            def body(i, last):
                for j in range(2):
                    if mix is not None:
                        dve.wait_ge(copied[j], i + 1)
                        nc.vector.tensor_tensor(dif[j][:], z[j][:, 0:n], z[j][:, 1:n + 1],
                                                ALU.subtract).then_inc(differed[j], 1)
                        dve.wait_ge(differed[j], i + 1)
                        dve.wait_ge(stored[j], i * 16)
                        nc.vector.scalar_tensor_tensor(
                            out=res[j][:], in0=dif[j][:], scalar=mu[:, bass.ds(i * 2 + j, 1)], in1=z[j][:, 1:n + 1],
                            op0=ALU.mult, op1=ALU.add).then_inc(mixed[j], 1)
                    if not last:
                        split_lo(i + 1, j)

            if mix is not None:
                for j in range(2):
                    nc.vector.memset(z[j][:, 0:1], 0.0).then_inc(zeroed, 1)
                dve.wait_ge(zeroed, 2)
                dve.wait_ge(mu_loaded, 16)
            split_lo(0, 0)
            split_lo(0, 1)
            if pairs > 1:
                with dve.Fori(0, pairs - 1) as i:
                    body(i, False)
            body(pairs - 1, True)

        @block.tensor
        def _(pe):
            with pe.Fori(0, pairs) as i:
                for j in range(2):
                    pe.wait_ge(w_lo_done, i * 2 + j + 1)
                    pe.wait_ge(copied[j], i)
                    for h in range(halves):
                        at = slice(h * half, (h + 1) * half)
                        for k in range(KD):
                            o = ps[:, j, h, 0:half]
                            nc.tensor.matmul(o, w_hi[j][:, k, :], hi[:, k, at], start=(k == 0), stop=False)
                            nc.tensor.matmul(o, w_hi[j][:, k, :], lo[:, k, at], start=False, stop=False)
                            mm = nc.tensor.matmul(o, w_lo[j][:, k, :], hi[:, k, at], start=False, stop=(k == KD - 1))
                    mm.then_inc(multiplied[j], 1)


def gate_product(core, tag, w, col0, cols, hi, lo, gates):
    nc = core.nc
    with ExitStack() as ctx:
        raw = sbuf(nc, ctx, f"{tag}_raw", [P, KD, cols])
        w_hi = sbuf(nc, ctx, f"{tag}_wh", [P, KD, cols], F32R)
        w_lo = sbuf(nc, ctx, f"{tag}_wl", [P, KD, cols], F32R)
        ps = psum(nc, ctx, f"{tag}_ps", [P, TT, cols])
        loaded, hi_done, lo_done, multiplied, done = (core.sem(f"{tag}_{n}") for n in
                                                      ("loaded", "hi_done", "lo_done", "multiplied", "done"))
        block = ctx.enter_context(nc.Block())

        @block.sync
        def _(sp):
            sp.dma_start(raw[:], w.rearrange("(k p) n -> p k n", p=P)[:, :, col0:col0 + cols]).then_inc(loaded, 16)

        @block.scalar
        def _(act):
            act.wait_ge(loaded, 16)
            nc.scalar.copy(w_hi[:], raw[:]).then_inc(hi_done, 1)
            act.wait_ge(multiplied, 1)
            nc.scalar.activation(gates[:], ps[:], ACT.Sigmoid).then_inc(done, 1)

        @block.vector
        def _(dve):
            dve.wait_ge(hi_done, 1)
            nc.vector.tensor_tensor(w_lo[:], raw[:], w_hi[:].bitcast(F32), ALU.subtract).then_inc(lo_done, 1)

        @block.tensor
        def _(pe):
            pe.wait_ge(lo_done, 1)
            for t in range(TT):
                rows = slice(t * P, (t + 1) * P)
                for k in range(KD):
                    nc.tensor.matmul(ps[:, t, :], hi[:, k, rows], w_hi[:, k, :], start=(k == 0), stop=False)
                    nc.tensor.matmul(ps[:, t, :], lo[:, k, rows], w_hi[:, k, :], start=False, stop=False)
                    mm = nc.tensor.matmul(ps[:, t, :], hi[:, k, rows], w_lo[:, k, :], start=False, stop=(k == KD - 1))
            mm.then_inc(multiplied, 1)


def rotate_and_turn(core, tag, projT, cos_dram, sin_dram, rotated, ropeT, turned_rows, turned_dst, consts):
    nc = core.nc
    ident = consts["ident"]
    NR, NV = len(rotated), len(turned_rows)
    with ExitStack() as ctx:
        cos = sbuf(nc, ctx, f"{tag}_cos", [P, T])
        sin = sbuf(nc, ctx, f"{tag}_sin", [P, T])
        x = sbuf(nc, ctx, f"{tag}_x", [P, 2, T])
        xs = sbuf(nc, ctx, f"{tag}_xs", [P, 2, T])
        v = sbuf(nc, ctx, f"{tag}_v", [P, 2, T])
        vt = sbuf(nc, ctx, f"{tag}_vt", [P, 2, TT, P])
        ps = psum(nc, ctx, f"{tag}_ps", [P, 2, TT, P])
        tables = core.sem(f"{tag}_tables")
        x_loaded = core.sems(f"{tag}_x_loaded", 2)
        v_loaded = core.pool_dma_sems(f"{tag}_v_loaded", 2)
        by_cos = core.sem(f"{tag}_by_cos")
        by_sin = core.sem(f"{tag}_by_sin")
        rotated_done = core.sem(f"{tag}_rotated")
        x_stored = core.sems(f"{tag}_x_stored", 2)
        v_stored = core.pool_dma_sems(f"{tag}_v_stored", 2)
        flipped = core.sem(f"{tag}_flipped")
        copied = core.sem(f"{tag}_copied")
        block = ctx.enter_context(nc.Block())

        @block.sync
        def _(sp):
            sp.dma_start(cos[:], cos_dram).then_inc(tables, 16)
            sp.dma_start(sin[:], sin_dram).then_inc(tables, 16)
            for n, row in enumerate(rotated):
                b = n % 2
                if n >= 2:
                    sp.wait_ge(x_stored[b], 16 * (n // 2))
                sp.dma_start(x[:, b, :], projT[row:row + P, :]).then_inc(x_loaded[b], 16)
                for q in range(4):
                    sp.dma_start(xs[q * 32:q * 32 + 32, b, :],
                                 projT[row + (q ^ 1) * 32:row + (q ^ 1) * 32 + 32, :]).then_inc(x_loaded[b], 16)
                sp.wait_ge(rotated_done, n + 1)
                sp.dma_start(ropeT[n * P:n * P + P, :], x[:, b, :]).then_inc(x_stored[b], 16)
            for b in range(2):
                sp.wait_ge(x_stored[b], 16 * (NR // 2))

        @block.vector
        def _(dve):
            dve.wait_ge(tables, 32)
            for n in range(NR):
                b = n % 2
                dve.wait_ge(x_loaded[b], 80 * (n // 2 + 1))
                nc.vector.tensor_tensor(x[:, b, :], x[:, b, :], cos[:], ALU.mult).then_inc(by_cos, 1)
                nc.vector.tensor_tensor(xs[:, b, :], xs[:, b, :], sin[:], ALU.mult).then_inc(by_sin, 1)
                dve.wait_ge(by_cos, n + 1)
                dve.wait_ge(by_sin, n + 1)
                nc.vector.tensor_tensor(x[:, b, :], x[:, b, :], xs[:, b, :], ALU.add).then_inc(rotated_done, 1)

        @block.gpsimd
        def _(pool):
            for n in range(NV):
                if n >= 2:
                    pool.wait_ge(flipped, n - 1)
                source, row = turned_rows[n]
                pool.dma_start(v[:, n % 2, :], source[row:row + P, :]).then_inc(v_loaded[n % 2], 16)
                if n >= 1:
                    pool.wait_ge(copied, n)
                    pool.dma_start(turned_dst[n - 1].rearrange("(t p) c -> p t c", p=P), vt[:, (n - 1) % 2]
                                   ).then_inc(v_stored[(n - 1) % 2], 16)
            pool.wait_ge(copied, NV)
            pool.dma_start(turned_dst[NV - 1].rearrange("(t p) c -> p t c", p=P), vt[:, (NV - 1) % 2]
                           ).then_inc(v_stored[(NV - 1) % 2], 16)
            for b in range(2):
                pool.wait_ge(v_stored[b], 16 * ((NV + 1 - b) // 2))

        @block.tensor
        def _(pe):
            for n in range(NV):
                pe.wait_ge(v_loaded[n % 2], 16 * (n // 2 + 1))
                if n >= 2:
                    pe.wait_ge(copied, n - 1)
                for t in range(TT):
                    last = nc.tensor.transpose(ps[:, n % 2, t, :], v[:, n % 2, t * P:(t + 1) * P], ident[:])
                last.then_inc(flipped, 1)

        @block.scalar
        def _(act):
            for n in range(NV):
                act.wait_ge(flipped, n + 1)
                if n >= 2:
                    act.wait_ge(v_stored[n % 2], 16 * (n // 2))
                nc.scalar.copy(vt[:, n % 2], ps[:, n % 2]).then_inc(copied, 1)


def compress(core, tag, projT, k_row, v_row, k_par, v_par, cmp_cos, cmp_sin, kc_out, vc_out):
    nc = core.nc
    BL, ST, DH, G = 32, 16, 64, 2
    NB = (T - BL) // ST + 1
    NC = G * NB
    HID = 256
    with ExitStack() as ctx:
        kv = sbuf(nc, ctx, f"{tag}_kv", [DH, 2, G, T])
        pe_t = sbuf(nc, ctx, f"{tag}_pe", [DH, 2, BL])
        w1 = sbuf(nc, ctx, f"{tag}_w1", [DH, 2, BL, HID])
        w2 = sbuf(nc, ctx, f"{tag}_w2", [P, 2, 2, DH])
        w2s = sbuf(nc, ctx, f"{tag}_w2s", [P, 2, DH])
        blocks = sbuf(nc, ctx, f"{tag}_blocks", [DH, 2, BL, NC])
        hid = sbuf(nc, ctx, f"{tag}_hid", [P, 2, 2, NC])
        tab = sbuf(nc, ctx, f"{tag}_tab", [DH, 2, NC])
        kc = sbuf(nc, ctx, f"{tag}_kc", [DH, 2, NC])
        vc = sbuf(nc, ctx, f"{tag}_vc", [NB, G, DH])
        hid_ps = psum(nc, ctx, f"{tag}_hid_ps", [P, 2, 2, 256])
        kc_ps = psum(nc, ctx, f"{tag}_kc_ps", [DH, 2, NC])
        vc_ps = psum(nc, ctx, f"{tag}_vc_ps", [NB, G, DH])
        small = core.sem(f"{tag}_small")
        kv_loaded = core.sems(f"{tag}_kv_loaded", 2)
        w1_loaded = core.sems(f"{tag}_w1_loaded", 2)
        gathered = core.sem(f"{tag}_gathered")
        hid_mm = core.sem(f"{tag}_hid_mm")
        hid_done = core.sem(f"{tag}_hid_done")
        out_mm = core.sem(f"{tag}_out_mm")
        kc_step = core.sem(f"{tag}_kc_step")
        vc_done = core.sem(f"{tag}_vc_done")
        stored = core.sem(f"{tag}_stored")
        block = ctx.enter_context(nc.Block())

        @block.sync
        def _(sp):
            for s, (row, par) in enumerate(((k_row, k_par), (v_row, v_par))):
                for g in range(G):
                    sp.dma_start(kv[:, s, g, :], projT[row + g * DH:row + (g + 1) * DH, :]).then_inc(kv_loaded[s], 16)
                with nc.allow_non_contiguous_dma("position table per feature"):
                    sp.dma_start(pe_t[:, s, :], par[0].rearrange("j d -> d j")).then_inc(kv_loaded[s], 16)
                sp.dma_start(w1[:, s], par[1].rearrange("(j d) m -> d j m", d=DH)).then_inc(w1_loaded[s], 16)
                sp.dma_start(w2[:, s], par[2].rearrange("(m p) d -> p m d", p=P)).then_inc(small, 16)
            with nc.allow_non_contiguous_dma("swapped halves"):
                for q in range(2):
                    sp.dma_start(w2s[:, :, q * 32:q * 32 + 32],
                                 k_par[2].rearrange("(m p) d -> p m d", p=P)[:, :, (1 - q) * 32:(1 - q) * 32 + 32]
                                 ).then_inc(small, 16)
            sp.dma_start(tab[:, 0], cmp_cos).then_inc(small, 16)
            sp.dma_start(tab[:, 1], cmp_sin).then_inc(small, 16)
            sp.wait_ge(kc_step, 2)
            sp.dma_start(kc_out, kc[:, 0, :]).then_inc(stored, 16)
            sp.wait_ge(vc_done, 1)
            sp.dma_start(vc_out.rearrange("n (g d) -> n g d", g=G), vc[:]).then_inc(stored, 16)
            sp.wait_ge(stored, 32)

        @block.vector
        def _(dve):
            for s in range(2):
                dve.wait_ge(kv_loaded[s], 48)
                for jj in range(2):
                    for g in range(G):
                        src = kv[:, s, g, :].rearrange("p (b j) -> p j b", j=ST)[:, :, jj:jj + NB]
                        pos = pe_t[:, s, jj * ST:(jj + 1) * ST].unsqueeze(2).broadcast_to([DH, ST, NB])
                        nc.vector.tensor_tensor(blocks[:, s, jj * ST:(jj + 1) * ST, g * NB:(g + 1) * NB], src, pos,
                                                ALU.add).then_inc(gathered, 1)
            dve.wait_ge(out_mm, 1)
            dve.wait_ge(small, 96)
            nc.vector.tensor_tensor(kc[:], kc_ps[:], tab[:], ALU.mult).then_inc(kc_step, 1)
            dve.wait_ge(kc_step, 1)
            nc.vector.tensor_tensor(kc[:, 0, :], kc[:, 0, :], kc[:, 1, :], ALU.add).then_inc(kc_step, 1)
            dve.wait_ge(out_mm, 2)
            nc.vector.tensor_copy(vc[:], vc_ps[:]).then_inc(vc_done, 1)

        @block.tensor
        def _(pe):
            for s in range(2):
                pe.wait_ge(w1_loaded[s], 16)
                pe.wait_ge(gathered, 4 * s + 4)
                for m in range(2):
                    for j in range(BL):
                        mm = nc.tensor.matmul(hid_ps[:, s, m, 0:NC], w1[:, s, j, m * P:(m + 1) * P],
                                              blocks[:, s, j, :], start=(j == 0), stop=(j == BL - 1))
                mm.then_inc(hid_mm, 1)
            pe.wait_ge(small, 96)
            pe.wait_ge(hid_done, 1)
            for q, w in enumerate((w2[:, 0], w2s[:])):
                for m in range(2):
                    mm = nc.tensor.matmul(kc_ps[:, q, :], w[:, m, :], hid[:, 0, m, :], start=(m == 0), stop=(m == 1))
            mm.then_inc(out_mm, 1)
            pe.wait_ge(hid_done, 2)
            for g in range(G):
                for m in range(2):
                    mm = nc.tensor.matmul(vc_ps[:, g, :], hid[:, 1, m, g * NB:(g + 1) * NB], w2[:, 1, m, :],
                                          start=(m == 0), stop=(m == 1))
            mm.then_inc(out_mm, 1)

        @block.scalar
        def _(act):
            for s in range(2):
                act.wait_ge(hid_mm, s + 1)
                nc.scalar.activation(hid[:, s], hid_ps[:, s, :, 0:NC], ACT.Silu).then_inc(hid_done, 1)


def nsa_attention(core, tag, ropeT, kc_dram, v_tok, vc_dram, gates, consts, masks, o_dram):
    nc = core.nc
    ident = consts["ident"]
    DH, NB = 64, 63
    SCALE = DH ** -0.5
    ident_bf, tri_bf, edge_bf, cmp_mask, row_ok = (masks[n] for n in ("ident_bf", "tri", "edge", "cmp", "row_ok"))
    STEPS = 2 * TT
    CMP_COL = 5 * P
    with ExitStack() as ctx:
        q = sbuf(nc, ctx, f"{tag}_q", [DH, 2, T])
        ks = sbuf(nc, ctx, f"{tag}_ks", [DH, 2, T])
        kw = sbuf(nc, ctx, f"{tag}_kw", [DH, 2, T])
        kc = sbuf(nc, ctx, f"{tag}_kc", [DH, 2, NB])
        vs = sbuf(nc, ctx, f"{tag}_vs", [P, 2, TT, DH])
        vw = sbuf(nc, ctx, f"{tag}_vw", [P, 2, TT, DH])
        vc = sbuf(nc, ctx, f"{tag}_vc", [NB, 2, DH])
        prob = sbuf(nc, ctx, f"{tag}_prob", [P, 2, T])
        cscore = sbuf(nc, ctx, f"{tag}_cscore", [P, NB])
        cprob = sbuf(nc, ctx, f"{tag}_cprob", [P, P])
        top = sbuf(nc, ctx, f"{tag}_top", [P, 2, 2])
        bias = sbuf(nc, ctx, f"{tag}_bias", [P, 2, 2])
        den = sbuf(nc, ctx, f"{tag}_den", [P, 2, 3])
        rden = sbuf(nc, ctx, f"{tag}_rden", [P, 3])
        coef = sbuf(nc, ctx, f"{tag}_coef", [P, 3])
        probT = sbuf(nc, ctx, f"{tag}_probT", [P, 2, 4, P])
        o_part = sbuf(nc, ctx, f"{tag}_o_part", [P, 2, DH])
        o = sbuf(nc, ctx, f"{tag}_o", [P, 2, TT, DH])
        s_ps = psum(nc, ctx, f"{tag}_s_ps", [P, 2, T])
        t_ps = psum(nc, ctx, f"{tag}_t_ps", [P, 2, 4, P])
        o_ps = psum(nc, ctx, f"{tag}_o_ps", [P, 2, HALF])
        loaded = core.sems(f"{tag}_loaded", 2)
        scored = core.sem(f"{tag}_scored")
        maxed = core.sem(f"{tag}_maxed")
        biased = core.sem(f"{tag}_biased")
        exped = core.sem(f"{tag}_exped")
        flipped = core.sem(f"{tag}_flipped")
        copied = core.sems(f"{tag}_copied", 2)
        summed = core.sem(f"{tag}_summed")
        inverted = core.sem(f"{tag}_inverted")
        finished = core.sem(f"{tag}_finished")
        o_done = core.sem(f"{tag}_o_done")
        padded = core.sem(f"{tag}_padded")
        stored = core.pool_dma_sems(f"{tag}_stored", 2)
        block = ctx.enter_context(nc.Block())

        def parts(s):
            i = s // 2 % TT
            if s % 2 == 0:
                return [(1, 0, i + 1, 0)]
            first = max(0, i - 4)
            return [(2, first, i + 1 - first, 0), (0, 0, 1, CMP_COL)]

        def turns(s):
            out = []
            for br, first, n, col in parts(s):
                out += [(br, first + m, col + m * P, m == 0, m == n - 1) for m in range(n)]
            return [out[m:m + 4] for m in range(0, len(out), 4)]

        fills = [0]
        for s in range(2 * STEPS):
            fills.append(fills[-1] + len(turns(s)))
        FILLS = fills[-1]
        assert FILLS % 2 == 0
        EXPS = 3 * STEPS

        def exps_through(n, s):
            return n * EXPS + s // 2 * 3 + (3 if s % 2 else 1)

        @block.sync
        def _(sp):
            with sp.Fori(0, 2) as g:
                with sp.Fori(0, 2) as r:
                    for b in range(2):
                        sp.wait_ge(stored[b], g * 32 + r * 16)
                        for dst, src in (
                            (q[:, b, :], ropeT[bass.ds(g * (2 * P) + r * P + b * DH, DH), :]),
                            (ks[:, b, :], ropeT[bass.ds(g * DH + 4 * P, DH), :]),
                            (kw[:, b, :], ropeT[bass.ds(g * DH + 5 * P, DH), :]),
                            (kc[:, b, :], kc_dram[:, bass.ds(g * NB, NB)]),
                            (vs[:, b], v_tok[0].rearrange("(t p) c -> p t c", p=P)[:, :, bass.ds(g * DH, DH)]),
                            (vw[:, b], v_tok[1].rearrange("(t p) c -> p t c", p=P)[:, :, bass.ds(g * DH, DH)]),
                            (vc[:, b, :], vc_dram[:, bass.ds(g * DH, DH)]),
                        ):
                            sp.dma_start(dst, src).then_inc(loaded[b], 16)

        @block.gpsimd
        def _(pool):
            nc.gpsimd.memset(cprob[:], 0.0).then_inc(padded, 1)
            with pool.Fori(0, 4) as n:
                for b in range(2):
                    pool.wait_ge(o_done, n * (2 * TT) + (b + 1) * TT)
                    pool.dma_start(o_dram.rearrange("(t p) c -> p t c", p=P)[:, :, bass.ds(n * P + b * DH, DH)],
                                   o[:, b]).then_inc(stored[b], 16)
            for b in range(2):
                pool.wait_ge(stored[b], 64)

        @block.tensor
        def _(pe):
            def score(n, s):
                b, i = s // STEPS, s // 2 % TT
                if s % STEPS == 0:
                    pe.wait_ge(loaded[b], n * 112 + 112)
                if s >= 2:
                    pe.wait_ge(exped, exps_through(n, s - 2))
                rows = slice(i * P, (i + 1) * P)
                for br, first, cnt, col in parts(s):
                    if br == 0:
                        mm = nc.tensor.matmul(s_ps[:, 1, col:col + NB], q[:, b, rows], kc[:, b, :], start=True, stop=True)
                        continue
                    key = ks if br == 1 else kw
                    for m in range(0, cnt, 4):
                        w = min(4, cnt - m)
                        tri = m + w == cnt
                        edge = br == 2 and i >= 4 and m == 0
                        at = s_ps[:, s % 2, col + m * P:col + (m + w) * P]
                        mm = nc.tensor.matmul(at, q[:, b, rows], key[:, b, (first + m) * P:(first + m + w) * P],
                                              start=True, stop=not (tri or edge))
                        if edge:
                            mm = nc.tensor.matmul(at[:, 0:P], ident_bf[:], edge_bf[:], start=False, stop=not tri)
                        if tri:
                            mm = nc.tensor.matmul(at[:, (w - 1) * P:w * P], ident_bf[:], tri_bf[:],
                                                  start=False, stop=True)
                mm.then_inc(scored, 1)

            def attend(n, s):
                b, tile = s // STEPS, s // 2
                pe.wait_ge(exped, exps_through(n, s))
                if s % 2 == 0:
                    pe.wait_ge(o_done, n * (2 * TT) + max(tile - 1, 0))
                banks = turns(s)

                def values(f):
                    fill = fills[s] + f
                    pe.wait_ge(copied[fill % 2], n * (FILLS // 2) + fill // 2 + 1)
                    for m, (br, blk, col, first, last) in enumerate(banks[f]):
                        val = {0: vc[:, b, :], 1: vs[:, b, blk, :], 2: vw[:, b, blk, :]}[br]
                        keys = NB if br == 0 else P
                        mm = nc.tensor.matmul(o_ps[:, tile % 2, br * DH:(br + 1) * DH],
                                              probT[0:keys, fill % 2, m, :], val, start=first, stop=last)
                    return mm

                for f, bank in enumerate(banks):
                    fill = fills[s] + f
                    pe.wait_ge(copied[fill % 2], n * (FILLS // 2) + fill // 2)
                    for m, (br, blk, col, first, last) in enumerate(bank):
                        src = cprob[:] if br == 0 else prob[:, s % 2, col:col + P]
                        mm = nc.tensor.transpose(t_ps[:, fill % 2, m, :], src, ident[:])
                    mm.then_inc(flipped, 1)
                    if f >= 1:
                        values(f - 1)
                mm = values(len(banks) - 1)
                if s % 2 == 1:
                    mm.then_inc(summed, 1)

            with pe.Fori(0, 4) as n:
                score(n, 0)
                for s in range(2 * STEPS):
                    if s + 1 < 2 * STEPS:
                        score(n, s + 1)
                    attend(n, s)

        def copy_out(eng, copy, n, s, parity):
            for f, bank in enumerate(turns(s)):
                fill = fills[s] + f
                if fill % 2 == parity:
                    eng.wait_ge(flipped, n * FILLS + fill + 1)
                    copy(probT[:, parity, 0:len(bank), :], t_ps[:, parity, 0:len(bank), :]).then_inc(copied[parity], 1)

        @block.scalar
        def _(act):
            def exps(n, s):
                tile, i = s // 2, s // 2 % TT
                cols = (i + 1) * P if s % 2 == 0 else min(i + 1, 5) * P
                act.wait_ge(biased, n * (2 * STEPS) + s + 1)
                act.wait_ge(flipped, n * FILLS + (fills[s - 1] if s >= 2 else 0))
                act.wait_ge(inverted, n * (2 * TT) + max(tile - 1, 0))
                nc.scalar.activation(prob[:, s % 2, 0:cols], s_ps[:, s % 2, 0:cols], ACT.Exp, bias=bias[:, s % 2, 0:1],
                                     scale=SCALE, accum_out=den[:, tile % 2, 1 + s % 2:2 + s % 2]).then_inc(exped, 1)
                if s % 2 == 1:
                    nc.scalar.activation(cprob[:, 0:NB], cscore[:], ACT.Exp, bias=bias[:, 1, 1:2], scale=SCALE,
                                         accum_out=den[:, tile % 2, 0:1]).then_inc(exped, 1)

            act.wait_ge(padded, 1)
            with act.Fori(0, 4) as n:
                exps(n, 0)
                for s in range(2 * STEPS):
                    if s + 1 < 2 * STEPS:
                        exps(n, s + 1)
                    copy_out(act, nc.scalar.copy, n, s, 1)

        @block.vector
        def _(dve):
            MAXES = 4 * STEPS

            def bias_of(n, s):
                i = s // 2 % TT
                before = n * MAXES + s // 2 * 4 + s % 2
                cols = (i + 1) * P if s % 2 == 0 else min(i + 1, 5) * P
                dve.wait_ge(scored, n * (2 * STEPS) + s + 1)
                nc.vector.tensor_reduce(top[:, s % 2, 0:1], s_ps[:, s % 2, 0:cols], AX_X, ALU.max).then_inc(maxed, 1)
                if s % 2 == 1:
                    nc.vector.tensor_tensor(cscore[:], s_ps[:, 1, CMP_COL:CMP_COL + NB], cmp_mask[:, i, :],
                                            ALU.add).then_inc(maxed, 1)
                    dve.wait_ge(maxed, before + 2)
                    nc.vector.tensor_reduce(top[:, 1, 1:2], cscore[:], AX_X, ALU.max).then_inc(maxed, 1)
                dve.wait_ge(maxed, before + (3 if s % 2 else 1))
                nc.vector.tensor_scalar(bias[:, s % 2, 0:1 + s % 2], top[:, s % 2, 0:1 + s % 2], -SCALE, None,
                                        ALU.mult).then_inc(biased, 1)

            def finish(n, tile):
                b, i = tile // TT, tile % TT
                FIN = 2 * TT * 3 + 2
                before = n * FIN + tile * 3 + (tile > 0) + (tile > TT)
                dve.wait_ge(summed, n * (2 * TT) + tile + 1)
                if i == 0:
                    dve.wait_ge(stored[b], n * 16)
                nc.vector.reciprocal(rden[:], den[:, tile % 2, :]).then_inc(inverted, 1)
                dve.wait_ge(inverted, n * (2 * TT) + tile + 1)
                nc.vector.tensor_tensor(coef[:], rden[:], gates[:, i, bass.ds(n * 6 + b * 3, 3)],
                                        ALU.mult).then_inc(finished, 1)
                k = 1
                dve.wait_ge(finished, before + k)
                if i == 0:
                    nc.vector.tensor_tensor(coef[:, 0:1], coef[:, 0:1], row_ok[:], ALU.mult).then_inc(finished, 1)
                    k += 1
                    dve.wait_ge(finished, before + k)
                op = o_ps[:, tile % 2, :]
                nc.vector.tensor_scalar(o_part[:, 0, :], op[:, 0:DH], coef[:, 0:1], None, ALU.mult).then_inc(finished, 1)
                dve.wait_ge(finished, before + k + 1)
                nc.vector.scalar_tensor_tensor(out=o_part[:, 1, :], in0=op[:, DH:2 * DH], scalar=coef[:, 1:2],
                                               in1=o_part[:, 0, :], op0=ALU.mult, op1=ALU.add).then_inc(finished, 1)
                dve.wait_ge(finished, before + k + 2)
                nc.vector.scalar_tensor_tensor(out=o[:, b, i, :], in0=op[:, 2 * DH:3 * DH], scalar=coef[:, 2:3],
                                               in1=o_part[:, 1, :], op0=ALU.mult, op1=ALU.add).then_inc(o_done, 1)

            with dve.Fori(0, 4) as n:
                bias_of(n, 0)
                for s in range(2 * STEPS):
                    if s + 1 < 2 * STEPS:
                        bias_of(n, s + 1)
                    if s % 2 == 0 and s >= 2:
                        finish(n, s // 2 - 1)
                    copy_out(dve, nc.vector.tensor_copy, n, s, 0)
                finish(n, 2 * TT - 1)


def load_masks(core, ctx, a):
    nc = core.nc
    shapes = {"ident_bf": [P, P], "tri": [P, P], "edge": [P, P], "cmp": [P, TT, 63], "row_ok": [P, 1]}
    wide = {n: sbuf(nc, ctx, f"wide_{n}", s) for n, s in shapes.items()}
    narrow = {n: sbuf(nc, ctx, f"narrow_{n}", shapes[n], BF16) for n in ("ident_bf", "tri", "edge")}
    loaded, narrowed = core.sem("masks_loaded"), core.sem("masks_narrowed")
    with nc.Block() as block:
        @block.sync
        def _(sp):
            for name, tile in wide.items():
                sp.dma_start(tile[:], a[f"mask_{name}"]).then_inc(loaded, 16)
            sp.wait_ge(loaded, 16 * len(wide))

        @block.vector
        def _(dve):
            dve.wait_ge(loaded, 16 * len(wide))
            for name, tile in narrow.items():
                nc.vector.tensor_copy(tile[:], wide[name][:]).then_inc(narrowed, 1)
            dve.wait_ge(narrowed, len(narrow))
    return {**wide, **narrow}


def shape_tables():
    half, NB = 32, 63
    inv = np.power(np.float32(10000.0), -np.arange(half, dtype=np.float32) / np.float32(half)).astype(np.float32)

    def angles(pos):
        ang = (pos.astype(np.float32)[None, :] * inv[:, None]).astype(np.float32)
        return np.cos(ang).astype(np.float32), np.sin(ang).astype(np.float32)

    c, s = angles(np.arange(T))
    cc, cs = angles(np.arange(NB) * 16 + 31)
    t = np.arange(P)
    neg = np.float32(-1e30)
    tok = np.arange(T).reshape(TT, P)
    cmp_ok = (np.arange(NB) * 16 + 31)[None, None, :] <= tok.T[:, :, None]
    return {
        "ident_": np.eye(P, dtype=np.float32),
        "cos_t": np.tile(c, (4, 1)),
        "sin_t": np.concatenate([-s, s, -s, s]),
        "ccos": np.tile(cc, (2, 2)),
        "csin": np.tile(np.concatenate([-cs, cs]), (1, 2)),
        "mask_ident_bf": np.eye(P, dtype=np.float32),
        "mask_tri": np.where(t[None, :] > t[:, None], neg, 0).astype(np.float32),
        "mask_edge": np.where(t[None, :] <= t[:, None], neg, 0).astype(np.float32),
        "mask_cmp": np.where(cmp_ok, np.float32(0), neg).astype(np.float32),
        "mask_row_ok": (t >= 31).astype(np.float32)[:, None],
        **recurrence_tables(),
    }


CH = 64
NCH = T // CH
PAIRS = 4
RW = PAIRS * P


def rwkv_prepare(core, tag, z, par, consts, a, ops_dram, end_decay, bonus, g_tok):
    nc = core.nc
    w0_d, w2_d, a0_d, a2_d, g2_d, kk_d, ka_d, rk_d = par
    with ExitStack() as ctx:
        lora = sbuf(nc, ctx, f"{tag}_lora", [P, T])
        wlo = sbuf(nc, ctx, f"{tag}_wlo", [64, T])
        glo = sbuf(nc, ctx, f"{tag}_glo", [P, T])
        w2 = sbuf(nc, ctx, f"{tag}_w2", [P, RW])
        g2 = sbuf(nc, ctx, f"{tag}_g2", [P, RW])
        w0 = sbuf(nc, ctx, f"{tag}_w0", [1, RW])
        ones = sbuf(nc, ctx, f"{tag}_ones", [1, P])
        tri = sbuf(nc, ctx, f"{tag}_tri", [P, 2 * P])
        pairsum = sbuf(nc, ctx, f"{tag}_pairsum", [P, P])
        vecs = sbuf(nc, ctx, f"{tag}_vecs", [P, 4, PAIRS])
        one_ka = sbuf(nc, ctx, f"{tag}_one_ka", [P, PAIRS])
        rk_sel = sbuf(nc, ctx, f"{tag}_rk_sel", [P, PAIRS, 2])
        sel = sbuf(nc, ctx, f"{tag}_sel", [P, 2])
        sg = sbuf(nc, ctx, f"{tag}_sg", [P, TT, RW])
        r = sbuf(nc, ctx, f"{tag}_r", [P, T])
        k = sbuf(nc, ctx, f"{tag}_k", [P, T])
        dec = sbuf(nc, ctx, f"{tag}_dec", [P, 3, T])
        rate = sbuf(nc, ctx, f"{tag}_rate", [P, T])
        t1 = sbuf(nc, ctx, f"{tag}_t1", [P, T])
        sq = sbuf(nc, ctx, f"{tag}_sq", [P, T])
        nrm = sbuf(nc, ctx, f"{tag}_nrm", [P, T])
        u = sbuf(nc, ctx, f"{tag}_u", [P, T])
        kn = sbuf(nc, ctx, f"{tag}_kn", [P, T])
        ka = sbuf(nc, ctx, f"{tag}_ka", [P, T])
        rk = sbuf(nc, ctx, f"{tag}_rk", [P, T])
        res = sbuf(nc, ctx, f"{tag}_res", [P, 4, T])
        cum_ps = psum(nc, ctx, f"{tag}_cum_ps", [P, TT, 2, P])
        wide_ps = psum(nc, ctx, f"{tag}_wide_ps", [P, 3, HALF])
        bonus_ps = psum(nc, ctx, f"{tag}_bonus_ps", [P, TT, 2])
        small = core.sem(f"{tag}_small")
        lora_in = core.sem(f"{tag}_lora_in")
        ones_set = core.sem(f"{tag}_ones_set")
        squashed = core.sem(f"{tag}_squashed")
        vec_step = core.sem(f"{tag}_vec_step")
        z_mm = core.sem(f"{tag}_z_mm")
        z_sig = core.sem(f"{tag}_z_sig")
        g_mm = core.sem(f"{tag}_g_mm")
        g_copied = core.sem(f"{tag}_g_copied")
        rk_in = core.sem(f"{tag}_rk_in")
        squared = core.sem(f"{tag}_squared")
        cum_mm = core.sem(f"{tag}_cum_mm")
        cum_exp = core.sem(f"{tag}_cum_exp")
        rate_mm = core.sem(f"{tag}_rate_mm")
        rate_done = core.sem(f"{tag}_rate_done")
        norm_mm = core.sem(f"{tag}_norm_mm")
        norm_root = core.sem(f"{tag}_norm_root")
        vec = core.sem(f"{tag}_vec")
        done = core.sem(f"{tag}_done")
        bonus_mm = core.sem(f"{tag}_bonus_mm")
        bonus_done = core.sem(f"{tag}_bonus_done")
        stored = core.sem(f"{tag}_stored")
        block = ctx.enter_context(nc.Block())
        SMALL = 16 * 12
        VEC = 9

        @block.sync
        def _(sp):
            sp.dma_start(lora[:], z[3 * RW:3 * RW + P, :]).then_inc(lora_in, 16)
            sp.dma_start(glo[:], z[3 * RW + P:3 * RW + 2 * P, :]).then_inc(lora_in, 16)
            sp.dma_start(w2[0:64, :], w2_d).then_inc(small, 16)
            sp.dma_start(w2[64:P, :], a2_d).then_inc(small, 16)
            sp.dma_start(g2[:], g2_d).then_inc(small, 16)
            sp.dma_start(w0[:], w0_d.rearrange("(o n) -> o n", o=1)).then_inc(small, 16)
            sp.dma_start(tri[:], a["tri_decay"]).then_inc(small, 16)
            sp.dma_start(pairsum[:], a["pairsum"]).then_inc(small, 16)
            sp.dma_start(sel[:], a["head_sel"]).then_inc(small, 16)
            with nc.allow_non_contiguous_dma("vectors per channel"):
                for n, v in enumerate((a0_d, kk_d, ka_d, rk_d)):
                    sp.dma_start(vecs[:, n, :], v.rearrange("(c p) -> p c", p=P)).then_inc(small, 16)
            sp.dma_start(ones[:], a["ones_row"]).then_inc(small, 16)
            with sp.Fori(0, PAIRS) as p:
                sp.wait_ge(done, p * 4)
                sp.dma_start(r[:], z[bass.ds(p * P, P), :]).then_inc(rk_in, 16)
                sp.dma_start(k[:], z[bass.ds(p * P + RW, P), :]).then_inc(rk_in, 16)
                for n in range(4):
                    sp.wait_ge(done, p * 4 + n + 1)
                    sp.dma_start(ops_dram[n, bass.ds(p * P, P), :], res[:, n, :]).then_inc(stored, 16)
            sp.wait_ge(stored, 64 * PAIRS)

        @block.tensor
        def _(pe):
            pe.wait_ge(small, SMALL)
            pe.wait_ge(squashed, 2)
            for t in range(TT):
                rows = slice(t * P, (t + 1) * P)
                if t >= 2:
                    pe.wait_ge(z_sig, t - 1)
                nc.tensor.matmul(wide_ps[:, t % 2, :], wlo[:, rows], w2[0:64, :], start=True, stop=False)
                nc.tensor.matmul(wide_ps[:, t % 2, :], ones[:], w0[:], start=False, stop=True).then_inc(z_mm, 1)
            for t in range(TT):
                rows = slice(t * P, (t + 1) * P)
                if t < 2:
                    pe.wait_ge(z_sig, TT - 1 + t)
                else:
                    pe.wait_ge(g_copied, t - 1)
                nc.tensor.matmul(wide_ps[:, t % 2, :], glo[:, rows], g2[:], start=True, stop=True).then_inc(g_mm, 1)
            pe.wait_ge(g_copied, TT)
            for p in range(PAIRS):
                chan = slice(p * P, (p + 1) * P)
                if p >= 1:
                    pe.wait_ge(cum_exp, 3 * p)
                for t in range(TT):
                    mm = nc.tensor.matmul(cum_ps[:, t].rearrange("p a b -> p (a b)"), sg[:, t, chan], tri[:],
                                          start=True, stop=True)
                mm.then_inc(cum_mm, 1)
                for h in range(2):
                    at = slice(h * HALF, (h + 1) * HALF)
                    if p >= 1 or h >= 1:
                        pe.wait_ge(rate_done, 2 * p + h)
                    nc.tensor.matmul(wide_ps[:, 0, :], w2[64:P, chan], lora[64:P, at],
                                     start=True, stop=True).then_inc(rate_mm, 1)
                pe.wait_ge(squared, p + 1)
                for h in range(2):
                    at = slice(h * HALF, (h + 1) * HALF)
                    if p >= 1:
                        pe.wait_ge(norm_root, 2 * p - 1 + h)
                    nc.tensor.matmul(wide_ps[:, 1 + h, :], pairsum[:], sq[:, at], start=True, stop=True).then_inc(norm_mm, 1)
                pe.wait_ge(vec, VEC * p + 7)
                if p >= 1:
                    pe.wait_ge(bonus_done, p)
                else:
                    pe.wait_ge(vec_step, 2)
                for t in range(TT):
                    mm = nc.tensor.matmul(bonus_ps[:, t, :], rk[:, t * P:(t + 1) * P], rk_sel[:, p, :],
                                          start=True, stop=True)
                mm.then_inc(bonus_mm, 1)

        @block.scalar
        def _(act):
            act.wait_ge(lora_in, 32)
            nc.scalar.activation(wlo[:], lora[0:64, :], ACT.Tanh).then_inc(squashed, 1)
            nc.scalar.activation(glo[:], glo[:], ACT.Sigmoid).then_inc(squashed, 1)
            for t in range(TT):
                act.wait_ge(z_mm, t + 1)
                nc.scalar.activation(sg[:, t, :], wide_ps[:, t % 2, :], ACT.Sigmoid).then_inc(z_sig, 1)
            for t in range(TT):
                act.wait_ge(g_mm, t + 1)
                nc.scalar.copy(g_tok[:, t, :], wide_ps[:, t % 2, :]).then_inc(g_copied, 1)
            act.wait_ge(small, SMALL)
            for p in range(PAIRS):
                for h in range(2):
                    if p >= 1 and h == 0:
                        act.wait_ge(vec, VEC * (p - 1) + 8)
                    act.wait_ge(rate_mm, 2 * p + h + 1)
                    nc.scalar.activation(rate[:, h * HALF:(h + 1) * HALF], wide_ps[:, 0, :], ACT.Sigmoid,
                                         bias=vecs[:, 0, p:p + 1]).then_inc(rate_done, 1)
                act.wait_ge(rk_in, 32 * (p + 1))
                if p >= 1:
                    act.wait_ge(norm_mm, 2 * p)
                nc.scalar.activation(sq[:], k[:], ACT.Square, scale=vecs[:, 1, p:p + 1]).then_inc(squared, 1)
                if p >= 1:
                    act.wait_ge(done, 4 * p)
                    act.wait_ge(vec, VEC * p)
                act.wait_ge(cum_mm, p + 1)
                for n, (plane, sign) in enumerate(((0, 1.0), (0, -1.0), (1, 1.0))):
                    nc.scalar.activation(dec[:, n, :].rearrange("p (t c) -> p t c", c=P), cum_ps[:, :, plane, :],
                                         ACT.Exp, scale=sign).then_inc(cum_exp, 1)
                for h in range(2):
                    act.wait_ge(norm_mm, 2 * p + h + 1)
                    if p >= 1 and h == 0:
                        act.wait_ge(vec, VEC * (p - 1) + 6)
                    nc.scalar.activation(nrm[:, h * HALF:(h + 1) * HALF], wide_ps[:, 1 + h, :],
                                         ACT.Sqrt).then_inc(norm_root, 1)

        @block.vector
        def _(dve):
            dve.wait_ge(small, SMALL)
            nc.vector.tensor_scalar(one_ka[:], vecs[:, 2, :], -1.0, 1.0, ALU.mult, ALU.add).then_inc(vec_step, 1)
            nc.vector.tensor_tensor(rk_sel[:], vecs[:, 3, :].unsqueeze(2).broadcast_to([P, PAIRS, 2]),
                                    sel[:].unsqueeze(1).broadcast_to([P, PAIRS, 2]), ALU.mult).then_inc(vec_step, 1)
            dve.wait_ge(vec_step, 2)
            for p in range(PAIRS):
                v0 = VEC * p
                dve.wait_ge(rk_in, 32 * (p + 1))
                if p >= 1:
                    dve.wait_ge(bonus_mm, p)
                nc.vector.tensor_scalar(t1[:], k[:], vecs[:, 1, p:p + 1], None, ALU.mult).then_inc(vec, 1)
                dve.wait_ge(rate_done, 2 * p + 2)
                nc.vector.tensor_scalar(u[:], rate[:], vecs[:, 2, p:p + 1], one_ka[:, p:p + 1],
                                        ALU.mult, ALU.add).then_inc(vec, 1)
                dve.wait_ge(norm_root, 2 * p + 2)
                nc.vector.tensor_scalar(nrm[:], nrm[:], 1e-12, None, ALU.max).then_inc(vec, 1)
                dve.wait_ge(vec, v0 + 3)
                nc.vector.reciprocal(nrm[:], nrm[:]).then_inc(vec, 1)
                dve.wait_ge(vec, v0 + 4)
                nc.vector.tensor_tensor(kn[:], k[:], u[:], ALU.mult).then_inc(vec, 1)
                nc.vector.tensor_tensor(t1[:], t1[:], nrm[:], ALU.mult).then_inc(vec, 1)
                dve.wait_ge(vec, v0 + 6)
                nc.vector.tensor_tensor(rk[:], r[:], kn[:], ALU.mult).then_inc(vec, 1)
                nc.vector.tensor_tensor(ka[:], t1[:], rate[:], ALU.mult).then_inc(vec, 1)
                dve.wait_ge(cum_exp, 3 * p + 3)
                if p >= 1:
                    dve.wait_ge(stored, 64 * p)
                nc.vector.scalar_tensor_tensor(out=res[:, 0, :], in0=t1[:], scalar=-1.0, in1=dec[:, 2, :],
                                               op0=ALU.mult, op1=ALU.mult).then_inc(done, 1)
                dve.wait_ge(vec, v0 + 8)
                nc.vector.tensor_tensor(res[:, 1, :], ka[:], dec[:, 1, :], ALU.mult).then_inc(done, 1)
                nc.vector.tensor_tensor(res[:, 2, :], kn[:], dec[:, 1, :], ALU.mult).then_inc(done, 1)
                nc.vector.tensor_tensor(res[:, 3, :], r[:], dec[:, 0, :], ALU.mult).then_inc(done, 1)
                nc.vector.tensor_copy(end_decay[:, p, :], dec[:, 0, :].rearrange("p (c t) -> p c t", t=CH)[:, :, CH - 1]
                                      ).then_inc(vec, 1)
                dve.wait_ge(bonus_mm, p + 1)
                nc.vector.tensor_copy(bonus[:, :, 2 * p:2 * p + 2], bonus_ps[:]).then_inc(bonus_done, 1)


def rwkv_chunks(core, tag, ops_dram, v_dram, end_decay, consts, a, y_dram):
    nc = core.nc
    ident = consts["ident"]
    LEVELS = 5
    with ExitStack() as ctx:
        AR = [sbuf(nc, ctx, f"{tag}_AR{j}", [P, PAIRS, 2 * P]) for j in range(2)]
        B = [sbuf(nc, ctx, f"{tag}_B{j}", [P, PAIRS, P]) for j in range(2)]
        K = [sbuf(nc, ctx, f"{tag}_K{j}", [P, PAIRS, P]) for j in range(2)]
        V = [sbuf(nc, ctx, f"{tag}_V{j}", [P, PAIRS, CH]) for j in range(2)]
        LT = [sbuf(nc, ctx, f"{tag}_LT{j}", [P, PAIRS, P]) for j in range(2)]
        L = [sbuf(nc, ctx, f"{tag}_L{j}", [P, PAIRS, P]) for j in range(2)]
        LkT = [sbuf(nc, ctx, f"{tag}_LkT{j}", [P, PAIRS, P]) for j in range(2)]
        RkT = [sbuf(nc, ctx, f"{tag}_RkT{j}", [P, PAIRS, P]) for j in range(2)]
        BR = [sbuf(nc, ctx, f"{tag}_BR{j}", [P, PAIRS, 2 * P]) for j in range(2)]
        Ktok = [sbuf(nc, ctx, f"{tag}_Kt{j}", [P, PAIRS, P]) for j in range(2)]
        AX = [sbuf(nc, ctx, f"{tag}_AX{j}", [P, PAIRS, P + CH]) for j in range(2)]
        LTm = [sbuf(nc, ctx, f"{tag}_LTm{j}", [P, LEVELS, PAIRS, P]) for j in range(2)]
        Tm = [sbuf(nc, ctx, f"{tag}_T{j}", [P, PAIRS, P]) for j in range(2)]
        TT_ = [sbuf(nc, ctx, f"{tag}_TT{j}", [P, PAIRS, P]) for j in range(2)]
        Y1 = [sbuf(nc, ctx, f"{tag}_Y1{j}", [P, PAIRS, P]) for j in range(2)]
        WU = [sbuf(nc, ctx, f"{tag}_WU{j}", [P, PAIRS, P + CH]) for j in range(2)]
        GR = [sbuf(nc, ctx, f"{tag}_GR{j}", [P, PAIRS, 2 * P]) for j in range(2)]
        M = [sbuf(nc, ctx, f"{tag}_M{j}", [P, PAIRS, CH]) for j in range(2)]
        yo = [sbuf(nc, ctx, f"{tag}_yo{j}", [P, PAIRS, CH]) for j in range(2)]
        m_gram = sbuf(nc, ctx, f"{tag}_m_gram", [P, 2, P])
        m_low = sbuf(nc, ctx, f"{tag}_m_low", [P, P])
        m_one = sbuf(nc, ctx, f"{tag}_m_one", [P, 2, P])
        m_lev = sbuf(nc, ctx, f"{tag}_m_lev", [P, LEVELS, P])
        ps = [psum(nc, ctx, f"{tag}_ps{j}", [P, 4, HALF]) for j in range(2)]
        masks_in = core.sem(f"{tag}_masks_in")
        zeroed = core.sem(f"{tag}_zeroed")
        loaded = core.sems(f"{tag}_loaded", 2)
        products = core.sems(f"{tag}_products", 2)
        by_dve = core.sems(f"{tag}_by_dve", 2)
        by_act = core.sems(f"{tag}_by_act", 2)
        levels = core.sems(f"{tag}_levels", 2)
        y_stored = core.pool_dma_sems(f"{tag}_y_stored", 2)
        state = core.sem(f"{tag}_state")
        block = ctx.enter_context(nc.Block())

        pn = {}
        for name in ["gram_b", "gram_k", "gram_l", "turn_a", "turn_b", "turn_k", "x"] + \
                    [f"{w}{lv}" for lv in range(LEVELS) for w in ("y", "t", "tt") if not (w == "t" and lv == LEVELS - 1)] + \
                    ["wu", "gr", "s", "out"]:
            pn[name] = len(pn) + 1
        NP_ = len(pn)
        dn = {}
        for name in ["lt", "rbt", "lkt", "rkt", "l", "t_one", "tt_one", "t_start", "tt_start"] + \
                    [f"{w}{lv}" for lv in range(LEVELS) for w in ("t", "tt") if not (w == "t" and lv == LEVELS - 1)] + \
                    ["g", "rw"]:
            dn[name] = len(dn) + 1
        ND = len(dn)
        an = {}
        for name in ["a_tok", "b_tok", "k_tok", "x"] + [f"y{lv}" for lv in range(LEVELS)] + ["wu", "out"]:
            an[name] = len(an) + 1
        NA = len(an)

        def flat(tile):
            return tile.rearrange("p a b -> p (a b)")

        @block.sync
        def _(sp):
            for dst, name in ((m_gram, "m_gram"), (m_low, "m_low"), (m_one, "m_one"), (m_lev, "m_lev")):
                sp.dma_start(dst[:], a[name]).then_inc(masks_in, 16)
            sp.wait_ge(zeroed, 8)
            with sp.Fori(0, NCH // 2) as i:
                for j in range(2):
                    first = sp.snap(i * P + j * CH)
                    sp.wait_ge(products[j], i * NP_)
                    for n, dst in enumerate((AR[j][:, :, 0:P], B[j][:], K[j][:], AR[j][:, :, P:2 * P])):
                        for h in range(2):
                            rows = slice(h * CH, (h + 1) * CH)
                            src = ops_dram[n].rearrange("(q p) t -> p q t", p=P)[rows, :, bass.ds(first, CH)]
                            sp.dma_start(dst[rows, :, h * CH:(h + 1) * CH], src).then_inc(loaded[j], 16)
                    for h in range(2):
                        src = v_dram[bass.ds(first, CH), :].rearrange("t (q p) -> t q p", p=P)
                        sp.dma_start(V[j][h * CH:(h + 1) * CH], src[:, :, h * CH:(h + 1) * CH]).then_inc(loaded[j], 16)

        @block.gpsimd
        def _(pool):
            for j in range(2):
                nc.gpsimd.memset(AR[j][:], 0.0).then_inc(zeroed, 1)
                nc.gpsimd.memset(B[j][:], 0.0).then_inc(zeroed, 1)
                nc.gpsimd.memset(K[j][:], 0.0).then_inc(zeroed, 1)
                nc.gpsimd.memset(M[j][:], 0.0).then_inc(zeroed, 1)
            pool.wait_ge(masks_in, 64)
            with pool.Fori(0, NCH // 2) as i:
                for j in range(2):
                    pool.wait_ge(by_dve[j], i * ND + dn["lt"])
                    pool.wait_ge(products[j], i * NP_)
                    for lv in range(LEVELS):
                        nc.gpsimd.tensor_tensor(LTm[j][:, lv], LT[j][:],
                                                m_lev[:, lv, :].unsqueeze(1).broadcast_to([P, PAIRS, P]),
                                                ALU.mult).then_inc(levels[j], 1)
                for j in range(2):
                    pool.wait_ge(by_act[j], i * NA + an["out"])
                    for h in range(2):
                        dst = y_dram[bass.ds(i * P + j * CH, CH), :].rearrange("t (q p) -> t q p", p=P)
                        pool.dma_start(dst[:, :, h * CH:(h + 1) * CH], yo[j][h * CH:(h + 1) * CH]).then_inc(y_stored[j], 16)
            for j in range(2):
                pool.wait_ge(y_stored[j], 32 * NCH // 2)

        @block.tensor
        def _(pe):
            def group(i, j, bank, width, lhsT, rhs, per_bank, offset=0):
                for p in range(PAIRS):
                    at = ps[j][:, bank + p // per_bank, (p % per_bank) * width:(p % per_bank + 1) * width]
                    mm = nc.tensor.matmul(at, lhsT[:, p], rhs[:, p], start=True, stop=True)
                mm.then_inc(products[j], 1)

            def dve_at(i, j, name):
                pe.wait_ge(by_dve[j], i * ND + dn[name])

            def act_at(i, j, name):
                pe.wait_ge(by_act[j], i * NA + an[name])

            def turn(i, j, bank, src):
                for p in range(PAIRS):
                    mm = nc.tensor.transpose(ps[j][:, bank, p * P:(p + 1) * P], src[:, p], ident[:])
                mm.then_inc(products[j], 1)

            with pe.Fori(0, NCH // 2) as i:
                for j in range(2):
                    pe.wait_ge(loaded[j], i * 160 + 160)
                    pe.wait_ge(by_act[j], i * NA)
                    pe.wait_ge(by_dve[j], i * ND)
                    pe.wait_ge(state, i * 2)
                    group(i, j, 0, 2 * P, B[j], AR[j], 2)
                    group(i, j, 2, 2 * P, K[j], AR[j], 2)
                for j in range(2):
                    dve_at(i, j, "rbt")
                    group(i, j, 0, P, AR[j][:, :, 0:P], B[j], 4)
                    turn(i, j, 1, AR[j][:, :, 0:P])
                    dve_at(i, j, "rkt")
                    turn(i, j, 2, B[j])
                    turn(i, j, 3, K[j])
                for j in range(2):
                    act_at(i, j, "a_tok")
                    group(i, j, 1, CH, LkT[j], V[j], 4)
                for lv in range(LEVELS):
                    for j in range(2):
                        pe.wait_ge(levels[j], i * LEVELS + lv + 1)
                        dve_at(i, j, f"tt{lv - 1}" if lv else "tt_start")
                        if lv == 0:
                            act_at(i, j, "k_tok")
                        group(i, j, 0, P, LTm[j][:, lv], Tm[j], 4)
                    for j in range(2):
                        act_at(i, j, f"y{lv}")
                        if lv == 0:
                            act_at(i, j, "x")
                        if lv < LEVELS - 1:
                            group(i, j, 2, P, TT_[j], Y1[j], 4)
                        group(i, j, 3, P, Y1[j], TT_[j], 4)
                for j in range(2):
                    dve_at(i, j, f"tt{LEVELS - 1}")
                    group(i, j, 0, P + CH, TT_[j], AX[j], 2)
                for j in range(2):
                    act_at(i, j, "wu")
                    group(i, j, 2, 2 * P, WU[j][:, :, 0:P], BR[j], 2)
                for j in range(2):
                    dve_at(i, j, "rw")
                    for p in range(PAIRS):
                        at = ps[j][:, 0, p * CH:(p + 1) * CH]
                        nc.tensor.matmul(at, Ktok[j][:, p], V[j][:, p], start=True, stop=False)
                        nc.tensor.matmul(at, BR[j][:, p, 0:P], WU[j][:, p, P:P + CH], start=False, stop=False)
                        if p == 0:
                            pe.wait_ge(state, i * 2 + j)
                        mm = nc.tensor.matmul(at, GR[j][:, p, 0:P], M[j][:, p], start=False, stop=True)
                    mm.then_inc(products[j], 1)
                    for p in range(PAIRS):
                        at = ps[j][:, 1, p * CH:(p + 1) * CH]
                        nc.tensor.matmul(at, RkT[j][:, p], V[j][:, p], start=True, stop=False)
                        nc.tensor.matmul(at, BR[j][:, p, P:2 * P], WU[j][:, p, P:P + CH], start=False, stop=False)
                        mm = nc.tensor.matmul(at, GR[j][:, p, P:2 * P], M[j][:, p], start=False, stop=True)
                    mm.then_inc(products[j], 1)

        @block.scalar
        def _(act):
            def copy(i, j, name, product, dst, src):
                act.wait_ge(products[j], i * NP_ + pn[product])
                nc.scalar.copy(dst, src).then_inc(by_act[j], 1)

            def bank(j, n, width=P):
                return ps[j][:, n, 0:PAIRS * width].rearrange("p (q c) -> p q c", c=width)

            with act.Fori(0, NCH // 2) as i:
                for j in range(2):
                    copy(i, j, "a_tok", "turn_a", AX[j][:, :, 0:P], bank(j, 1))
                    copy(i, j, "b_tok", "turn_b", BR[j][:, :, 0:P], bank(j, 2))
                    copy(i, j, "k_tok", "turn_k", Ktok[j][:], bank(j, 3))
                for j in range(2):
                    copy(i, j, "x", "x", AX[j][:, :, P:P + CH], bank(j, 1, CH))
                for lv in range(LEVELS):
                    for j in range(2):
                        copy(i, j, f"y{lv}", f"y{lv}", Y1[j][:], bank(j, 0))
                for j in range(2):
                    act.wait_ge(products[j], i * NP_ + pn["wu"])
                    nc.scalar.copy(WU[j][:].rearrange("p (b q) c -> p b (q c)", b=2),
                                   ps[j][:, 0:2, 0:2 * (P + CH)]).then_inc(by_act[j], 1)
                for j in range(2):
                    act.wait_ge(y_stored[j], i * 32)
                    copy(i, j, "out", "out", yo[j][:], bank(j, 1, CH))

        @block.vector
        def _(dve):
            def two(j, first, part):
                return ps[j][:, first:first + 2, :].rearrange("p b (q w c) -> p (b q) w c", q=2, w=2)[:, :, part, :]

            def over_pairs(tile):
                return tile.unsqueeze(1).broadcast_to([P, PAIRS, P])

            def product(i, j, name):
                dve.wait_ge(products[j], i * NP_ + pn[name])

            def own(i, j, name):
                dve.wait_ge(by_dve[j], i * ND + dn[name])

            def op(j, out, in0, in1, how):
                nc.vector.tensor_tensor(out, in0, in1, how).then_inc(by_dve[j], 1)

            def bank(j, n, width=P):
                return ps[j][:, n, 0:PAIRS * width].rearrange("p (q c) -> p q c", c=width)

            dve.wait_ge(masks_in, 64)
            dve.wait_ge(zeroed, 8)
            with dve.Fori(0, NCH // 2) as i:
                for j in range(2):
                    product(i, j, "gram_b")
                    dve.wait_ge(levels[j], i * LEVELS)
                    op(j, LT[j][:], two(j, 0, 0), over_pairs(m_gram[:, 0]), ALU.mult)
                    op(j, BR[j][:, :, P:2 * P], two(j, 0, 1), over_pairs(m_gram[:, 1]), ALU.mult)
                    product(i, j, "gram_k")
                    op(j, LkT[j][:], two(j, 2, 0), over_pairs(m_gram[:, 0]), ALU.mult)
                    op(j, RkT[j][:], two(j, 2, 1), over_pairs(m_gram[:, 1]), ALU.mult)
                for j in range(2):
                    product(i, j, "gram_l")
                    op(j, L[j][:], bank(j, 0), over_pairs(m_low[:]), ALU.mult)
                    own(i, j, "l")
                    op(j, Tm[j][:], L[j][:], over_pairs(m_one[:, 0]), ALU.mult)
                    op(j, TT_[j][:], LT[j][:], over_pairs(m_one[:, 1]), ALU.mult)
                    own(i, j, "t_one")
                    op(j, Tm[j][:], Tm[j][:], over_pairs(ident[:]), ALU.add)
                    own(i, j, "tt_one")
                    op(j, TT_[j][:], TT_[j][:], over_pairs(ident[:]), ALU.add)
                for lv in range(LEVELS):
                    for j in range(2):
                        if lv < LEVELS - 1:
                            product(i, j, f"tt{lv}")
                            op(j, Tm[j][:], bank(j, 2), Tm[j][:], ALU.add)
                        product(i, j, f"tt{lv}")
                        op(j, TT_[j][:], bank(j, 3), TT_[j][:], ALU.add)
                for j in range(2):
                    product(i, j, "gr")
                    op(j, GR[j][:, :, 0:P], two(j, 2, 0), over_pairs(ident[:]), ALU.add)
                    op(j, GR[j][:, :, P:2 * P], two(j, 2, 1), AR[j][:, :, P:2 * P], ALU.add)
                for j in range(2):
                    product(i, j, "s")
                    dve.wait_ge(products[1 - j], i * NP_ + (pn["out"] if j else 0))
                    nc.vector.tensor_tensor(M[1 - j][:], bank(j, 0, CH),
                                            end_decay[:, :, bass.ds(i * 2 + j, 1)].broadcast_to([P, PAIRS, CH]),
                                            ALU.mult).then_inc(state, 1)


def recurrence_tables():
    n = np.arange(P)
    same = n[:, None] // CH == n[None, :] // CH
    s, t = n[:, None] % CH, n[None, :] % CH
    f = np.float32
    decay = -np.exp(f(-0.5))

    def pair_of(m, s, t):
        return same & (s // (2 * m) == t // (2 * m)) & (s // m % 2 == 0) & (t // m % 2 == 1)

    return {
        "tri_decay": np.concatenate([(same & (s <= t)) * decay, (same & (s < t)) * decay], 1).astype(f),
        "pairsum": same.astype(f),
        "head_sel": (n[:, None] // CH == np.arange(2)[None, :]).astype(f),
        "ones_row": np.ones((1, P), f),
        "m_gram": np.stack([same & (s < t), same & (s <= t)], 1).astype(f),
        "m_low": (same & (s > t)).astype(f),
        "m_one": np.stack([pair_of(1, t, s), pair_of(1, s, t)], 1).astype(f),
        "m_lev": np.stack([pair_of(m, s, t) for m in (2, 4, 8, 16, 32)], 1).astype(f),
    }


def mix_transpose(core, tag, o_dram, y_dram, v_dram, bonus, g_tok, gains, consts, hi, lo):
    nc = core.nc
    ident, eps = consts["ident"], consts["eps"]
    H = RW // 64
    with ExitStack() as ctx:
        o = sbuf(nc, ctx, f"{tag}_o", [P, 2, RW])
        y = sbuf(nc, ctx, f"{tag}_y", [P, 2, RW])
        v = sbuf(nc, ctx, f"{tag}_v", [P, 2, RW])
        sq = sbuf(nc, ctx, f"{tag}_sq", [P, 2, RW])
        mixed = sbuf(nc, ctx, f"{tag}_mixed", [P, 2, D])
        rows = sbuf(nc, ctx, f"{tag}_rows", [P, 3, RW])
        ssum = sbuf(nc, ctx, f"{tag}_ssum", [P, 2])
        root = sbuf(nc, ctx, f"{tag}_root", [P, 2, 1 + H])
        rstd = sbuf(nc, ctx, f"{tag}_rstd", [P, 2, 1 + H])
        mean = sbuf(nc, ctx, f"{tag}_mean", [P, H])
        var = sbuf(nc, ctx, f"{tag}_var", [P, 2, H])
        tp = psum(nc, ctx, f"{tag}_tp", [P, 4, 4, P])
        rows_in = core.sem(f"{tag}_rows_in")
        o_in = core.sems(f"{tag}_o_in", 2)
        squared = core.sems(f"{tag}_squared", 2)
        o_root = core.sems(f"{tag}_o_root", 2)
        var_done = core.sems(f"{tag}_var_done", 2)
        y_root = core.sems(f"{tag}_y_root", 2)
        step = core.sems(f"{tag}_step", 2)
        v_scaled = core.sems(f"{tag}_v_scaled", 2)
        turned = core.sems(f"{tag}_turned", 2)
        hi_done = core.sems(f"{tag}_hi_done", 2)
        lo_done = core.sems(f"{tag}_lo_done", 2)
        block = ctx.enter_context(nc.Block())
        STEPS = 11

        def heads(tile):
            return tile.rearrange("p (h c) -> p h c", h=H)

        def per_head(tile):
            return tile.unsqueeze(2).broadcast_to([P, H, 64])

        @block.sync
        def _(sp):
            for n, g in enumerate(gains):
                sp.dma_start(rows[:, n, :], g.rearrange("(o n) -> o n", o=1).broadcast_to([P, RW])).then_inc(rows_in, 16)
            with sp.Fori(0, TT // 2) as i:
                for b in range(2):
                    first = sp.snap((i * 2 + b) * P)
                    sp.wait_ge(step[b], i * STEPS)
                    for dst, src in ((o, o_dram), (y, y_dram), (v, v_dram)):
                        sp.dma_start(dst[:, b, :], src[bass.ds(first, P), :]).then_inc(o_in[b], 16)

        @block.gpsimd
        def _(pool):
            with pool.Fori(0, TT // 2) as i:
                for b in range(2):
                    pool.wait_ge(o_in[b], i * 48 + 48)
                    nc.gpsimd.tensor_tensor(heads(v[:, b, :]), heads(v[:, b, :]),
                                            per_head(bonus[:, bass.ds(i * 2 + b, 1), :].rearrange("p o h -> p (o h)")),
                                            ALU.mult).then_inc(v_scaled[b], 1)

        @block.scalar
        def _(act):
            with act.Fori(0, TT // 2) as i:
                for b in range(2):
                    act.wait_ge(o_in[b], i * 48 + 48)
                    act.wait_ge(step[b], i * STEPS)
                    nc.scalar.activation(sq[:, b, :], o[:, b, :], ACT.Square, accum_out=ssum[:, b:b + 1]
                                         ).then_inc(squared[b], 1)
                    act.wait_ge(squared[b], i + 1)
                    nc.scalar.activation(root[:, b, 0:1], ssum[:, b:b + 1], ACT.Sqrt, bias=eps[:, 0:1],
                                         scale=1.0 / RW).then_inc(o_root[b], 1)
                    act.wait_ge(var_done[b], i + 1)
                    nc.scalar.activation(root[:, b, 1:1 + H], var[:, b, :], ACT.Sqrt, bias=eps[:, 1:2],
                                         scale=1.0 / 64).then_inc(y_root[b], 1)
                for b in range(2):
                    act.wait_ge(turned[b], i + 1)
                    for k in range(2):
                        nc.scalar.copy(hi[:, 4 * k:4 * k + 4, bass.ds((i * 2 + b) * P, P)], tp[:, 2 * b + k]
                                       ).then_inc(hi_done[b], 1)

        @block.vector
        def _(dve):
            dve.wait_ge(rows_in, 48)
            with dve.Fori(0, TT // 2) as i:
                for b in range(2):
                    base = i * STEPS
                    yh = heads(y[:, b, :])
                    dve.wait_ge(o_in[b], i * 48 + 48)
                    nc.vector.tensor_reduce(mean[:], yh, AX_X, ALU.add).then_inc(step[b], 1)
                    dve.wait_ge(step[b], base + 1)
                    nc.vector.tensor_scalar(mean[:], mean[:], 1.0 / 64, None, ALU.mult).then_inc(step[b], 1)
                    dve.wait_ge(step[b], base + 2)
                    nc.vector.tensor_tensor(yh, yh, per_head(mean[:]), ALU.subtract).then_inc(step[b], 1)
                    dve.wait_ge(step[b], base + 3)
                    dve.wait_ge(squared[b], i + 1)
                    nc.vector.tensor_tensor(sq[:, b, :], y[:, b, :], y[:, b, :], ALU.mult).then_inc(step[b], 1)
                    dve.wait_ge(step[b], base + 4)
                    nc.vector.tensor_reduce(var[:, b, :], heads(sq[:, b, :]), AX_X, ALU.add).then_inc(var_done[b], 1)
                    dve.wait_ge(o_root[b], i + 1)
                    dve.wait_ge(y_root[b], i + 1)
                    nc.vector.reciprocal(rstd[:, b, :], root[:, b, :]).then_inc(step[b], 1)
                    dve.wait_ge(step[b], base + 5)
                    dve.wait_ge(turned[b], i)
                    nc.vector.scalar_tensor_tensor(out=mixed[:, b, 0:RW], in0=o[:, b, :], scalar=rstd[:, b, 0:1],
                                                   in1=rows[:, 0, :], op0=ALU.mult, op1=ALU.mult).then_inc(step[b], 1)
                    nc.vector.tensor_tensor(yh, yh, per_head(rstd[:, b, 1:1 + H]), ALU.mult).then_inc(step[b], 1)
                    dve.wait_ge(step[b], base + 7)
                    nc.vector.tensor_tensor(y[:, b, :], y[:, b, :], rows[:, 1, :], ALU.mult).then_inc(step[b], 1)
                    dve.wait_ge(step[b], base + 8)
                    nc.vector.tensor_tensor(y[:, b, :], y[:, b, :], rows[:, 2, :], ALU.add).then_inc(step[b], 1)
                    dve.wait_ge(step[b], base + 9)
                    dve.wait_ge(v_scaled[b], i + 1)
                    nc.vector.tensor_tensor(y[:, b, :], y[:, b, :], v[:, b, :], ALU.add).then_inc(step[b], 1)
                    dve.wait_ge(step[b], base + 10)
                    nc.vector.tensor_tensor(mixed[:, b, RW:D], y[:, b, :],
                                            g_tok[:, bass.ds(i * 2 + b, 1), :].rearrange("p o c -> p (o c)"),
                                            ALU.mult).then_inc(step[b], 1)
                for b in range(2):
                    for k in range(2):
                        dve.wait_ge(hi_done[b], i * 2 + k + 1)
                        at = (slice(None), slice(4 * k, 4 * k + 4), bass.ds((i * 2 + b) * P, P))
                        nc.vector.tensor_tensor(lo[at], tp[:, 2 * b + k], hi[at].bitcast(F32),
                                                ALU.subtract).then_inc(lo_done[b], 1)

        @block.tensor
        def _(pe):
            with pe.Fori(0, TT // 2) as i:
                for b in range(2):
                    pe.wait_ge(step[b], i * STEPS + STEPS)
                    pe.wait_ge(lo_done[b], i * 2)
                    for k in range(KD):
                        last = nc.tensor.transpose(tp[:, 2 * b + k // 4, k % 4, :], mixed[:, b, k * P:(k + 1) * P], ident[:])
                    last.then_inc(turned[b], 1)


def token_product(core, tag, w, hi, lo, tiles, y):
    nc = core.nc
    STEP = 4
    with ExitStack() as ctx:
        raw = sbuf(nc, ctx, f"{tag}_raw", [P, 2, D])
        w_hi = sbuf(nc, ctx, f"{tag}_wh", [P, KD, D], F32R)
        w_lo = sbuf(nc, ctx, f"{tag}_wl", [P, KD, D], F32R)
        ps = psum(nc, ctx, f"{tag}_ps", [P, 8, HALF])
        loaded = core.sems(f"{tag}_loaded", 2)
        hi_done = core.sem(f"{tag}_hi_done")
        lo_done = core.sem(f"{tag}_lo_done")
        multiplied = core.sem(f"{tag}_multiplied")
        copied = core.sems(f"{tag}_copied", 2)
        block = ctx.enter_context(nc.Block())
        groups = [range(t, min(t + STEP, tiles)) for t in range(0, tiles, STEP)]

        @block.sync
        def _(sp):
            for k in range(KD):
                if k >= 2:
                    sp.wait_ge(lo_done, k - 1)
                sp.dma_start(raw[:, k % 2, :], w[k * P:(k + 1) * P, :]).then_inc(loaded[k % 2], 16)

        @block.scalar
        def _(act):
            for k in range(KD):
                act.wait_ge(loaded[k % 2], 16 * (k // 2 + 1))
                nc.scalar.copy(w_hi[:, k, :], raw[:, k % 2, :]).then_inc(hi_done, 1)
            done = 0
            for g in groups:
                for n in range(2 * len(g)):
                    if n % 2 == 0:
                        act.wait_ge(multiplied, done + n + 1)
                        nc.scalar.copy(y[:, g[0] + n // 2, 0:HALF], ps[:, n, :]).then_inc(copied[0], 1)
                done += 2 * len(g)

        @block.vector
        def _(dve):
            for k in range(KD):
                dve.wait_ge(hi_done, k + 1)
                nc.vector.tensor_tensor(w_lo[:, k, :], raw[:, k % 2, :], w_hi[:, k, :].bitcast(F32),
                                        ALU.subtract).then_inc(lo_done, 1)
            done = 0
            for g in groups:
                for n in range(2 * len(g)):
                    if n % 2 == 1:
                        dve.wait_ge(multiplied, done + n + 1)
                        nc.vector.tensor_copy(y[:, g[0] + n // 2, HALF:D], ps[:, n, :]).then_inc(copied[1], 1)
                done += 2 * len(g)

        @block.tensor
        def _(pe):
            done = 0
            for g in groups:
                for k in range(KD):
                    pe.wait_ge(lo_done, k + 1)
                    for n in range(2 * len(g)):
                        rows = slice((g[0] + n // 2) * P, (g[0] + n // 2 + 1) * P)
                        cols = slice(n % 2 * HALF, (n % 2 + 1) * HALF)
                        if k == 0 and done:
                            pe.wait_ge(copied[n % 2], done // 2 - len(g) + n // 2 + 1)
                        nc.tensor.matmul(ps[:, n, :], hi[:, k, rows], w_hi[:, k, cols], start=(k == 0), stop=False)
                        nc.tensor.matmul(ps[:, n, :], hi[:, k, rows], w_lo[:, k, cols], start=False, stop=False)
                        mm = nc.tensor.matmul(ps[:, n, :], lo[:, k, rows], w_hi[:, k, cols], start=False, stop=(k == KD - 1))
                        if k == KD - 1:
                            mm.then_inc(multiplied, 1)
                done += 2 * len(g)


def memory_attention(core, tag, qT_dram, kT_dram, v, consts, hi, lo):
    nc = core.nc
    ident = consts["ident"]
    MH, MD, MT = 4, 256, 256
    SCALE = MD ** -0.5
    with ExitStack() as ctx:
        q = sbuf(nc, ctx, f"{tag}_q", [P, 2, 2, T])
        kT = sbuf(nc, ctx, f"{tag}_k", [P, 2, 2, MT])
        vh = sbuf(nc, ctx, f"{tag}_v", [P, 2, 2, MD])
        prob = sbuf(nc, ctx, f"{tag}_prob", [P, 2, MT])
        top = sbuf(nc, ctx, f"{tag}_top", [P, 2])
        bias = sbuf(nc, ctx, f"{tag}_bias", [P, 2])
        den = sbuf(nc, ctx, f"{tag}_den", [P, 2])
        rden = sbuf(nc, ctx, f"{tag}_rden", [P, 2])
        probT = sbuf(nc, ctx, f"{tag}_probT", [P, 2, 2, HALF])
        s_ps = psum(nc, ctx, f"{tag}_s_ps", [P, 2, HALF])
        t_ps = psum(nc, ctx, f"{tag}_t_ps", [P, 2, HALF])
        o_ps = psum(nc, ctx, f"{tag}_o_ps", [P, 4, HALF])
        loaded = core.sems(f"{tag}_loaded", 2)
        v_copied = core.sems(f"{tag}_v_copied", 2)
        scored = core.sem(f"{tag}_scored")
        maxed = core.sem(f"{tag}_maxed")
        biased = core.sem(f"{tag}_biased")
        exped = core.sem(f"{tag}_exped")
        inverted = core.sem(f"{tag}_inverted")
        scaled = core.sem(f"{tag}_scaled")
        flipped = core.sem(f"{tag}_flipped")
        copied = core.sem(f"{tag}_copied")
        summed = core.sem(f"{tag}_summed")
        hi_done = core.sem(f"{tag}_hi_done")
        lo_done = core.sem(f"{tag}_lo_done")
        block = ctx.enter_context(nc.Block())
        TILES = 2 * TT

        @block.sync
        def _(sp):
            with sp.Fori(0, MH // 2) as n:
                for b in range(2):
                    row = sp.snap((n * 2 + b) * MD)
                    sp.wait_ge(summed, n * 8)
                    sp.dma_start(q[:, b], qT_dram[bass.ds(row, MD), :].rearrange("(c p) t -> p c t", p=P)).then_inc(loaded[b], 16)
                    sp.dma_start(kT[:, b], kT_dram[bass.ds(row, MD), :].rearrange("(c p) t -> p c t", p=P)).then_inc(loaded[b], 16)

        @block.gpsimd
        def _(pool):
            with pool.Fori(0, MH // 2) as n:
                for b in range(2):
                    pool.wait_ge(summed, n * 8)
                    nc.gpsimd.tensor_copy(vh[:, b], v[:, :, bass.ds((n * 2 + b) * MD, MD)]).then_inc(v_copied[b], 1)

        @block.tensor
        def _(pe):
            def score(n, s):
                b, i = s // TT, s % TT
                if i == 0:
                    pe.wait_ge(loaded[b], n * 32 + 32)
                pe.wait_ge(exped, n * TILES + max(s - 1, 0))
                for c in range(2):
                    mm = nc.tensor.matmul(s_ps[:, s % 2, 0:MT], q[:, b, c, i * P:(i + 1) * P], kT[:, b, c, :],
                                          start=(c == 0), stop=(c == 1))
                mm.then_inc(scored, 1)

            def turn(n, s):
                pe.wait_ge(scaled, n * TILES + s + 1)
                pe.wait_ge(copied, n * TILES + max(s - 1, 0))
                for c in range(2):
                    mm = nc.tensor.transpose(t_ps[:, s % 2, c * P:(c + 1) * P], prob[:, s % 2, c * P:(c + 1) * P], ident[:])
                mm.then_inc(flipped, 1)

            def values(n, s):
                b, half = s // TT, s % TT // 4
                pe.wait_ge(copied, n * TILES + s + 1)
                if s == 3:
                    pe.wait_ge(v_copied[0], n + 1)
                if s == TT + 3:
                    pe.wait_ge(v_copied[1], n + 1)
                for c in range(2):
                    m = s // 4 * 2 + c
                    pe.wait_ge(lo_done, n * 8 + max(m - 3, 0))
                    for kt in range(2):
                        mm = nc.tensor.matmul(o_ps[:, m % 4, :], vh[:, b, kt, c * P:(c + 1) * P], probT[:, half, kt, :],
                                              start=(kt == 0), stop=(kt == 1))
                    mm.then_inc(summed, 1)

            with pe.Fori(0, MH // 2) as n:
                score(n, 0)
                for s in range(TILES):
                    if s + 1 < TILES:
                        score(n, s + 1)
                    turn(n, s)
                    if s % 4 == 0 and s:
                        values(n, s - 1)
                values(n, TILES - 1)

        @block.scalar
        def _(act):
            def exps(n, s):
                act.wait_ge(biased, n * TILES + s + 1)
                act.wait_ge(flipped, n * TILES + max(s - 1, 0))
                nc.scalar.activation(prob[:, s % 2, :], s_ps[:, s % 2, 0:MT], ACT.Exp, bias=bias[:, s % 2:s % 2 + 1],
                                     scale=SCALE, accum_out=den[:, s % 2:s % 2 + 1]).then_inc(exped, 1)

            def out(n, m):
                b, half, c = m // 4, m // 2 % 2, m % 2
                act.wait_ge(summed, n * 8 + m + 1)
                nc.scalar.copy(hi[:, bass.ds((n * 2 + b) * 2 + c, 1), half * HALF:(half + 1) * HALF].rearrange("p o c -> p (o c)"),
                               o_ps[:, m % 4, :]).then_inc(hi_done, 1)

            with act.Fori(0, MH // 2) as n:
                exps(n, 0)
                for s in range(TILES):
                    if s + 1 < TILES:
                        exps(n, s + 1)
                    act.wait_ge(flipped, n * TILES + s + 1)
                    act.wait_ge(summed, n * 8 + (max(s // 4 - 1, 0)) * 2)
                    nc.scalar.copy(probT[:, s // 4 % 2, :, s % 4 * P:(s % 4 + 1) * P],
                                   t_ps[:, s % 2, 0:MT].rearrange("p (c t) -> p c t", c=2)).then_inc(copied, 1)
                    if s % 4 == 1 and s > 4:
                        out(n, s // 4 * 2 - 2)
                        out(n, s // 4 * 2 - 1)
                out(n, 6)
                out(n, 7)

        @block.vector
        def _(dve):
            def bias_of(n, s):
                dve.wait_ge(scored, n * TILES + s + 1)
                nc.vector.tensor_reduce(top[:, s % 2:s % 2 + 1], s_ps[:, s % 2, 0:MT], AX_X, ALU.max).then_inc(maxed, 1)
                dve.wait_ge(maxed, n * TILES + s + 1)
                nc.vector.tensor_scalar(bias[:, s % 2:s % 2 + 1], top[:, s % 2:s % 2 + 1], -SCALE, None,
                                        ALU.mult).then_inc(biased, 1)

            def out(n, m):
                b, half, c = m // 4, m // 2 % 2, m % 2
                dve.wait_ge(hi_done, n * 8 + m + 1)
                at = (slice(None), bass.ds((n * 2 + b) * 2 + c, 1), slice(half * HALF, (half + 1) * HALF))
                nc.vector.tensor_tensor(lo[at].rearrange("p o c -> p (o c)"), o_ps[:, m % 4, :],
                                        hi[at].bitcast(F32).rearrange("p o c -> p (o c)"),
                                        ALU.subtract).then_inc(lo_done, 1)

            with dve.Fori(0, MH // 2) as n:
                bias_of(n, 0)
                for s in range(TILES):
                    if s + 1 < TILES:
                        bias_of(n, s + 1)
                    dve.wait_ge(exped, n * TILES + s + 1)
                    nc.vector.reciprocal(rden[:, s % 2:s % 2 + 1], den[:, s % 2:s % 2 + 1]).then_inc(inverted, 1)
                    dve.wait_ge(inverted, n * TILES + s + 1)
                    nc.vector.tensor_scalar(prob[:, s % 2, :], prob[:, s % 2, :], rden[:, s % 2:s % 2 + 1], None,
                                            ALU.mult).then_inc(scaled, 1)
                    if s % 4 == 2 and s > 4:
                        out(n, s // 4 * 2 - 2)
                        out(n, s // 4 * 2 - 1)
                out(n, 6)
                out(n, 7)


def block_kernel(nc, a, out):
    f = {n: (v[0] if len(v.shape) > 1 and v.shape[0] == 1 and n not in ("ones_row",) else v) for n, v in a.items()}

    def scratch(name, shape):
        return nc.dram_tensor(name, shape, F32, kind="Internal").ap()

    x0, mem, dst = f["x"], f["mem"], out[0]
    x1, x2, x3 = scratch("x1", (T, D)), scratch("x2", (T, D)), scratch("x3", (T, D))
    projT = scratch("projT", (10 * P, T))
    z = scratch("z", (14 * P, T))
    ropeT = scratch("ropeT", (6 * P, T))
    v_tok = [scratch("v_slc", (T, P)), scratch("v_win", (T, P))]
    rv_tok = scratch("rv_tok", (T, RW))
    kc, vc = scratch("kc", (64, 126)), scratch("vc", (63, P))
    o_nsa, y_rwkv = scratch("o_nsa", (T, RW)), scratch("y_rwkv", (T, RW))
    ops_dram = scratch("ops", (4, RW, T))
    qm, km = scratch("qm", (D, T)), scratch("km", (D, 256))

    core = Core(nc)
    with ExitStack() as ctx:
        consts = make_consts(core, ctx, f["ident_"])
        hi = sbuf(nc, ctx, "hT_hi", [P, KD, T], F32R)
        lo = sbuf(nc, ctx, "hT_lo", [P, KD, T], F32R)

        def ffn(n, x_in, x_out):
            with ExitStack() as inner:
                y = sbuf(nc, inner, f"ffn{n}_y", [P, TT, D])
                norm_transpose(core, f"n{n}", x_in, f[f"ffn{n}_pre_g"], TT, consts, hi, lo)
                ffn_products(core, f"f{n}", f[f"ffn{n}_w_gate"], f[f"ffn{n}_w_up"], f[f"ffn{n}_w_down"], hi, lo, y)
                residual(core, f"r{n}", x_in, y, f[f"ffn{n}_post_g"], 0.5, consts, x_out)
            core.clear()

        ffn(1, x0, x1)
        with ExitStack() as mixer:
            gates = sbuf(nc, mixer, "gates", [P, TT, 24])
            norm_transpose(core, "nm", x1, f["mix_pre_g"], TT, consts, hi, lo)
            gate_product(core, "gp", f["w_in"], 10 * P, 24, hi, lo, gates)
            feature_product(core, "pn", f["w_in"], 0, 10, hi, lo, T, projT, 0)
            feature_product(core, "pr", f["w_in"], 10 * P + 24, 14, hi, lo, T, z, 0, mix=f["rwkv_mu"])
            core.clear()
            with ExitStack() as inner:
                masks = load_masks(core, inner, f)
                compress(core, "cp", projT, 4 * P, 5 * P, [f[f"cmp_{n}_k"] for n in ("pe", "w1", "w2")],
                         [f[f"cmp_{n}_v"] for n in ("pe", "w1", "w2")], f["ccos"], f["csin"], kc, vc)
                rotate_and_turn(core, "rt", projT, f["cos_t"], f["sin_t"], [0, P, 2 * P, 3 * P, 6 * P, 8 * P], ropeT,
                                [(projT, 7 * P), (projT, 9 * P)] + [(z, (8 + n) * P) for n in range(PAIRS)],
                                v_tok + [rv_tok[:, n * P:(n + 1) * P] for n in range(PAIRS)], consts)
                nsa_attention(core, "at", ropeT, kc, v_tok, vc, gates, consts, masks, o_nsa)
            core.clear()
            bonus = sbuf(nc, mixer, "bonus", [P, TT, 8])
            g_tok = sbuf(nc, mixer, "g_tok", [P, TT, RW])
            end_decay = sbuf(nc, mixer, "end_decay", [P, PAIRS, NCH])
            par = [f[f"rwkv_{n}"] for n in ("w0", "w2", "a0", "a2", "g2", "k_k", "k_a", "r_k")]
            rwkv_prepare(core, "rp", z, par, consts, f, ops_dram, end_decay, bonus, g_tok)
            rwkv_chunks(core, "rc", ops_dram, rv_tok, end_decay, consts, f, y_rwkv)
            core.clear()
            mix_transpose(core, "mt", o_nsa, y_rwkv, rv_tok, bonus, g_tok,
                          [f["nsa_out_g"], f["rwkv_gn_g"], f["rwkv_gn_b"]], consts, hi, lo)
            with ExitStack() as inner:
                y = sbuf(nc, inner, "mix_y", [P, TT, D])
                token_product(core, "wo", f["w_out"], hi, lo, TT, y)
                residual(core, "rm", x1, y, f["mix_post_g"], 1.0, consts, x2)
            core.clear()

        with ExitStack() as inner:
            v = sbuf(nc, inner, "mem_v", [P, 2, D])
            norm_transpose(core, "nk", mem, f["mem_kv_g"], 2, consts, hi, lo)
            feature_product(core, "pk", f["mem_wk"], 0, KD, hi, lo, 256, km, 0)
            token_product(core, "pv", f["mem_wv"], hi, lo, 2, v)
            norm_transpose(core, "nq", x2, f["mem_pre_g"], TT, consts, hi, lo)
            feature_product(core, "pq", f["mem_wq"], 0, KD, hi, lo, T, qm, 0)
            core.clear()
            memory_attention(core, "ma", qm, km, v, consts, hi, lo)
        with ExitStack() as inner:
            y = sbuf(nc, inner, "mem_y", [P, TT, D])
            token_product(core, "mo", f["mem_wo"], hi, lo, TT, y)
            residual(core, "rq", x2, y, f["mem_post_g"], 1.0, consts, x3)
        core.clear()
        ffn(2, x3, dst)


_INS = ['x', 'mem',
        'ffn1_pre_g', 'ffn1_w_gate', 'ffn1_w_up', 'ffn1_w_down', 'ffn1_post_g',
        'mix_pre_g', 'w_in', 'cmp_pe_k', 'cmp_w1_k', 'cmp_w2_k', 'cmp_pe_v', 'cmp_w1_v', 'cmp_w2_v', 'nsa_out_g',
        'rwkv_mu', 'rwkv_w0', 'rwkv_w2', 'rwkv_a0', 'rwkv_a2', 'rwkv_g2', 'rwkv_k_k', 'rwkv_k_a', 'rwkv_r_k',
        'rwkv_gn_g', 'rwkv_gn_b', 'w_out', 'mix_post_g',
        'mem_pre_g', 'mem_kv_g', 'mem_wq', 'mem_wk', 'mem_wv', 'mem_wo', 'mem_post_g',
        'ffn2_pre_g', 'ffn2_w_gate', 'ffn2_w_up', 'ffn2_w_down', 'ffn2_post_g']


def kernel(**inputs):
    import numpy as _np
    import concourse.bacc as _bacc
    from concourse import mybir as _mybir
    from concourse.bass_utils import run_bass_kernel_spmd as _run

    nc = _bacc.Bacc("TRN2", target_bir_lowering=False, num_devices=1)
    arrays = {f"in_{n}": _np.ascontiguousarray(inputs[n]) for n in _INS}
    arrays.update({f"in_{n}": _np.ascontiguousarray(v) for n, v in shape_tables().items()})
    a = {n[3:]: nc.dram_tensor(n, v.shape, _mybir.dt.from_np(v.dtype), kind="ExternalInput").ap()
         for n, v in arrays.items()}
    out = nc.dram_tensor("out_0", (1, T, D), F32, kind="ExternalOutput").ap()
    block_kernel(nc, a, out)
    r = _run(nc, [arrays], core_ids=[0])
    return r.results[0]["out_0"]
```

```python
from contextlib import ExitStack

import numpy as np

import concourse.bass as bass
from concourse import mybir

P = 128
F32 = mybir.dt.float32
F32R = mybir.dt.float32r
BF16 = mybir.dt.bfloat16
ALU = mybir.AluOpType
ACT = mybir.ActivationFunctionType
AX_X = mybir.AxisListType.X

D = 1024
T = 1024
KD = D // P
TT = T // P
HALF = 512
NORM_EPS = 1e-6
GROUP_EPS = 64e-5


class Core:

    def __init__(self, nc):
        self.nc, self.taken = nc, []

    def sem(self, name):
        self.taken.append(self.nc.alloc_semaphore(name=name))
        return self.taken[-1]

    def sems(self, name, n):
        return [self.sem(f"{name}{i}") for i in range(n)]

    def pool_dma_sems(self, name, n):
        return [self.nc.alloc_semaphore(name=f"{name}{i}") for i in range(n)]

    def clear(self):
        nc = self.nc
        with nc.Block() as block:
            @block.sync
            def _(sp):
                for s in self.taken:
                    sp.sem_clear(s)
        for s in self.taken:
            nc.release_semaphore(s)
        self.taken = []


def sbuf(nc, ctx, name, shape, dt=F32):
    return ctx.enter_context(nc.sbuf_tensor(name, shape, dt))


def psum(nc, ctx, name, shape, dt=F32):
    return ctx.enter_context(nc.psum_tensor(name, shape, dt))


def norm_transpose(core, tag, src, gain, tiles, consts, hi, lo):
    nc = core.nc
    ident, eps = consts["ident"], consts["eps"]
    with ExitStack() as ctx:
        x = sbuf(nc, ctx, f"{tag}_x", [P, 2, D])
        xn = sbuf(nc, ctx, f"{tag}_xn", [P, 2, D])
        sq = sbuf(nc, ctx, f"{tag}_sq", [P, 2, D])
        g = sbuf(nc, ctx, f"{tag}_g", [P, KD])
        ssum = sbuf(nc, ctx, f"{tag}_ssum", [P, 2])
        root = sbuf(nc, ctx, f"{tag}_root", [P, 2])
        rstd = sbuf(nc, ctx, f"{tag}_rstd", [P, 2])
        tp = psum(nc, ctx, f"{tag}_tp", [P, 4, 4, P])
        g_loaded = core.sem(f"{tag}_g_loaded")
        x_loaded = core.sems(f"{tag}_x_loaded", 2)
        squared = core.sems(f"{tag}_squared", 2)
        rooted = core.sems(f"{tag}_rooted", 2)
        inverted = core.sems(f"{tag}_inverted", 2)
        scaled = core.sems(f"{tag}_scaled", 2)
        turned = core.sems(f"{tag}_turned", 2)
        hi_done = core.sems(f"{tag}_hi_done", 2)
        lo_done = core.sems(f"{tag}_lo_done", 2)
        block = ctx.enter_context(nc.Block())

        @block.sync
        def _(sp):
            with nc.allow_non_contiguous_dma("gain per feature"):
                sp.dma_start(g[:], gain.rearrange("(k p) -> p k", p=P)).then_inc(g_loaded, 16)
            with sp.Fori(0, tiles // 2) as i:
                for b in range(2):
                    sp.wait_ge(scaled[b], i)
                    sp.dma_start(x[:, b, :], src[bass.ds((i * 2 + b) * P, P), :]).then_inc(x_loaded[b], 16)

        @block.scalar
        def _(act):
            act.wait_ge(g_loaded, 16)
            with act.Fori(0, tiles // 2) as i:
                for b in range(2):
                    act.wait_ge(x_loaded[b], i * 16 + 16)
                    nc.scalar.activation(sq[:, b, :], x[:, b, :], ACT.Square,
                                         accum_out=ssum[:, b:b + 1]).then_inc(squared[b], 1)
                    act.wait_ge(squared[b], i + 1)
                    act.wait_ge(inverted[b], i)
                    nc.scalar.activation(root[:, b:b + 1], ssum[:, b:b + 1], ACT.Sqrt, bias=eps[:, 0:1],
                                         scale=1.0 / D).then_inc(rooted[b], 1)
                for b in range(2):
                    act.wait_ge(turned[b], i + 1)
                    for k in range(KD):
                        nc.scalar.activation(hi[:, k, bass.ds((i * 2 + b) * P, P)], tp[:, 2 * b + k // 4, k % 4, :],
                                             ACT.Copy, scale=g[:, k:k + 1]).then_inc(hi_done[b], 1)

        @block.vector
        def _(dve):
            dve.wait_ge(g_loaded, 16)
            with dve.Fori(0, tiles // 2) as i:
                for b in range(2):
                    dve.wait_ge(rooted[b], i + 1)
                    nc.vector.reciprocal(rstd[:, b:b + 1], root[:, b:b + 1]).then_inc(inverted[b], 1)
                    dve.wait_ge(inverted[b], i + 1)
                    dve.wait_ge(turned[b], i)
                    nc.vector.tensor_scalar(xn[:, b, :], x[:, b, :], rstd[:, b:b + 1], None,
                                            ALU.mult).then_inc(scaled[b], 1)
                for b in range(2):
                    dve.wait_ge(turned[b], i + 1)
                    for k in range(KD):
                        dve.wait_ge(hi_done[b], i * KD + k // 4 * 4 + 4)
                        at = (slice(None), k, bass.ds((i * 2 + b) * P, P))
                        nc.vector.scalar_tensor_tensor(
                            out=lo[at], in0=tp[:, 2 * b + k // 4, k % 4, :], scalar=g[:, k:k + 1],
                            in1=hi[at].bitcast(F32), op0=ALU.mult, op1=ALU.subtract).then_inc(lo_done[b], 1)

        @block.tensor
        def _(pe):
            with pe.Fori(0, tiles // 2) as i:
                for b in range(2):
                    pe.wait_ge(scaled[b], i + 1)
                    pe.wait_ge(lo_done[b], i * KD)
                    for k in range(KD):
                        last = nc.tensor.transpose(tp[:, 2 * b + k // 4, k % 4, :],
                                                   xn[:, b, k * P:(k + 1) * P], ident[:])
                    last.then_inc(turned[b], 1)


def ffn_products(core, tag, w_gate, w_up, w_down, hi, lo, y):
    nc = core.nc
    F = w_gate.shape[1]
    PAIRS = F // (2 * P)
    with ExitStack() as ctx:
        raw = [sbuf(nc, ctx, f"{tag}_raw{n}", [P, KD, 2 * P]) for n in "gu"]
        raw_d = sbuf(nc, ctx, f"{tag}_rawd", [P, 2, D])
        w_hi = [[sbuf(nc, ctx, f"{tag}_{n}{j}h", [P, KD, P], F32R) for n in "gu"] for j in range(2)]
        w_lo = [[sbuf(nc, ctx, f"{tag}_{n}{j}l", [P, KD, P], F32R) for n in "gu"] for j in range(2)]
        d_hi = [sbuf(nc, ctx, f"{tag}_d{j}h", [P, D], F32R) for j in range(2)]
        d_lo = [sbuf(nc, ctx, f"{tag}_d{j}l", [P, D], F32R) for j in range(2)]
        a_hi = [sbuf(nc, ctx, f"{tag}_a{j}h", [P, T], F32R) for j in range(2)]
        a_lo = [sbuf(nc, ctx, f"{tag}_a{j}l", [P, T], F32R) for j in range(2)]
        silu = sbuf(nc, ctx, f"{tag}_silu", [P, 2, HALF])
        prod = sbuf(nc, ctx, f"{tag}_prod", [P, 2, HALF])
        gate_ps = psum(nc, ctx, f"{tag}_gate_ps", [P, 2, HALF])
        up_ps = psum(nc, ctx, f"{tag}_up_ps", [P, 2, HALF])
        down_ps = psum(nc, ctx, f"{tag}_down_ps", [P, 4, HALF])
        gu_loaded = core.sem(f"{tag}_gu_loaded")
        d_loaded = core.sem(f"{tag}_d_loaded")
        gu_hi = core.sem(f"{tag}_gu_hi")
        gu_lo = core.sem(f"{tag}_gu_lo")
        dn_hi = core.sem(f"{tag}_dn_hi")
        dn_lo = core.sem(f"{tag}_dn_lo")
        gu_mm = core.sems(f"{tag}_gu_mm", 2)
        silu_done = core.sems(f"{tag}_silu_done", 2)
        prod_done = core.sems(f"{tag}_prod_done", 2)
        a_hi_done = core.sems(f"{tag}_a_hi_done", 2)
        a_ready = core.sems(f"{tag}_a_ready", 2)
        dn_mm = core.sems(f"{tag}_dn_mm", 4)
        added = core.sems(f"{tag}_added", 4)
        y_zeroed = core.sem(f"{tag}_y_zeroed")
        block = ctx.enter_context(nc.Block())

        gu_dram = [w.rearrange("(k p) n -> p k n", p=P) for w in (w_gate, w_up)]
        d_dram = w_down.rearrange("(c p) n -> p c n", p=P)

        @block.gpsimd
        def _(pool):
            nc.gpsimd.memset(y[:], 0.0).then_inc(y_zeroed, 1)

        @block.sync
        def _(sp):
            with sp.Fori(0, PAIRS) as i:
                sp.wait_ge(gu_lo, i * 4)
                for n in range(2):
                    sp.dma_start(raw[n][:], gu_dram[n][:, :, bass.ds(i * 2 * P, 2 * P)]).then_inc(gu_loaded, 16)
                sp.wait_ge(dn_lo, i * 2)
                sp.dma_start(raw_d[:], d_dram[:, bass.ds(i * 2, 2), :]).then_inc(d_loaded, 16)

        @block.scalar
        def _(act):
            def body(i, last):
                for j in range(2):
                    for h in range(2):
                        act.wait_ge(gu_mm[h], i * 2 + j + 1)
                        act.wait_ge(prod_done[h], i * 2 + j)
                        nc.scalar.activation(silu[:, h, :], gate_ps[:, h, :], ACT.Silu).then_inc(silu_done[h], 1)
                        act.wait_ge(prod_done[h], i * 2 + j + 1)
                        nc.scalar.copy(a_hi[j][:, h * HALF:(h + 1) * HALF], prod[:, h, :]).then_inc(a_hi_done[h], 1)
                        if j == 0 and h == 0:
                            act.wait_ge(d_loaded, i * 16 + 16)
                            for c in range(2):
                                nc.scalar.copy(d_hi[c][:], raw_d[:, c, :]).then_inc(dn_hi, 1)
                    if not last:
                        if j == 0:
                            act.wait_ge(gu_loaded, i * 32 + 64)
                        for n in range(2):
                            nc.scalar.copy(w_hi[j][n][:], raw[n][:, :, j * P:(j + 1) * P]).then_inc(gu_hi, 1)

            act.wait_ge(gu_loaded, 32)
            for j in range(2):
                for n in range(2):
                    nc.scalar.copy(w_hi[j][n][:], raw[n][:, :, j * P:(j + 1) * P]).then_inc(gu_hi, 1)
            with act.Fori(0, PAIRS - 1) as i:
                body(i, False)
            body(PAIRS - 1, True)

        @block.vector
        def _(dve):
            def split_lo(pair, j):
                for n in range(2):
                    dve.wait_ge(gu_hi, pair * 4 + 2 * j + n + 1)
                    nc.vector.tensor_tensor(w_lo[j][n][:], raw[n][:, :, j * P:(j + 1) * P],
                                            w_hi[j][n][:].bitcast(F32), ALU.subtract).then_inc(gu_lo, 1)

            def body(i, last):
                for j in range(2):
                    for h in range(2):
                        dve.wait_ge(silu_done[h], i * 2 + j + 1)
                        dve.wait_ge(a_ready[h], i * 2 + j)
                        nc.vector.tensor_tensor(prod[:, h, :], up_ps[:, h, :], silu[:, h, :],
                                                ALU.mult).then_inc(prod_done[h], 1)
                        dve.wait_ge(a_hi_done[h], i * 2 + j + 1)
                        at = slice(h * HALF, (h + 1) * HALF)
                        nc.vector.tensor_tensor(a_lo[j][:, at], prod[:, h, :], a_hi[j][:, at].bitcast(F32),
                                                ALU.subtract).then_inc(a_ready[h], 1)
                        if j == 0 and h == 0:
                            for c in range(2):
                                dve.wait_ge(dn_hi, i * 2 + c + 1)
                                nc.vector.tensor_tensor(d_lo[c][:], raw_d[:, c, :], d_hi[c][:].bitcast(F32),
                                                        ALU.subtract).then_inc(dn_lo, 1)
                for m in range(16):
                    t, h = m // 2, m % 2
                    at = (slice(None), t, slice(h * HALF, (h + 1) * HALF))
                    dve.wait_ge(dn_mm[m % 4], i * 4 + m // 4 + 1)
                    nc.vector.tensor_tensor(y[at], down_ps[:, m % 4, :], y[at], ALU.add).then_inc(added[m % 4], 1)
                    if m in (1, 5) and not last:
                        split_lo(i + 1, m // 4)

            split_lo(0, 0)
            split_lo(0, 1)
            dve.wait_ge(y_zeroed, 1)
            with dve.Fori(0, PAIRS - 1) as i:
                body(i, False)
            body(PAIRS - 1, True)

        @block.tensor
        def _(pe):
            def hidden(i, j, h):
                pe.wait_ge(gu_lo, i * 4 + 2 * j + 2)
                pe.wait_ge(prod_done[h], i * 2 + j)
                at = slice(h * HALF, (h + 1) * HALF)
                for k in range(KD):
                    for ps, n in ((gate_ps, 0), (up_ps, 1)):
                        nc.tensor.matmul(ps[:, h, :], w_hi[j][n][:, k, :], hi[:, k, at], start=(k == 0), stop=False)
                        nc.tensor.matmul(ps[:, h, :], w_hi[j][n][:, k, :], lo[:, k, at], start=False, stop=False)
                        mm = nc.tensor.matmul(ps[:, h, :], w_lo[j][n][:, k, :], hi[:, k, at],
                                              start=False, stop=(k == KD - 1))
                mm.then_inc(gu_mm[h], 1)

            def down(i, m):
                t, h = m // 2, m % 2
                if m == 0:
                    pe.wait_ge(dn_lo, i * 2 + 2)
                if m % 8 == 0:
                    pe.wait_ge(a_ready[m // 8], i * 2 + 2)
                pe.wait_ge(added[m % 4], i * 4 + m // 4)
                rows, cols = slice(t * P, (t + 1) * P), slice(h * HALF, (h + 1) * HALF)
                for c in range(2):
                    nc.tensor.matmul(down_ps[:, m % 4, :], a_hi[c][:, rows], d_hi[c][:, cols], start=(c == 0), stop=False)
                    nc.tensor.matmul(down_ps[:, m % 4, :], a_hi[c][:, rows], d_lo[c][:, cols], start=False, stop=False)
                    mm = nc.tensor.matmul(down_ps[:, m % 4, :], a_lo[c][:, rows], d_hi[c][:, cols],
                                          start=False, stop=(c == 1))
                mm.then_inc(dn_mm[m % 4], 1)

            with pe.Fori(0, PAIRS) as i:
                for j in range(2):
                    for h in range(2):
                        hidden(i, j, h)
                for m in range(16):
                    down(i, m)


def residual(core, tag, x_in, y, gain, factor, consts, x_out):
    nc = core.nc
    eps = consts["eps"]
    with ExitStack() as ctx:
        x = sbuf(nc, ctx, f"{tag}_x", [P, 2, D])
        sq = sbuf(nc, ctx, f"{tag}_sq", [P, 2, D])
        g = sbuf(nc, ctx, f"{tag}_g", [P, D])
        ssum = sbuf(nc, ctx, f"{tag}_ssum", [P, TT])
        root = sbuf(nc, ctx, f"{tag}_root", [P, TT])
        rstd = sbuf(nc, ctx, f"{tag}_rstd", [P, TT])
        g_loaded = core.sem(f"{tag}_g_loaded")
        x_loaded = core.sems(f"{tag}_x_loaded", 2)
        squared = core.sem(f"{tag}_squared")
        rooted = core.sem(f"{tag}_rooted")
        inverted = core.sem(f"{tag}_inverted")
        scaled = core.sem(f"{tag}_scaled")
        summed = core.sems(f"{tag}_summed", 2)
        stored = core.sems(f"{tag}_stored", 2)
        block = ctx.enter_context(nc.Block())

        @block.sync
        def _(sp):
            sp.dma_start(g[:], gain.rearrange("(o n) -> o n", o=1).broadcast_to([P, D])).then_inc(g_loaded, 16)
            with sp.Fori(0, TT // 2) as i:
                for b in range(2):
                    sp.wait_ge(stored[b], i * 16)
                    sp.dma_start(x[:, b, :], x_in[bass.ds((i * 2 + b) * P, P), :]).then_inc(x_loaded[b], 16)

        @block.scalar
        def _(act):
            for t in range(TT):
                if t >= 2:
                    act.wait_ge(squared, t - 1)
                nc.scalar.activation(sq[:, t % 2, :], y[:, t, :], ACT.Square,
                                     accum_out=ssum[:, t:t + 1]).then_inc(squared, 1)
            act.wait_ge(squared, TT)
            nc.scalar.activation(root[:], ssum[:], ACT.Sqrt, bias=eps[:, 0:1], scale=1.0 / D).then_inc(rooted, 1)
            with act.Fori(0, TT // 2) as i:
                for b in range(2):
                    act.wait_ge(summed[b], i + 1)
                    act.dma_start(x_out[bass.ds((i * 2 + b) * P, P), :], x[:, b, :]).then_inc(stored[b], 16)
            for b in range(2):
                act.wait_ge(stored[b], TT // 2 * 16)

        @block.vector
        def _(dve):
            dve.wait_ge(rooted, 1)
            dve.wait_ge(g_loaded, 16)
            nc.vector.reciprocal(rstd[:], root[:]).then_inc(inverted, 1)
            dve.wait_ge(inverted, 1)
            if factor != 1.0:
                nc.vector.tensor_scalar(rstd[:], rstd[:], factor, None, ALU.mult).then_inc(inverted, 1)
                dve.wait_ge(inverted, 2)
            for t in range(TT):
                b = t % 2
                nc.vector.scalar_tensor_tensor(out=y[:, t, :], in0=y[:, t, :], scalar=rstd[:, t:t + 1], in1=g[:],
                                               op0=ALU.mult, op1=ALU.mult).then_inc(scaled, 1)
                dve.wait_ge(scaled, t + 1)
                dve.wait_ge(x_loaded[b], 16 * (t // 2 + 1))
                nc.vector.tensor_tensor(x[:, b, :], x[:, b, :], y[:, t, :], ALU.add).then_inc(summed[b], 1)


def make_consts(core, ctx, ident_dram):
    nc = core.nc
    ident = sbuf(nc, ctx, "ident", [P, P])
    eps = sbuf(nc, ctx, "eps", [P, 2])
    loaded, set_ = core.sem("ident_loaded"), core.sem("eps_set")
    with nc.Block() as block:
        @block.sync
        def _(sp):
            sp.dma_start(ident[:], ident_dram).then_inc(loaded, 16)
            sp.wait_ge(loaded, 16)

        @block.vector
        def _(dve):
            nc.vector.memset(eps[:, 0:1], NORM_EPS).then_inc(set_, 1)
            nc.vector.memset(eps[:, 1:2], GROUP_EPS).then_inc(set_, 1)
            dve.wait_ge(set_, 2)
    return {"ident": ident, "eps": eps}


def feature_product(core, tag, w, col0, chunks, hi, lo, n, dst, row0, mix=None):
    nc = core.nc
    half = min(n, HALF)
    halves = n // half
    with ExitStack() as ctx:
        raw = sbuf(nc, ctx, f"{tag}_raw", [P, KD, 2 * P])
        w_hi = [sbuf(nc, ctx, f"{tag}_w{j}h", [P, KD, P], F32R) for j in range(2)]
        w_lo = [sbuf(nc, ctx, f"{tag}_w{j}l", [P, KD, P], F32R) for j in range(2)]
        z = [sbuf(nc, ctx, f"{tag}_z{j}", [P, n + 1]) for j in range(2)]
        if mix is not None:
            res = [sbuf(nc, ctx, f"{tag}_res{j}", [P, n]) for j in range(2)]
            dif = [sbuf(nc, ctx, f"{tag}_dif{j}", [P, n]) for j in range(2)]
            mu = sbuf(nc, ctx, f"{tag}_mu", [P, chunks])
        ps = psum(nc, ctx, f"{tag}_ps", [P, 2, 2, HALF])
        loaded = core.sem(f"{tag}_loaded")
        mu_loaded = core.sem(f"{tag}_mu_loaded")
        w_hi_done = core.sem(f"{tag}_w_hi_done")
        w_lo_done = core.sem(f"{tag}_w_lo_done")
        multiplied = core.sems(f"{tag}_multiplied", 2)
        copied = core.sems(f"{tag}_copied", 2)
        differed = core.sems(f"{tag}_differed", 2)
        mixed = core.sems(f"{tag}_mixed", 2)
        stored = core.sems(f"{tag}_stored", 2)
        zeroed = core.sem(f"{tag}_zeroed")
        block = ctx.enter_context(nc.Block())
        w_dram = w.rearrange("(k p) n -> p k n", p=P)
        pairs = chunks // 2
        done = mixed if mix is not None else copied
        out = res if mix is not None else [t[:, 1:n + 1] for t in z]

        @block.sync
        def _(sp):
            def load(i):
                sp.dma_start(raw[:], w_dram[:, :, bass.ds(i * (2 * P) + col0, 2 * P)]).then_inc(loaded, 16)

            def store(i):
                for j in range(2):
                    sp.wait_ge(done[j], i + 1)
                    sp.dma_start(dst[bass.ds(i * (2 * P) + (row0 + j * P), P), :], out[j][:] if mix is not None else out[j]
                                 ).then_inc(stored[j], 16)

            if mix is not None:
                with nc.allow_non_contiguous_dma("blend per feature"):
                    sp.dma_start(mu[:], mix.rearrange("(c p) -> p c", p=P)).then_inc(mu_loaded, 16)
            load(0)
            with sp.Fori(0, pairs - 1) as i:
                sp.wait_ge(w_lo_done, i * 2 + 2)
                load(i + 1)
                store(i)
            store(pairs - 1)
            for j in range(2):
                sp.wait_ge(stored[j], 16 * pairs)

        @block.scalar
        def _(act):
            def split_hi(j):
                nc.scalar.copy(w_hi[j][:], raw[:, :, j * P:(j + 1) * P]).then_inc(w_hi_done, 1)

            def body(i, last):
                for j in range(2):
                    act.wait_ge(multiplied[j], i + 1)
                    if mix is not None:
                        act.wait_ge(mixed[j], i)
                    else:
                        act.wait_ge(stored[j], i * 16)
                    nc.scalar.copy(z[j][:, 1:n + 1], ps[:, j, 0:halves, 0:half]).then_inc(copied[j], 1)
                    if not last:
                        if j == 0:
                            act.wait_ge(loaded, i * 16 + 32)
                        split_hi(j)

            act.wait_ge(loaded, 16)
            split_hi(0)
            split_hi(1)
            with act.Fori(0, pairs - 1) as i:
                body(i, False)
            body(pairs - 1, True)

        @block.vector
        def _(dve):
            def split_lo(i, j):
                dve.wait_ge(w_hi_done, i * 2 + j + 1)
                nc.vector.tensor_tensor(w_lo[j][:], raw[:, :, j * P:(j + 1) * P], w_hi[j][:].bitcast(F32),
                                        ALU.subtract).then_inc(w_lo_done, 1)

            def body(i, last):
                for j in range(2):
                    if mix is not None:
                        dve.wait_ge(copied[j], i + 1)
                        nc.vector.tensor_tensor(dif[j][:], z[j][:, 0:n], z[j][:, 1:n + 1],
                                                ALU.subtract).then_inc(differed[j], 1)
                        dve.wait_ge(differed[j], i + 1)
                        dve.wait_ge(stored[j], i * 16)
                        nc.vector.scalar_tensor_tensor(
                            out=res[j][:], in0=dif[j][:], scalar=mu[:, bass.ds(i * 2 + j, 1)], in1=z[j][:, 1:n + 1],
                            op0=ALU.mult, op1=ALU.add).then_inc(mixed[j], 1)
                    if not last:
                        split_lo(i + 1, j)

            if mix is not None:
                for j in range(2):
                    nc.vector.memset(z[j][:, 0:1], 0.0).then_inc(zeroed, 1)
                dve.wait_ge(zeroed, 2)
                dve.wait_ge(mu_loaded, 16)
            split_lo(0, 0)
            split_lo(0, 1)
            if pairs > 1:
                with dve.Fori(0, pairs - 1) as i:
                    body(i, False)
            body(pairs - 1, True)

        @block.tensor
        def _(pe):
            with pe.Fori(0, pairs) as i:
                for j in range(2):
                    pe.wait_ge(w_lo_done, i * 2 + j + 1)
                    pe.wait_ge(copied[j], i)
                    for h in range(halves):
                        at = slice(h * half, (h + 1) * half)
                        for k in range(KD):
                            o = ps[:, j, h, 0:half]
                            nc.tensor.matmul(o, w_hi[j][:, k, :], hi[:, k, at], start=(k == 0), stop=False)
                            nc.tensor.matmul(o, w_hi[j][:, k, :], lo[:, k, at], start=False, stop=False)
                            mm = nc.tensor.matmul(o, w_lo[j][:, k, :], hi[:, k, at], start=False, stop=(k == KD - 1))
                    mm.then_inc(multiplied[j], 1)


def gate_product(core, tag, w, col0, cols, hi, lo, gates):
    nc = core.nc
    with ExitStack() as ctx:
        raw = sbuf(nc, ctx, f"{tag}_raw", [P, KD, cols])
        w_hi = sbuf(nc, ctx, f"{tag}_wh", [P, KD, cols], F32R)
        w_lo = sbuf(nc, ctx, f"{tag}_wl", [P, KD, cols], F32R)
        ps = psum(nc, ctx, f"{tag}_ps", [P, TT, cols])
        loaded, hi_done, lo_done, multiplied, done = (core.sem(f"{tag}_{n}") for n in
                                                      ("loaded", "hi_done", "lo_done", "multiplied", "done"))
        block = ctx.enter_context(nc.Block())

        @block.sync
        def _(sp):
            sp.dma_start(raw[:], w.rearrange("(k p) n -> p k n", p=P)[:, :, col0:col0 + cols]).then_inc(loaded, 16)

        @block.scalar
        def _(act):
            act.wait_ge(loaded, 16)
            nc.scalar.copy(w_hi[:], raw[:]).then_inc(hi_done, 1)
            act.wait_ge(multiplied, 1)
            nc.scalar.activation(gates[:], ps[:], ACT.Sigmoid).then_inc(done, 1)

        @block.vector
        def _(dve):
            dve.wait_ge(hi_done, 1)
            nc.vector.tensor_tensor(w_lo[:], raw[:], w_hi[:].bitcast(F32), ALU.subtract).then_inc(lo_done, 1)

        @block.tensor
        def _(pe):
            pe.wait_ge(lo_done, 1)
            for t in range(TT):
                rows = slice(t * P, (t + 1) * P)
                for k in range(KD):
                    nc.tensor.matmul(ps[:, t, :], hi[:, k, rows], w_hi[:, k, :], start=(k == 0), stop=False)
                    nc.tensor.matmul(ps[:, t, :], lo[:, k, rows], w_hi[:, k, :], start=False, stop=False)
                    mm = nc.tensor.matmul(ps[:, t, :], hi[:, k, rows], w_lo[:, k, :], start=False, stop=(k == KD - 1))
            mm.then_inc(multiplied, 1)


def rotate_and_turn(core, tag, projT, cos_dram, sin_dram, rotated, rot_hi, rot_lo, turned_rows, turned_dst, consts):
    nc = core.nc
    ident = consts["ident"]
    NR, NV = len(rotated), len(turned_rows)
    with ExitStack() as ctx:
        cos = sbuf(nc, ctx, f"{tag}_cos", [P, T])
        sin = sbuf(nc, ctx, f"{tag}_sin", [P, T])
        x = sbuf(nc, ctx, f"{tag}_x", [P, 2, T])
        xs = sbuf(nc, ctx, f"{tag}_xs", [P, 2, T])
        r_hi = sbuf(nc, ctx, f"{tag}_r_hi", [P, 2, T], F32R)
        r_lo = sbuf(nc, ctx, f"{tag}_r_lo", [P, 2, T], F32R)
        v = sbuf(nc, ctx, f"{tag}_v", [P, 2, T])
        vt = sbuf(nc, ctx, f"{tag}_vt", [P, 2, TT, P])
        ps = psum(nc, ctx, f"{tag}_ps", [P, 2, TT, P])
        tables = core.sem(f"{tag}_tables")
        x_loaded = core.sems(f"{tag}_x_loaded", 2)
        v_loaded = core.pool_dma_sems(f"{tag}_v_loaded", 2)
        by_cos = core.sem(f"{tag}_by_cos")
        by_sin = core.sem(f"{tag}_by_sin")
        rotated_done = core.sem(f"{tag}_rotated")
        r_hi_done = core.sem(f"{tag}_r_hi_done")
        r_lo_done = core.sem(f"{tag}_r_lo_done")
        x_stored = core.sems(f"{tag}_x_stored", 2)
        v_stored = core.pool_dma_sems(f"{tag}_v_stored", 2)
        flipped = core.sem(f"{tag}_flipped")
        copied = core.sem(f"{tag}_copied")
        block = ctx.enter_context(nc.Block())

        @block.sync
        def _(sp):
            def store(n):
                sp.wait_ge(r_lo_done, n + 1)
                sp.dma_start(rot_hi[n * P:n * P + P, :], r_hi[:, n % 2, :].bitcast(F32)).then_inc(x_stored[n % 2], 16)
                sp.dma_start(rot_lo[n * P:n * P + P, :], r_lo[:, n % 2, :].bitcast(F32)).then_inc(x_stored[n % 2], 16)

            sp.dma_start(cos[:], cos_dram).then_inc(tables, 16)
            sp.dma_start(sin[:], sin_dram).then_inc(tables, 16)
            for n, row in enumerate(rotated):
                b = n % 2
                if n >= 2:
                    sp.wait_ge(r_lo_done, n - 1)
                sp.dma_start(x[:, b, :], projT[row:row + P, :]).then_inc(x_loaded[b], 16)
                for q in range(4):
                    sp.dma_start(xs[q * 32:q * 32 + 32, b, :],
                                 projT[row + (q ^ 1) * 32:row + (q ^ 1) * 32 + 32, :]).then_inc(x_loaded[b], 16)
                if n >= 1:
                    store(n - 1)
            store(NR - 1)
            for b in range(2):
                sp.wait_ge(x_stored[b], 32 * (NR // 2))

        @block.vector
        def _(dve):
            dve.wait_ge(tables, 32)
            for n in range(NR):
                b = n % 2
                dve.wait_ge(x_loaded[b], 80 * (n // 2 + 1))
                nc.vector.tensor_tensor(x[:, b, :], x[:, b, :], cos[:], ALU.mult).then_inc(by_cos, 1)
                nc.vector.tensor_tensor(xs[:, b, :], xs[:, b, :], sin[:], ALU.mult).then_inc(by_sin, 1)
                dve.wait_ge(by_cos, n + 1)
                dve.wait_ge(by_sin, n + 1)
                nc.vector.tensor_tensor(x[:, b, :], x[:, b, :], xs[:, b, :], ALU.add).then_inc(rotated_done, 1)
                dve.wait_ge(r_hi_done, n + 1)
                nc.vector.tensor_tensor(r_lo[:, b, :], x[:, b, :], r_hi[:, b, :].bitcast(F32),
                                        ALU.subtract).then_inc(r_lo_done, 1)

        @block.gpsimd
        def _(pool):
            for n in range(NV):
                if n >= 2:
                    pool.wait_ge(flipped, n - 1)
                source, row = turned_rows[n]
                pool.dma_start(v[:, n % 2, :], source[row:row + P, :]).then_inc(v_loaded[n % 2], 16)
                if n >= 1:
                    pool.wait_ge(copied, n)
                    pool.dma_start(turned_dst[n - 1].rearrange("(t p) c -> p t c", p=P), vt[:, (n - 1) % 2]
                                   ).then_inc(v_stored[(n - 1) % 2], 16)
            pool.wait_ge(copied, NV)
            pool.dma_start(turned_dst[NV - 1].rearrange("(t p) c -> p t c", p=P), vt[:, (NV - 1) % 2]
                           ).then_inc(v_stored[(NV - 1) % 2], 16)
            for b in range(2):
                pool.wait_ge(v_stored[b], 16 * ((NV + 1 - b) // 2))

        @block.tensor
        def _(pe):
            for n in range(NV):
                pe.wait_ge(v_loaded[n % 2], 16 * (n // 2 + 1))
                if n >= 2:
                    pe.wait_ge(copied, n - 1)
                for t in range(TT):
                    last = nc.tensor.transpose(ps[:, n % 2, t, :], v[:, n % 2, t * P:(t + 1) * P], ident[:])
                last.then_inc(flipped, 1)

        @block.scalar
        def _(act):
            for n in range(max(NV, NR)):
                if n < NR:
                    act.wait_ge(rotated_done, n + 1)
                    if n >= 2:
                        act.wait_ge(x_stored[n % 2], 32 * (n // 2))
                    nc.scalar.copy(r_hi[:, n % 2, :], x[:, n % 2, :]).then_inc(r_hi_done, 1)
                if n < NV:
                    act.wait_ge(flipped, n + 1)
                    if n >= 2:
                        act.wait_ge(v_stored[n % 2], 16 * (n // 2))
                    nc.scalar.copy(vt[:, n % 2], ps[:, n % 2]).then_inc(copied, 1)


def compress(core, tag, projT, k_row, v_row, k_par, v_par, cmp_cos, cmp_sin, kc_hi_out, kc_lo_out, vc_out):
    nc = core.nc
    BL, ST, DH, G = 32, 16, 64, 2
    NB = (T - BL) // ST + 1
    NC = G * NB
    HID = 256
    with ExitStack() as ctx:
        kv = sbuf(nc, ctx, f"{tag}_kv", [DH, 2, G, T])
        pe_t = sbuf(nc, ctx, f"{tag}_pe", [DH, 2, BL])
        w1 = sbuf(nc, ctx, f"{tag}_w1", [DH, 2, BL, HID])
        w2 = sbuf(nc, ctx, f"{tag}_w2", [P, 2, 2, DH])
        w2s = sbuf(nc, ctx, f"{tag}_w2s", [P, 2, DH])
        blocks = sbuf(nc, ctx, f"{tag}_blocks", [DH, 2, BL, NC])
        hid = sbuf(nc, ctx, f"{tag}_hid", [P, 2, 2, NC])
        tab = sbuf(nc, ctx, f"{tag}_tab", [DH, 2, NC])
        kc = sbuf(nc, ctx, f"{tag}_kc", [DH, 2, NC])
        kc_hi = sbuf(nc, ctx, f"{tag}_kc_hi", [DH, NC], F32R)
        kc_lo = sbuf(nc, ctx, f"{tag}_kc_lo", [DH, NC], F32R)
        vc = sbuf(nc, ctx, f"{tag}_vc", [NB, G, DH])
        hid_ps = psum(nc, ctx, f"{tag}_hid_ps", [P, 2, 2, 256])
        kc_ps = psum(nc, ctx, f"{tag}_kc_ps", [DH, 2, NC])
        vc_ps = psum(nc, ctx, f"{tag}_vc_ps", [NB, G, DH])
        small = core.sem(f"{tag}_small")
        kv_loaded = core.sems(f"{tag}_kv_loaded", 2)
        w1_loaded = core.sems(f"{tag}_w1_loaded", 2)
        gathered = core.sem(f"{tag}_gathered")
        hid_mm = core.sem(f"{tag}_hid_mm")
        hid_done = core.sem(f"{tag}_hid_done")
        out_mm = core.sem(f"{tag}_out_mm")
        kc_step = core.sem(f"{tag}_kc_step")
        vc_done = core.sem(f"{tag}_vc_done")
        stored = core.sem(f"{tag}_stored")
        block = ctx.enter_context(nc.Block())

        @block.sync
        def _(sp):
            for s, (row, par) in enumerate(((k_row, k_par), (v_row, v_par))):
                for g in range(G):
                    sp.dma_start(kv[:, s, g, :], projT[row + g * DH:row + (g + 1) * DH, :]).then_inc(kv_loaded[s], 16)
                with nc.allow_non_contiguous_dma("position table per feature"):
                    sp.dma_start(pe_t[:, s, :], par[0].rearrange("j d -> d j")).then_inc(kv_loaded[s], 16)
                sp.dma_start(w1[:, s], par[1].rearrange("(j d) m -> d j m", d=DH)).then_inc(w1_loaded[s], 16)
                sp.dma_start(w2[:, s], par[2].rearrange("(m p) d -> p m d", p=P)).then_inc(small, 16)
            with nc.allow_non_contiguous_dma("swapped halves"):
                for q in range(2):
                    sp.dma_start(w2s[:, :, q * 32:q * 32 + 32],
                                 k_par[2].rearrange("(m p) d -> p m d", p=P)[:, :, (1 - q) * 32:(1 - q) * 32 + 32]
                                 ).then_inc(small, 16)
            sp.dma_start(tab[:, 0], cmp_cos).then_inc(small, 16)
            sp.dma_start(tab[:, 1], cmp_sin).then_inc(small, 16)
            sp.wait_ge(kc_step, 4)
            sp.dma_start(kc_hi_out, kc_hi[:].bitcast(F32)).then_inc(stored, 16)
            sp.dma_start(kc_lo_out, kc_lo[:].bitcast(F32)).then_inc(stored, 16)
            sp.wait_ge(vc_done, 1)
            sp.dma_start(vc_out.rearrange("n (g d) -> n g d", g=G), vc[:]).then_inc(stored, 16)
            sp.wait_ge(stored, 48)

        @block.vector
        def _(dve):
            for s in range(2):
                dve.wait_ge(kv_loaded[s], 48)
                for jj in range(2):
                    for g in range(G):
                        src = kv[:, s, g, :].rearrange("p (b j) -> p j b", j=ST)[:, :, jj:jj + NB]
                        pos = pe_t[:, s, jj * ST:(jj + 1) * ST].unsqueeze(2).broadcast_to([DH, ST, NB])
                        nc.vector.tensor_tensor(blocks[:, s, jj * ST:(jj + 1) * ST, g * NB:(g + 1) * NB], src, pos,
                                                ALU.add).then_inc(gathered, 1)
            dve.wait_ge(out_mm, 1)
            dve.wait_ge(small, 96)
            nc.vector.tensor_tensor(kc[:], kc_ps[:], tab[:], ALU.mult).then_inc(kc_step, 1)
            dve.wait_ge(kc_step, 1)
            nc.vector.tensor_tensor(kc[:, 0, :], kc[:, 0, :], kc[:, 1, :], ALU.add).then_inc(kc_step, 1)
            dve.wait_ge(kc_step, 2)
            nc.vector.tensor_copy(kc_hi[:], kc[:, 0, :]).then_inc(kc_step, 1)
            dve.wait_ge(kc_step, 3)
            nc.vector.tensor_tensor(kc_lo[:], kc[:, 0, :], kc_hi[:].bitcast(F32), ALU.subtract).then_inc(kc_step, 1)
            dve.wait_ge(out_mm, 2)
            nc.vector.tensor_copy(vc[:], vc_ps[:]).then_inc(vc_done, 1)

        @block.tensor
        def _(pe):
            for s in range(2):
                pe.wait_ge(w1_loaded[s], 16)
                pe.wait_ge(gathered, 4 * s + 4)
                for m in range(2):
                    for j in range(BL):
                        mm = nc.tensor.matmul(hid_ps[:, s, m, 0:NC], w1[:, s, j, m * P:(m + 1) * P],
                                              blocks[:, s, j, :], start=(j == 0), stop=(j == BL - 1))
                mm.then_inc(hid_mm, 1)
            pe.wait_ge(small, 96)
            pe.wait_ge(hid_done, 1)
            for q, w in enumerate((w2[:, 0], w2s[:])):
                for m in range(2):
                    mm = nc.tensor.matmul(kc_ps[:, q, :], w[:, m, :], hid[:, 0, m, :], start=(m == 0), stop=(m == 1))
            mm.then_inc(out_mm, 1)
            pe.wait_ge(hid_done, 2)
            for g in range(G):
                for m in range(2):
                    mm = nc.tensor.matmul(vc_ps[:, g, :], hid[:, 1, m, g * NB:(g + 1) * NB], w2[:, 1, m, :],
                                          start=(m == 0), stop=(m == 1))
            mm.then_inc(out_mm, 1)

        @block.scalar
        def _(act):
            for s in range(2):
                act.wait_ge(hid_mm, s + 1)
                nc.scalar.activation(hid[:, s], hid_ps[:, s, :, 0:NC], ACT.Silu).then_inc(hid_done, 1)


def load_masks(core, ctx, a):
    nc = core.nc
    shapes = {"ident_bf": [P, P], "tri": [P, P], "edge": [P, P], "cmp": [P, TT, 63], "row_ok": [P, 1]}
    wide = {n: sbuf(nc, ctx, f"wide_{n}", s) for n, s in shapes.items()}
    narrow = {n: sbuf(nc, ctx, f"narrow_{n}", shapes[n], BF16) for n in ("ident_bf", "tri", "edge")}
    loaded, narrowed = core.sem("masks_loaded"), core.sem("masks_narrowed")
    with nc.Block() as block:
        @block.sync
        def _(sp):
            for name, tile in wide.items():
                sp.dma_start(tile[:], a[f"mask_{name}"]).then_inc(loaded, 16)
            sp.wait_ge(loaded, 16 * len(wide))

        @block.vector
        def _(dve):
            dve.wait_ge(loaded, 16 * len(wide))
            for name, tile in narrow.items():
                nc.vector.tensor_copy(tile[:], wide[name][:]).then_inc(narrowed, 1)
            dve.wait_ge(narrowed, len(narrow))
    return {**wide, **narrow}


def shape_tables():
    half, NB = 32, 63
    inv = np.power(np.float32(10000.0), -np.arange(half, dtype=np.float32) / np.float32(half)).astype(np.float32)

    def angles(pos):
        ang = (pos.astype(np.float32)[None, :] * inv[:, None]).astype(np.float32)
        return np.cos(ang).astype(np.float32), np.sin(ang).astype(np.float32)

    c, s = angles(np.arange(T))
    cc, cs = angles(np.arange(NB) * 16 + 31)
    t = np.arange(P)
    neg = np.float32(-1e30)
    tok = np.arange(T).reshape(TT, P)
    cmp_ok = (np.arange(NB) * 16 + 31)[None, None, :] <= tok.T[:, :, None]
    return {
        "ident_": np.eye(P, dtype=np.float32),
        "cos_t": np.tile(c, (4, 1)),
        "sin_t": np.concatenate([-s, s, -s, s]),
        "ccos": np.tile(cc, (2, 2)),
        "csin": np.tile(np.concatenate([-cs, cs]), (1, 2)),
        "mask_ident_bf": np.eye(P, dtype=np.float32),
        "mask_tri": np.where(t[None, :] > t[:, None], neg, 0).astype(np.float32),
        "mask_edge": np.where(t[None, :] <= t[:, None], neg, 0).astype(np.float32),
        "mask_cmp": np.where(cmp_ok, np.float32(0), neg).astype(np.float32),
        "mask_row_ok": (t >= 31).astype(np.float32)[:, None],
        **recurrence_tables(),
    }


CH = 64
NCH = T // CH
PAIRS = 4
RW = PAIRS * P


def rwkv_prepare(core, tag, z, par, consts, a, ops_dram, end_decay, bonus, g_tok):
    nc = core.nc
    w0_d, w2_d, a0_d, a2_d, g2_d, kk_d, ka_d, rk_d = par
    with ExitStack() as ctx:
        lora = sbuf(nc, ctx, f"{tag}_lora", [P, T])
        wlo = sbuf(nc, ctx, f"{tag}_wlo", [64, T])
        glo = sbuf(nc, ctx, f"{tag}_glo", [P, T])
        w2 = sbuf(nc, ctx, f"{tag}_w2", [P, RW])
        g2 = sbuf(nc, ctx, f"{tag}_g2", [P, RW])
        w0 = sbuf(nc, ctx, f"{tag}_w0", [1, RW])
        ones = sbuf(nc, ctx, f"{tag}_ones", [1, P])
        tri = sbuf(nc, ctx, f"{tag}_tri", [P, 2 * P])
        pairsum = sbuf(nc, ctx, f"{tag}_pairsum", [P, P])
        vecs = sbuf(nc, ctx, f"{tag}_vecs", [P, 4, PAIRS])
        one_ka = sbuf(nc, ctx, f"{tag}_one_ka", [P, PAIRS])
        rk_sel = sbuf(nc, ctx, f"{tag}_rk_sel", [P, PAIRS, 2])
        sel = sbuf(nc, ctx, f"{tag}_sel", [P, 2])
        sg = sbuf(nc, ctx, f"{tag}_sg", [P, TT, RW])
        r = sbuf(nc, ctx, f"{tag}_r", [P, T])
        k = sbuf(nc, ctx, f"{tag}_k", [P, T])
        dec = sbuf(nc, ctx, f"{tag}_dec", [P, 3, T])
        rate = sbuf(nc, ctx, f"{tag}_rate", [P, T])
        t1 = sbuf(nc, ctx, f"{tag}_t1", [P, T])
        sq = sbuf(nc, ctx, f"{tag}_sq", [P, T])
        nrm = sbuf(nc, ctx, f"{tag}_nrm", [P, T])
        u = sbuf(nc, ctx, f"{tag}_u", [P, T])
        kn = sbuf(nc, ctx, f"{tag}_kn", [P, T])
        ka = sbuf(nc, ctx, f"{tag}_ka", [P, T])
        rk = sbuf(nc, ctx, f"{tag}_rk", [P, T])
        res = sbuf(nc, ctx, f"{tag}_res", [P, 4, T])
        cum_ps = psum(nc, ctx, f"{tag}_cum_ps", [P, TT, 2, P])
        wide_ps = psum(nc, ctx, f"{tag}_wide_ps", [P, 3, HALF])
        bonus_ps = psum(nc, ctx, f"{tag}_bonus_ps", [P, TT, 2])
        small = core.sem(f"{tag}_small")
        lora_in = core.sem(f"{tag}_lora_in")
        ones_set = core.sem(f"{tag}_ones_set")
        squashed = core.sem(f"{tag}_squashed")
        vec_step = core.sem(f"{tag}_vec_step")
        z_mm = core.sem(f"{tag}_z_mm")
        z_sig = core.sem(f"{tag}_z_sig")
        g_mm = core.sem(f"{tag}_g_mm")
        g_copied = core.sem(f"{tag}_g_copied")
        rk_in = core.sem(f"{tag}_rk_in")
        squared = core.sem(f"{tag}_squared")
        cum_mm = core.sem(f"{tag}_cum_mm")
        cum_exp = core.sem(f"{tag}_cum_exp")
        rate_mm = core.sem(f"{tag}_rate_mm")
        rate_done = core.sem(f"{tag}_rate_done")
        norm_mm = core.sem(f"{tag}_norm_mm")
        norm_root = core.sem(f"{tag}_norm_root")
        vec = core.sem(f"{tag}_vec")
        done = core.sem(f"{tag}_done")
        bonus_mm = core.sem(f"{tag}_bonus_mm")
        bonus_done = core.sem(f"{tag}_bonus_done")
        stored = core.sem(f"{tag}_stored")
        block = ctx.enter_context(nc.Block())
        SMALL = 16 * 12
        VEC = 9

        @block.sync
        def _(sp):
            sp.dma_start(lora[:], z[3 * RW:3 * RW + P, :]).then_inc(lora_in, 16)
            sp.dma_start(glo[:], z[3 * RW + P:3 * RW + 2 * P, :]).then_inc(lora_in, 16)
            sp.dma_start(w2[0:64, :], w2_d).then_inc(small, 16)
            sp.dma_start(w2[64:P, :], a2_d).then_inc(small, 16)
            sp.dma_start(g2[:], g2_d).then_inc(small, 16)
            sp.dma_start(w0[:], w0_d.rearrange("(o n) -> o n", o=1)).then_inc(small, 16)
            sp.dma_start(tri[:], a["tri_decay"]).then_inc(small, 16)
            sp.dma_start(pairsum[:], a["pairsum"]).then_inc(small, 16)
            sp.dma_start(sel[:], a["head_sel"]).then_inc(small, 16)
            with nc.allow_non_contiguous_dma("vectors per channel"):
                for n, v in enumerate((a0_d, kk_d, ka_d, rk_d)):
                    sp.dma_start(vecs[:, n, :], v.rearrange("(c p) -> p c", p=P)).then_inc(small, 16)
            sp.dma_start(ones[:], a["ones_row"]).then_inc(small, 16)
            with sp.Fori(0, PAIRS) as p:
                sp.wait_ge(done, p * 4)
                sp.dma_start(r[:], z[bass.ds(p * P, P), :]).then_inc(rk_in, 16)
                sp.dma_start(k[:], z[bass.ds(p * P + RW, P), :]).then_inc(rk_in, 16)
                for n in range(4):
                    sp.wait_ge(done, p * 4 + n + 1)
                    sp.dma_start(ops_dram[n, bass.ds(p * P, P), :], res[:, n, :]).then_inc(stored, 16)
            sp.wait_ge(stored, 64 * PAIRS)

        @block.tensor
        def _(pe):
            pe.wait_ge(small, SMALL)
            pe.wait_ge(squashed, 2)
            for t in range(TT):
                rows = slice(t * P, (t + 1) * P)
                if t >= 2:
                    pe.wait_ge(z_sig, t - 1)
                nc.tensor.matmul(wide_ps[:, t % 2, :], wlo[:, rows], w2[0:64, :], start=True, stop=False)
                nc.tensor.matmul(wide_ps[:, t % 2, :], ones[:], w0[:], start=False, stop=True).then_inc(z_mm, 1)
            for t in range(TT):
                rows = slice(t * P, (t + 1) * P)
                if t < 2:
                    pe.wait_ge(z_sig, TT - 1 + t)
                else:
                    pe.wait_ge(g_copied, t - 1)
                nc.tensor.matmul(wide_ps[:, t % 2, :], glo[:, rows], g2[:], start=True, stop=True).then_inc(g_mm, 1)
            pe.wait_ge(g_copied, TT)
            for p in range(PAIRS):
                chan = slice(p * P, (p + 1) * P)
                if p >= 1:
                    pe.wait_ge(cum_exp, 3 * p)
                for t in range(TT):
                    mm = nc.tensor.matmul(cum_ps[:, t].rearrange("p a b -> p (a b)"), sg[:, t, chan], tri[:],
                                          start=True, stop=True)
                mm.then_inc(cum_mm, 1)
                for h in range(2):
                    at = slice(h * HALF, (h + 1) * HALF)
                    if p >= 1 or h >= 1:
                        pe.wait_ge(rate_done, 2 * p + h)
                    nc.tensor.matmul(wide_ps[:, 0, :], w2[64:P, chan], lora[64:P, at],
                                     start=True, stop=True).then_inc(rate_mm, 1)
                pe.wait_ge(squared, p + 1)
                for h in range(2):
                    at = slice(h * HALF, (h + 1) * HALF)
                    if p >= 1:
                        pe.wait_ge(norm_root, 2 * p - 1 + h)
                    nc.tensor.matmul(wide_ps[:, 1 + h, :], pairsum[:], sq[:, at], start=True, stop=True).then_inc(norm_mm, 1)
                pe.wait_ge(vec, VEC * p + 7)
                if p >= 1:
                    pe.wait_ge(bonus_done, p)
                else:
                    pe.wait_ge(vec_step, 2)
                for t in range(TT):
                    mm = nc.tensor.matmul(bonus_ps[:, t, :], rk[:, t * P:(t + 1) * P], rk_sel[:, p, :],
                                          start=True, stop=True)
                mm.then_inc(bonus_mm, 1)

        @block.scalar
        def _(act):
            act.wait_ge(lora_in, 32)
            nc.scalar.activation(wlo[:], lora[0:64, :], ACT.Tanh).then_inc(squashed, 1)
            nc.scalar.activation(glo[:], glo[:], ACT.Sigmoid).then_inc(squashed, 1)
            for t in range(TT):
                act.wait_ge(z_mm, t + 1)
                nc.scalar.activation(sg[:, t, :], wide_ps[:, t % 2, :], ACT.Sigmoid).then_inc(z_sig, 1)
            for t in range(TT):
                act.wait_ge(g_mm, t + 1)
                nc.scalar.copy(g_tok[:, t, :], wide_ps[:, t % 2, :]).then_inc(g_copied, 1)
            act.wait_ge(small, SMALL)
            for p in range(PAIRS):
                for h in range(2):
                    if p >= 1 and h == 0:
                        act.wait_ge(vec, VEC * (p - 1) + 8)
                    act.wait_ge(rate_mm, 2 * p + h + 1)
                    nc.scalar.activation(rate[:, h * HALF:(h + 1) * HALF], wide_ps[:, 0, :], ACT.Sigmoid,
                                         bias=vecs[:, 0, p:p + 1]).then_inc(rate_done, 1)
                act.wait_ge(rk_in, 32 * (p + 1))
                if p >= 1:
                    act.wait_ge(norm_mm, 2 * p)
                nc.scalar.activation(sq[:], k[:], ACT.Square, scale=vecs[:, 1, p:p + 1]).then_inc(squared, 1)
                if p >= 1:
                    act.wait_ge(done, 4 * p)
                    act.wait_ge(vec, VEC * p)
                act.wait_ge(cum_mm, p + 1)
                for n, (plane, sign) in enumerate(((0, 1.0), (0, -1.0), (1, 1.0))):
                    nc.scalar.activation(dec[:, n, :].rearrange("p (t c) -> p t c", c=P), cum_ps[:, :, plane, :],
                                         ACT.Exp, scale=sign).then_inc(cum_exp, 1)
                for h in range(2):
                    act.wait_ge(norm_mm, 2 * p + h + 1)
                    if p >= 1 and h == 0:
                        act.wait_ge(vec, VEC * (p - 1) + 6)
                    nc.scalar.activation(nrm[:, h * HALF:(h + 1) * HALF], wide_ps[:, 1 + h, :],
                                         ACT.Sqrt).then_inc(norm_root, 1)

        @block.vector
        def _(dve):
            dve.wait_ge(small, SMALL)
            nc.vector.tensor_scalar(one_ka[:], vecs[:, 2, :], -1.0, 1.0, ALU.mult, ALU.add).then_inc(vec_step, 1)
            nc.vector.tensor_tensor(rk_sel[:], vecs[:, 3, :].unsqueeze(2).broadcast_to([P, PAIRS, 2]),
                                    sel[:].unsqueeze(1).broadcast_to([P, PAIRS, 2]), ALU.mult).then_inc(vec_step, 1)
            dve.wait_ge(vec_step, 2)
            for p in range(PAIRS):
                v0 = VEC * p
                dve.wait_ge(rk_in, 32 * (p + 1))
                if p >= 1:
                    dve.wait_ge(bonus_mm, p)
                nc.vector.tensor_scalar(t1[:], k[:], vecs[:, 1, p:p + 1], None, ALU.mult).then_inc(vec, 1)
                dve.wait_ge(rate_done, 2 * p + 2)
                nc.vector.tensor_scalar(u[:], rate[:], vecs[:, 2, p:p + 1], one_ka[:, p:p + 1],
                                        ALU.mult, ALU.add).then_inc(vec, 1)
                dve.wait_ge(norm_root, 2 * p + 2)
                nc.vector.tensor_scalar(nrm[:], nrm[:], 1e-12, None, ALU.max).then_inc(vec, 1)
                dve.wait_ge(vec, v0 + 3)
                nc.vector.reciprocal(nrm[:], nrm[:]).then_inc(vec, 1)
                dve.wait_ge(vec, v0 + 4)
                nc.vector.tensor_tensor(kn[:], k[:], u[:], ALU.mult).then_inc(vec, 1)
                nc.vector.tensor_tensor(t1[:], t1[:], nrm[:], ALU.mult).then_inc(vec, 1)
                dve.wait_ge(vec, v0 + 6)
                nc.vector.tensor_tensor(rk[:], r[:], kn[:], ALU.mult).then_inc(vec, 1)
                nc.vector.tensor_tensor(ka[:], t1[:], rate[:], ALU.mult).then_inc(vec, 1)
                dve.wait_ge(cum_exp, 3 * p + 3)
                if p >= 1:
                    dve.wait_ge(stored, 64 * p)
                nc.vector.scalar_tensor_tensor(out=res[:, 0, :], in0=t1[:], scalar=-1.0, in1=dec[:, 2, :],
                                               op0=ALU.mult, op1=ALU.mult).then_inc(done, 1)
                dve.wait_ge(vec, v0 + 8)
                nc.vector.tensor_tensor(res[:, 1, :], ka[:], dec[:, 1, :], ALU.mult).then_inc(done, 1)
                nc.vector.tensor_tensor(res[:, 2, :], kn[:], dec[:, 1, :], ALU.mult).then_inc(done, 1)
                nc.vector.tensor_tensor(res[:, 3, :], r[:], dec[:, 0, :], ALU.mult).then_inc(done, 1)
                nc.vector.tensor_copy(end_decay[:, p, :], dec[:, 0, :].rearrange("p (c t) -> p c t", t=CH)[:, :, CH - 1]
                                      ).then_inc(vec, 1)
                dve.wait_ge(bonus_mm, p + 1)
                nc.vector.tensor_copy(bonus[:, :, 2 * p:2 * p + 2], bonus_ps[:]).then_inc(bonus_done, 1)


DH = 64
NB = 63
STEPS = 2 * TT
CMP_COL = 5 * P
LEVELS = 5


def branches(s):
    i = s // 2 % TT
    if s % 2 == 0:
        return [(1, 0, i + 1, 0)]
    first = max(0, i - 4)
    return [(2, first, i + 1 - first, 0), (0, 0, 1, CMP_COL)]


def turns(s):
    out = []
    for br, first, n, col in branches(s):
        out += [(br, first + m, col + m * P, m == 0, m == n - 1) for m in range(n)]
    return [out[m:m + 4] for m in range(0, len(out), 4)]


PRODUCTS = ["gram_b", "gram_k", "gram_l", "turn_a", "turn_b", "turn_k", "x",
            *[f"{w}{lv}" for lv in range(LEVELS) for w in ("y", "t", "tt")],
            "check", "fix1", "fix2", "wu", "gr", "s", "out"]
WEIGHT = {"gram_b": 4096, "gram_k": 4096, "gram_l": 2048, "turn_a": 512, "turn_b": 512, "turn_k": 512, "x": 1024,
          "check": 2048, "fix1": 2048, "fix2": 2048, "wu": 3072, "gr": 4096, "s": 3072, "out": 3072}


def joint_plan():
    attention, fill, pending = [("score", 0)], 0, None
    for s in range(2 * STEPS):
        if s + 1 < 2 * STEPS:
            attention.append(("score", s + 1))
        for f, bank in enumerate(turns(s)):
            attention.append(("bank", s, f, fill))
            if pending:
                attention.append(pending)
                if pending[4]:
                    attention.append(("finish", pending[1] // 2))
            pending = ("values", s, f, fill, s % 2 == 1 and f == len(turns(s)) - 1)
            fill += 1
    attention += [pending, ("finish", 2 * TT - 1)]
    recurrence = []
    for c in (0, 2):
        recurrence += [("rw", c + j, name) for name in PRODUCTS[:-2] for j in range(2)]
        recurrence += [("rw", c + j, name) for j in range(2) for name in PRODUCTS[-2:]]

    def weight(e):
        if e[0] == "score":
            return sum(n * P for _, _, n, _ in branches(e[1])) * 2 + 128
        if e[0] == "rw":
            return WEIGHT.get(e[2], 512)
        return {"bank": 512, "values": 1024, "finish": 0}[e[0]]

    total = [sum(map(weight, x)) for x in (attention, recurrence)]
    plan, done, at = [], [0, 0], [0, 0]
    while at[0] < len(attention) or at[1] < len(recurrence):
        share = [done[n] / total[n] if at[n] < len((attention, recurrence)[n]) else 2 for n in range(2)]
        n = 0 if share[0] < share[1] else 1
        e = (attention, recurrence)[n][at[n]]
        plan.append(e)
        done[n] += weight(e)
        at[n] += 1
    return plan, fill


def attend_and_recur(core, tag, rot_hi, rot_lo, kc_hi_dram, kc_lo_dram, v_tok, vc_dram, gates, masks, o_dram,
                     ops_dram, rv_dram, end_decay, consts, a, y_dram):
    nc = core.nc
    ident = consts["ident"]
    SCALE = DH ** -0.5
    ident_bf, tri_bf, edge_bf, cmp_mask, row_ok = (masks[n] for n in ("ident_bf", "tri", "edge", "cmp", "row_ok"))
    plan, FILLS = joint_plan()
    assert FILLS % 2 == 0
    TURNS = 4
    with ExitStack() as ctx:
        qh = sbuf(nc, ctx, f"{tag}_qh", [P, 2, T], F32R)
        ql = sbuf(nc, ctx, f"{tag}_ql", [DH, 2, T], F32R)
        ks = sbuf(nc, ctx, f"{tag}_ks", [P, T], F32R)
        kw = sbuf(nc, ctx, f"{tag}_kw", [P, T], F32R)
        kc = sbuf(nc, ctx, f"{tag}_kc", [P, NB + 1], F32R)
        vs = sbuf(nc, ctx, f"{tag}_vs", [P, TT, DH])
        vw = sbuf(nc, ctx, f"{tag}_vw", [P, TT, DH])
        vc = sbuf(nc, ctx, f"{tag}_vc", [NB, DH])
        prob = sbuf(nc, ctx, f"{tag}_prob", [P, 2, T])
        cscore = sbuf(nc, ctx, f"{tag}_cscore", [P, NB])
        cprob = sbuf(nc, ctx, f"{tag}_cprob", [P, P])
        top = sbuf(nc, ctx, f"{tag}_top", [P, 2, 2])
        bias = sbuf(nc, ctx, f"{tag}_bias", [P, 2, 2])
        den = sbuf(nc, ctx, f"{tag}_den", [P, 2, 3])
        rden = sbuf(nc, ctx, f"{tag}_rden", [P, 3])
        coef = sbuf(nc, ctx, f"{tag}_coef", [P, 3])
        probT = sbuf(nc, ctx, f"{tag}_probT", [P, 2, 4, P])
        o_sum = sbuf(nc, ctx, f"{tag}_o_sum", [P, 3 * DH])
        o_part = sbuf(nc, ctx, f"{tag}_o_part", [P, 2, DH])
        o = sbuf(nc, ctx, f"{tag}_o", [P, 2, TT, DH])
        s_ps = psum(nc, ctx, f"{tag}_s_ps", [P, T])
        t_ps = psum(nc, ctx, f"{tag}_t_ps", [P, 4, P])
        o_ps = psum(nc, ctx, f"{tag}_o_ps", [P, HALF])
        def two(name, width, dt=F32):
            return [sbuf(nc, ctx, f"{tag}_{name}{j}", [P, PAIRS, width], dt) for j in range(2)]

        AR, B, K, V = two("AR", 2 * P), two("B", P), two("K", P), two("V", CH)
        LT, L, LkT, RkT = two("LT", P), two("L", P), two("LkT", P), two("RkT", P)
        BR = two("BR", 2 * P)
        Ktok = two("Kt", P)
        AX = two("AX", P + CH)
        LTm = [sbuf(nc, ctx, f"{tag}_LTm{j}", [P, LEVELS, PAIRS, P], F32R) for j in range(2)]
        T0, TT0, Y1 = two("T0", P, F32R), two("TT0", P, F32R), two("Y1", P, F32R)
        near = two("near", P)
        E, TTf = two("E", P), two("TTf", P)
        WU, GR, M, yo = two("WU", P + CH), two("GR", 2 * P), two("M", CH), two("yo", CH)
        m_gram = sbuf(nc, ctx, f"{tag}_m_gram", [P, 2, P])
        m_low = sbuf(nc, ctx, f"{tag}_m_low", [P, P])
        m_one = sbuf(nc, ctx, f"{tag}_m_one", [P, 2, P])
        m_lev = sbuf(nc, ctx, f"{tag}_m_lev", [P, LEVELS, P])
        ps = [psum(nc, ctx, f"{tag}_ps{j}", [P, 2, HALF]) for j in range(2)]

        q_in = core.sems(f"{tag}_q_in", 2)
        kv_in = core.sem(f"{tag}_kv_in")
        padded = core.sem(f"{tag}_padded")
        scored = core.sem(f"{tag}_scored")
        maxed = core.sem(f"{tag}_maxed")
        biased = core.sem(f"{tag}_biased")
        exped = core.sem(f"{tag}_exped")
        flipped = core.sem(f"{tag}_flipped")
        copied = core.sems(f"{tag}_copied", 2)
        summed = core.sem(f"{tag}_summed")
        o_read = core.sem(f"{tag}_o_read")
        inverted = core.sem(f"{tag}_inverted")
        finished = core.sem(f"{tag}_finished")
        o_done = core.sem(f"{tag}_o_done")
        o_stored = core.pool_dma_sems(f"{tag}_o_stored", 2)
        masks_in = core.sem(f"{tag}_masks_in")
        zeroed = core.sem(f"{tag}_zeroed")
        ops_in = core.sems(f"{tag}_ops_in", 2)
        products = core.sems(f"{tag}_products", 2)
        by_dve = core.sems(f"{tag}_by_dve", 2)
        by_act = core.sems(f"{tag}_by_act", 2)
        by_pool = core.sems(f"{tag}_by_pool", 2)
        state = core.sem(f"{tag}_state")
        y_stored = core.pool_dma_sems(f"{tag}_y_stored", 2)
        block = ctx.enter_context(nc.Block())

        def numbered(names):
            return {name: k + 1 for k, name in enumerate(names)}

        pn = numbered(PRODUCTS)
        dn = numbered(["lt", "rbt", "lkt", "rkt", "l", *[f"{w}{lv}" for lv in range(LEVELS) for w in ("t", "tt")],
                       "e", "u", "ttf", "g", "rw"])
        an = numbered(["a_tok", "b_tok", "k_tok", "x", *[f"y{lv}" for lv in range(LEVELS)], "wu", "out"])
        gn = numbered(["one", "t_start", "one_t", "tt_start", *[f"lev{lv}" for lv in range(LEVELS)], "i_t0"])

        def through(numbers, n, c, name):
            return n * (2 * len(numbers)) + (c // 2) * len(numbers) + (numbers[name] if name else 0)

        EXPS = 3 * STEPS

        def exps_through(n, s):
            return n * EXPS + s // 2 * 3 + (3 if s % 2 else 1)

        def over_pairs(tile):
            return tile.unsqueeze(1).broadcast_to([P, PAIRS, P])

        def bank(j, k, width=P):
            return ps[j][:, k, 0:PAIRS * width].rearrange("p (q c) -> p q c", c=width)

        def plane(j, part):
            return ps[j][:].rearrange("p b (q w c) -> p (b q) w c", q=2, w=2)[:, :, part, :]

        @block.sync
        def _(sp):
            def load_q(n, b):
                row = n * P + b * DH
                for half in range(2):
                    sp.dma_start(qh[half * DH:(half + 1) * DH, b, :].bitcast(F32), rot_hi[bass.ds(row, DH), :]).then_inc(q_in[b], 16)
                sp.dma_start(ql[:, b, :].bitcast(F32), rot_lo[bass.ds(row, DH), :]).then_inc(q_in[b], 16)

            def load_kv(g):
                for h, (rot, kcd) in enumerate(((rot_hi, kc_hi_dram), (rot_lo, kc_lo_dram))):
                    rows = slice(h * DH, (h + 1) * DH)
                    sp.dma_start(ks[rows, :].bitcast(F32), rot[bass.ds(g * DH + 4 * P, DH), :]).then_inc(kv_in, 16)
                    sp.dma_start(kw[rows, :].bitcast(F32), rot[bass.ds(g * DH + 5 * P, DH), :]).then_inc(kv_in, 16)
                    sp.dma_start(kc[rows, 0:NB].bitcast(F32), kcd[:, bass.ds(g * NB, NB)]).then_inc(kv_in, 16)
                for dst, src in ((vs, v_tok[0]), (vw, v_tok[1])):
                    sp.dma_start(dst[:], src.rearrange("(t p) c -> p t c", p=P)[:, :, bass.ds(g * DH, DH)]).then_inc(kv_in, 16)
                sp.dma_start(vc[:], vc_dram[:, bass.ds(g * DH, DH)]).then_inc(kv_in, 16)

            def load_op(j, first, which, dst):
                for h in range(2):
                    rows = slice(h * CH, (h + 1) * CH)
                    src = ops_dram[which].rearrange("(q p) t -> p q t", p=P)[rows, :, bass.ds(first, CH)]
                    sp.dma_start(dst[rows, :, h * CH:(h + 1) * CH], src).then_inc(ops_in[j], 16)

            def load_v(j, first):
                for h in range(2):
                    src = rv_dram[bass.ds(first, CH), :].rearrange("t (q p) -> t q p", p=P)
                    sp.dma_start(V[j][h * CH:(h + 1) * CH], src[:, :, h * CH:(h + 1) * CH]).then_inc(ops_in[j], 16)

            for dst, name in ((m_gram, "m_gram"), (m_low, "m_low"), (m_one, "m_one"), (m_lev, "m_lev")):
                sp.dma_start(dst[:], a[name]).then_inc(masks_in, 16)
            sp.wait_ge(zeroed, 8)
            for j in range(2):
                for which, dst in enumerate((AR[j][:, :, 0:P], B[j][:], K[j][:], AR[j][:, :, P:2 * P])):
                    load_op(j, j * CH, which, dst)
                load_v(j, j * CH)
            load_q(0, 0)
            load_kv(0)
            load_q(0, 1)

            def body(n, last):
                for e in plan:
                    if e[0] == "rw" and e[2] in ("turn_k", "s", "out"):
                        c, j = e[1], e[1] % 2
                        if last and c >= 2:
                            continue
                        first = n * (4 * CH) + (c + 2) * CH
                        if not last:
                            first = sp.snap(first)
                        sp.wait_ge(products[j], through(pn, n, c, e[2]))
                        if e[2] == "turn_k":
                            for which, dst in enumerate((AR[j][:, :, 0:P], B[j][:], K[j][:])):
                                load_op(j, first, which, dst)
                        elif e[2] == "s":
                            load_op(j, first, 3, AR[j][:, :, P:2 * P])
                        else:
                            load_v(j, first)
                    if e == ("finish", TT - 1) and not last:
                        sp.wait_ge(summed, n * (2 * TT) + TT)
                        load_q(n + 1, 0)
                if not last:
                    sp.wait_ge(summed, n * (2 * TT) + 2 * TT)
                    load_kv(nc.s_assert_within(
                        (n + 1) >> 1, 0, 1, skip_runtime_bounds_check_because="n is at most 2"))
                    load_q(n + 1, 1)

            with sp.Fori(0, TURNS - 1) as n:
                body(n, False)
            body(TURNS - 1, True)

        @block.gpsimd
        def _(pool):
            for j in range(2):
                for tile in (AR[j], B[j], K[j], M[j]):
                    nc.gpsimd.memset(tile[:], 0.0).then_inc(zeroed, 1)
            nc.gpsimd.memset(cprob[:], 0.0).then_inc(padded, 1)
            nc.gpsimd.memset(kc[:, NB:NB + 1].bitcast(F32), 0.0).then_inc(padded, 1)
            pool.wait_ge(masks_in, 64)

            def op(j, out, in0, in1, how):
                nc.gpsimd.tensor_tensor(out, in0, in1, how).then_inc(by_pool[j], 1)

            with pool.Fori(0, TURNS) as n:
                for e in plan:
                    if e[0] == "finish" and e[1] % TT == TT - 1:
                        b = e[1] // TT
                        pool.wait_ge(o_done, n * (2 * TT) + (b + 1) * TT)
                        pool.dma_start(o_dram.rearrange("(t p) c -> p t c", p=P)[:, :, bass.ds(n * P + b * DH, DH)],
                                       o[:, b]).then_inc(o_stored[b], 16)
                    if e[0] != "rw":
                        continue
                    c, j, name = e[1], e[1] % 2, e[2]
                    if name == "gram_l":
                        for sq, tri, part, start in (("one", L, 0, T0), ("one_t", LT, 1, TT0)):
                            pool.wait_ge(by_dve[j], through(dn, n, c, "l"))
                            if sq == "one_t":
                                pool.wait_ge(by_pool[j], through(gn, n, c, "t_start"))
                            op(j, near[j][:], tri[j][:], over_pairs(m_one[:, part]), ALU.mult)
                            pool.wait_ge(by_pool[j], through(gn, n, c, sq))
                            op(j, start[j][:], near[j][:], over_pairs(ident[:]), ALU.add)
                        for lv in range(LEVELS):
                            op(j, LTm[j][:, lv], LT[j][:], over_pairs(m_lev[:, lv, :]), ALU.mult)
                    elif name == f"tt{LEVELS - 1}":
                        pool.wait_ge(by_dve[j], through(dn, n, c, f"t{LEVELS - 1}"))
                        op(j, near[j][:], over_pairs(ident[:]), T0[j][:].bitcast(F32), ALU.subtract)
                    elif name == "out":
                        pool.wait_ge(by_act[j], through(an, n, c, "out"))
                        for h in range(2):
                            dst = y_dram[bass.ds(n * (4 * CH) + c * CH, CH), :].rearrange("t (q p) -> t q p", p=P)
                            pool.dma_start(dst[:, :, h * CH:(h + 1) * CH], yo[j][h * CH:(h + 1) * CH]).then_inc(y_stored[j], 16)
            for j in range(2):
                pool.wait_ge(o_stored[j], 16 * TURNS)
                pool.wait_ge(y_stored[j], 32 * 2 * TURNS)

        @block.tensor
        def _(pe):
            def score(n, s):
                b, i = s // STEPS, s // 2 % TT
                if s % STEPS == 0:
                    pe.wait_ge(q_in[b], n * 48 + 48)
                if s == 0:
                    pe.wait_ge(kv_in, n * 144 + 144)
                    pe.wait_ge(exped, n * EXPS)
                else:
                    pe.wait_ge(exped, exps_through(n, s - 1))
                rows = slice(i * P, (i + 1) * P)
                for br, first, cnt, col in branches(s):
                    key = (kc, ks, kw)[br]
                    for m in range(0, cnt, 4):
                        w = min(4, cnt - m)
                        tri = br > 0 and m + w == cnt
                        edge = br == 2 and i >= 4 and m == 0
                        width = w * P if br else NB + 1
                        at = s_ps[:, col + m * P:col + m * P + width]
                        keys = slice((first + m) * P, (first + m) * P + width)
                        nc.tensor.matmul(at, qh[:, b, rows], key[:, keys], start=True, stop=False)
                        mm = nc.tensor.matmul(at, ql[:, b, rows], key[0:DH, keys], start=False, stop=not (tri or edge))
                        if edge:
                            mm = nc.tensor.matmul(at[:, 0:P], ident_bf[:], edge_bf[:], start=False, stop=not tri)
                        if tri:
                            mm = nc.tensor.matmul(at[:, (w - 1) * P:w * P], ident_bf[:], tri_bf[:],
                                                  start=False, stop=True)
                mm.then_inc(scored, 1)

            def turn_probs(n, s, f, fill):
                if f == 0:
                    pe.wait_ge(exped, exps_through(n, s))
                pe.wait_ge(copied[(fill - 1) % 2], n * (FILLS // 2) + (fill + 1) // 2 if fill else n * (FILLS // 2))
                for m, (br, blk, col, first, last) in enumerate(turns(s)[f]):
                    src = cprob[:] if br == 0 else prob[:, s % 2, col:col + P]
                    mm = nc.tensor.transpose(t_ps[:, m, :], src, ident[:])
                mm.then_inc(flipped, 1)

            def values(n, s, f, fill, ends):
                b, tile = s // STEPS, s // 2
                pe.wait_ge(copied[fill % 2], n * (FILLS // 2) + fill // 2 + 1)
                if s % 2 == 0 and f == 0:
                    pe.wait_ge(o_read, n * (2 * TT) + tile)
                for m, (br, blk, col, first, last) in enumerate(turns(s)[f]):
                    val = (vc[:], vs[:, blk, :], vw[:, blk, :])[br]
                    keys = NB if br == 0 else P
                    mm = nc.tensor.matmul(o_ps[:, br * DH:(br + 1) * DH], probT[0:keys, fill % 2, m, :], val,
                                          start=first, stop=last)
                if ends:
                    mm.then_inc(summed, 1)

            def recur(n, c, name):
                j = c % 2

                def dve(what):
                    pe.wait_ge(by_dve[j], through(dn, n, c, what))

                def act(what):
                    pe.wait_ge(by_act[j], through(an, n, c, what))

                def pool(what):
                    pe.wait_ge(by_pool[j], through(gn, n, c, what))

                def group(k, width, lhsT, rhs):
                    per_bank = HALF // width
                    for p in range(PAIRS):
                        at = ps[j][:, k + p // per_bank, (p % per_bank) * width:(p % per_bank + 1) * width]
                        mm = nc.tensor.matmul(at, lhsT[:, p], rhs[:, p], start=True, stop=True)
                    mm.then_inc(products[j], 1)

                def turn(k, src):
                    for p in range(PAIRS):
                        mm = nc.tensor.transpose(ps[j][:, k, p * P:(p + 1) * P], src[:, p], ident[:])
                    mm.then_inc(products[j], 1)

                if name == "gram_b":
                    pe.wait_ge(ops_in[j], n * 320 + (c // 2) * 160 + 160)
                    act(None)
                    pe.wait_ge(state, n * 4 + c - j)
                    group(0, 2 * P, B[j], AR[j])
                elif name == "gram_k":
                    dve("rbt")
                    group(0, 2 * P, K[j], AR[j])
                elif name == "gram_l":
                    dve("rkt")
                    group(0, P, AR[j][:, :, 0:P], B[j])
                elif name == "turn_a":
                    turn(1, AR[j][:, :, 0:P])
                elif name == "turn_b":
                    dve("l")
                    turn(0, B[j])
                elif name == "turn_k":
                    act("a_tok")
                    turn(1, K[j])
                elif name == "x":
                    act("b_tok")
                    group(0, CH, LkT[j], V[j])
                elif name[0] == "y":
                    lv = int(name[1:])
                    pool(f"lev{lv}")
                    if lv == 0:
                        act("x")
                    else:
                        dve(f"tt{lv - 1}")
                    group(0, P, LTm[j][:, lv], T0[j])
                elif name[:2] == "tt":
                    group(0, P, Y1[j], TT0[j])
                elif name[0] == "t":
                    lv = int(name[1:])
                    act(f"y{lv}")
                    group(1, P, TT0[j], Y1[j])
                elif name == "check":
                    dve(f"tt{LEVELS - 1}")
                    group(1, P, LT[j], T0[j][:].bitcast(F32))
                elif name == "fix1":
                    dve("e")
                    group(0, P, E[j], TT0[j][:].bitcast(F32))
                elif name == "fix2":
                    dve("u")
                    group(1, P, E[j], near[j])
                elif name == "wu":
                    dve("ttf")
                    for p in range(PAIRS):
                        at = ps[j][:, p // 2, (p % 2) * (P + CH):(p % 2 + 1) * (P + CH)]
                        mm = nc.tensor.matmul(at, TTf[j][:, p], AX[j][:, p], start=True, stop=True)
                    mm.then_inc(products[j], 1)
                elif name == "gr":
                    act("wu")
                    group(0, 2 * P, WU[j][:, :, 0:P], BR[j])
                elif name == "s":
                    dve("rw")
                    for p in range(PAIRS):
                        at = ps[j][:, 0, p * CH:(p + 1) * CH]
                        nc.tensor.matmul(at, Ktok[j][:, p], V[j][:, p], start=True, stop=False)
                        nc.tensor.matmul(at, BR[j][:, p, 0:P], WU[j][:, p, P:P + CH], start=False, stop=False)
                        if p == 0:
                            pe.wait_ge(state, n * 4 + c)
                        mm = nc.tensor.matmul(at, GR[j][:, p, 0:P], M[j][:, p], start=False, stop=True)
                    mm.then_inc(products[j], 1)
                else:
                    for p in range(PAIRS):
                        at = ps[j][:, 1, p * CH:(p + 1) * CH]
                        nc.tensor.matmul(at, RkT[j][:, p], V[j][:, p], start=True, stop=False)
                        nc.tensor.matmul(at, BR[j][:, p, P:2 * P], WU[j][:, p, P:P + CH], start=False, stop=False)
                        mm = nc.tensor.matmul(at, GR[j][:, p, P:2 * P], M[j][:, p], start=False, stop=True)
                    mm.then_inc(products[j], 1)

            pe.wait_ge(padded, 2)
            with pe.Fori(0, TURNS) as n:
                for e in plan:
                    if e[0] == "score":
                        score(n, e[1])
                    elif e[0] == "bank":
                        turn_probs(n, *e[1:])
                    elif e[0] == "values":
                        values(n, *e[1:])
                    elif e[0] == "rw":
                        recur(n, *e[1:])

        def copy_probs(eng, copy, n, fill, blocks):
            eng.wait_ge(flipped, n * FILLS + fill + 1)
            copy(probT[:, fill % 2, 0:blocks, :], t_ps[:, 0:blocks, :]).then_inc(copied[fill % 2], 1)

        fills = [sum(len(turns(x)) for x in range(s)) for s in range(2 * STEPS + 1)]

        @block.scalar
        def _(act):
            def exps(n, s):
                tile, i = s // 2, s // 2 % TT
                cols = (i + 1) * P if s % 2 == 0 else min(i + 1, 5) * P
                act.wait_ge(biased, n * (2 * STEPS) + s + 1)
                act.wait_ge(flipped, n * FILLS + (fills[s - 1] if s >= 2 else 0))
                act.wait_ge(inverted, n * (2 * TT) + max(tile - 1, 0))
                nc.scalar.activation(prob[:, s % 2, 0:cols], s_ps[:, 0:cols], ACT.Exp, bias=bias[:, s % 2, 0:1],
                                     scale=SCALE, accum_out=den[:, tile % 2, 1 + s % 2:2 + s % 2]).then_inc(exped, 1)
                if s % 2 == 1:
                    nc.scalar.activation(cprob[:, 0:NB], cscore[:], ACT.Exp, bias=bias[:, 1, 1:2], scale=SCALE,
                                         accum_out=den[:, tile % 2, 0:1]).then_inc(exped, 1)

            def recur(n, c, name):
                j = c % 2

                def copy(dst, src):
                    act.wait_ge(products[j], through(pn, n, c, name))
                    nc.scalar.copy(dst, src).then_inc(by_act[j], 1)

                if name == "turn_a":
                    copy(AX[j][:, :, 0:P], bank(j, 1))
                elif name == "turn_b":
                    copy(BR[j][:, :, 0:P], bank(j, 0))
                elif name == "turn_k":
                    copy(Ktok[j][:], bank(j, 1))
                elif name == "x":
                    copy(AX[j][:, :, P:P + CH], bank(j, 0, CH))
                elif name[0] == "y":
                    copy(Y1[j][:], bank(j, 0))
                elif name == "wu":
                    copy(WU[j][:].rearrange("p (b q) c -> p b (q c)", b=2), ps[j][:, 0:2, 0:2 * (P + CH)])
                elif name == "out":
                    act.wait_ge(y_stored[j], n * 64 + (c // 2) * 32)
                    copy(yo[j][:], bank(j, 1, CH))

            act.wait_ge(padded, 2)
            with act.Fori(0, TURNS) as n:
                for e in plan:
                    if e[0] == "score":
                        exps(n, e[1])
                    elif e[0] == "bank" and e[3] % 2:
                        copy_probs(act, nc.scalar.copy, n, e[3], len(turns(e[1])[e[2]]))
                    elif e[0] == "rw":
                        recur(n, *e[1:])

        @block.vector
        def _(dve):
            MAXES = 4 * STEPS

            def bias_of(n, s):
                i = s // 2 % TT
                before = n * MAXES + s // 2 * 4 + s % 2
                cols = (i + 1) * P if s % 2 == 0 else min(i + 1, 5) * P
                dve.wait_ge(scored, n * (2 * STEPS) + s + 1)
                nc.vector.tensor_reduce(top[:, s % 2, 0:1], s_ps[:, 0:cols], AX_X, ALU.max).then_inc(maxed, 1)
                if s % 2 == 1:
                    nc.vector.tensor_tensor(cscore[:], s_ps[:, CMP_COL:CMP_COL + NB], cmp_mask[:, i, :],
                                            ALU.add).then_inc(maxed, 1)
                    dve.wait_ge(maxed, before + 2)
                    nc.vector.tensor_reduce(top[:, 1, 1:2], cscore[:], AX_X, ALU.max).then_inc(maxed, 1)
                dve.wait_ge(maxed, before + (3 if s % 2 else 1))
                nc.vector.tensor_scalar(bias[:, s % 2, 0:1 + s % 2], top[:, s % 2, 0:1 + s % 2], -SCALE, None,
                                        ALU.mult).then_inc(biased, 1)

            def finish(n, tile):
                b, i = tile // TT, tile % TT
                FIN = 2 * TT * 3 + 2
                before = n * FIN + tile * 3 + (tile > 0) + (tile > TT)
                dve.wait_ge(summed, n * (2 * TT) + tile + 1)
                if i == 0:
                    dve.wait_ge(o_stored[b], n * 16)
                nc.vector.tensor_copy(o_sum[:], o_ps[:, 0:3 * DH]).then_inc(o_read, 1)
                nc.vector.reciprocal(rden[:], den[:, tile % 2, :]).then_inc(inverted, 1)
                dve.wait_ge(inverted, n * (2 * TT) + tile + 1)
                nc.vector.tensor_tensor(coef[:], rden[:], gates[:, i, bass.ds(n * 6 + b * 3, 3)],
                                        ALU.mult).then_inc(finished, 1)
                k = 1
                dve.wait_ge(finished, before + k)
                if i == 0:
                    nc.vector.tensor_tensor(coef[:, 0:1], coef[:, 0:1], row_ok[:], ALU.mult).then_inc(finished, 1)
                    k += 1
                    dve.wait_ge(finished, before + k)
                dve.wait_ge(o_read, n * (2 * TT) + tile + 1)
                nc.vector.tensor_scalar(o_part[:, 0, :], o_sum[:, 0:DH], coef[:, 0:1], None, ALU.mult).then_inc(finished, 1)
                dve.wait_ge(finished, before + k + 1)
                nc.vector.scalar_tensor_tensor(out=o_part[:, 1, :], in0=o_sum[:, DH:2 * DH], scalar=coef[:, 1:2],
                                               in1=o_part[:, 0, :], op0=ALU.mult, op1=ALU.add).then_inc(finished, 1)
                dve.wait_ge(finished, before + k + 2)
                nc.vector.scalar_tensor_tensor(out=o[:, b, i, :], in0=o_sum[:, 2 * DH:3 * DH], scalar=coef[:, 2:3],
                                               in1=o_part[:, 1, :], op0=ALU.mult, op1=ALU.add).then_inc(o_done, 1)

            def recur(n, c, name):
                j = c % 2

                def op(out, in0, in1, how):
                    nc.vector.tensor_tensor(out, in0, in1, how).then_inc(by_dve[j], 1)

                if name in ("gram_b", "gram_k", "gram_l", "check", "fix1", "fix2", "gr", "s") or name[0] == "t" and name[1] != "u":
                    dve.wait_ge(products[j], through(pn, n, c, name))
                if name == "gram_b":
                    op(LT[j][:], plane(j, 0), over_pairs(m_gram[:, 0]), ALU.mult)
                    op(BR[j][:, :, P:2 * P], plane(j, 1), over_pairs(m_gram[:, 1]), ALU.mult)
                elif name == "gram_k":
                    op(LkT[j][:], plane(j, 0), over_pairs(m_gram[:, 0]), ALU.mult)
                    op(RkT[j][:], plane(j, 1), over_pairs(m_gram[:, 1]), ALU.mult)
                elif name == "gram_l":
                    op(L[j][:], bank(j, 0), over_pairs(m_low[:]), ALU.mult)
                elif name[:2] == "tt":
                    op(TT0[j][:], bank(j, 0), TT0[j][:].bitcast(F32), ALU.add)
                elif name[0] == "t" and name[1] != "u":
                    op(T0[j][:], bank(j, 1), T0[j][:].bitcast(F32), ALU.add)
                elif name == "check":
                    dve.wait_ge(by_pool[j], through(gn, n, c, "i_t0"))
                    op(E[j][:], bank(j, 1), near[j][:], ALU.add)
                elif name == "fix1":
                    op(near[j][:], bank(j, 0), TT0[j][:].bitcast(F32), ALU.add)
                elif name == "fix2":
                    op(TTf[j][:], bank(j, 1), TT0[j][:].bitcast(F32), ALU.add)
                elif name == "gr":
                    op(GR[j][:, :, 0:P], plane(j, 0), over_pairs(ident[:]), ALU.add)
                    op(GR[j][:, :, P:2 * P], plane(j, 1), AR[j][:, :, P:2 * P], ALU.add)
                elif name == "s":
                    dve.wait_ge(products[1 - j], through(pn, n, c - 1, "out") if j else through(pn, n, c, None))
                    nc.vector.tensor_tensor(M[1 - j][:], bank(j, 0, CH),
                                            end_decay[:, :, bass.ds(n * 4 + c, 1)].broadcast_to([P, PAIRS, CH]),
                                            ALU.mult).then_inc(state, 1)

            dve.wait_ge(masks_in, 64)
            dve.wait_ge(zeroed, 8)
            with dve.Fori(0, TURNS) as n:
                for e in plan:
                    if e[0] == "score":
                        bias_of(n, e[1])
                    elif e[0] == "bank" and e[3] % 2 == 0:
                        copy_probs(dve, nc.vector.tensor_copy, n, e[3], len(turns(e[1])[e[2]]))
                    elif e[0] == "finish":
                        finish(n, e[1])
                    elif e[0] == "rw":
                        recur(n, *e[1:])


def recurrence_tables():
    n = np.arange(P)
    same = n[:, None] // CH == n[None, :] // CH
    s, t = n[:, None] % CH, n[None, :] % CH
    f = np.float32
    decay = -np.exp(f(-0.5))

    def pair_of(m, s, t):
        return same & (s // (2 * m) == t // (2 * m)) & (s // m % 2 == 0) & (t // m % 2 == 1)

    return {
        "tri_decay": np.concatenate([(same & (s <= t)) * decay, (same & (s < t)) * decay], 1).astype(f),
        "pairsum": same.astype(f),
        "head_sel": (n[:, None] // CH == np.arange(2)[None, :]).astype(f),
        "ones_row": np.ones((1, P), f),
        "m_gram": np.stack([same & (s < t), same & (s <= t)], 1).astype(f),
        "m_low": (same & (s > t)).astype(f),
        "m_one": np.stack([pair_of(1, t, s), pair_of(1, s, t)], 1).astype(f),
        "m_lev": np.stack([pair_of(m, s, t) for m in (2, 4, 8, 16, 32)], 1).astype(f),
    }


def mix_transpose(core, tag, o_dram, y_dram, v_dram, bonus, g_tok, gains, consts, hi, lo):
    nc = core.nc
    ident, eps = consts["ident"], consts["eps"]
    H = RW // 64
    with ExitStack() as ctx:
        o = sbuf(nc, ctx, f"{tag}_o", [P, 2, RW])
        y = sbuf(nc, ctx, f"{tag}_y", [P, 2, RW])
        v = sbuf(nc, ctx, f"{tag}_v", [P, 2, RW])
        sq = sbuf(nc, ctx, f"{tag}_sq", [P, 2, RW])
        mixed = sbuf(nc, ctx, f"{tag}_mixed", [P, 2, D])
        rows = sbuf(nc, ctx, f"{tag}_rows", [P, 3, RW])
        ssum = sbuf(nc, ctx, f"{tag}_ssum", [P, 2])
        root = sbuf(nc, ctx, f"{tag}_root", [P, 2, 1 + H])
        rstd = sbuf(nc, ctx, f"{tag}_rstd", [P, 2, 1 + H])
        mean = sbuf(nc, ctx, f"{tag}_mean", [P, H])
        var = sbuf(nc, ctx, f"{tag}_var", [P, 2, H])
        tp = psum(nc, ctx, f"{tag}_tp", [P, 4, 4, P])
        rows_in = core.sem(f"{tag}_rows_in")
        o_in = core.sems(f"{tag}_o_in", 2)
        squared = core.sems(f"{tag}_squared", 2)
        o_root = core.sems(f"{tag}_o_root", 2)
        var_done = core.sems(f"{tag}_var_done", 2)
        y_root = core.sems(f"{tag}_y_root", 2)
        step = core.sems(f"{tag}_step", 2)
        v_scaled = core.sems(f"{tag}_v_scaled", 2)
        turned = core.sems(f"{tag}_turned", 2)
        hi_done = core.sems(f"{tag}_hi_done", 2)
        lo_done = core.sems(f"{tag}_lo_done", 2)
        block = ctx.enter_context(nc.Block())
        STEPS = 11

        def heads(tile):
            return tile.rearrange("p (h c) -> p h c", h=H)

        def per_head(tile):
            return tile.unsqueeze(2).broadcast_to([P, H, 64])

        @block.sync
        def _(sp):
            for n, g in enumerate(gains):
                sp.dma_start(rows[:, n, :], g.rearrange("(o n) -> o n", o=1).broadcast_to([P, RW])).then_inc(rows_in, 16)
            with sp.Fori(0, TT // 2) as i:
                for b in range(2):
                    first = sp.snap((i * 2 + b) * P)
                    sp.wait_ge(step[b], i * STEPS)
                    for dst, src in ((o, o_dram), (y, y_dram), (v, v_dram)):
                        sp.dma_start(dst[:, b, :], src[bass.ds(first, P), :]).then_inc(o_in[b], 16)

        @block.gpsimd
        def _(pool):
            with pool.Fori(0, TT // 2) as i:
                for b in range(2):
                    pool.wait_ge(o_in[b], i * 48 + 48)
                    nc.gpsimd.tensor_tensor(heads(v[:, b, :]), heads(v[:, b, :]),
                                            per_head(bonus[:, bass.ds(i * 2 + b, 1), :].rearrange("p o h -> p (o h)")),
                                            ALU.mult).then_inc(v_scaled[b], 1)

        @block.scalar
        def _(act):
            with act.Fori(0, TT // 2) as i:
                for b in range(2):
                    act.wait_ge(o_in[b], i * 48 + 48)
                    act.wait_ge(step[b], i * STEPS)
                    nc.scalar.activation(sq[:, b, :], o[:, b, :], ACT.Square, accum_out=ssum[:, b:b + 1]
                                         ).then_inc(squared[b], 1)
                    act.wait_ge(squared[b], i + 1)
                    nc.scalar.activation(root[:, b, 0:1], ssum[:, b:b + 1], ACT.Sqrt, bias=eps[:, 0:1],
                                         scale=1.0 / RW).then_inc(o_root[b], 1)
                    act.wait_ge(var_done[b], i + 1)
                    nc.scalar.activation(root[:, b, 1:1 + H], var[:, b, :], ACT.Sqrt, bias=eps[:, 1:2],
                                         scale=1.0 / 64).then_inc(y_root[b], 1)
                for b in range(2):
                    act.wait_ge(turned[b], i + 1)
                    for k in range(2):
                        nc.scalar.copy(hi[:, 4 * k:4 * k + 4, bass.ds((i * 2 + b) * P, P)], tp[:, 2 * b + k]
                                       ).then_inc(hi_done[b], 1)

        @block.vector
        def _(dve):
            dve.wait_ge(rows_in, 48)
            with dve.Fori(0, TT // 2) as i:
                for b in range(2):
                    base = i * STEPS
                    yh = heads(y[:, b, :])
                    dve.wait_ge(o_in[b], i * 48 + 48)
                    nc.vector.tensor_reduce(mean[:], yh, AX_X, ALU.add).then_inc(step[b], 1)
                    dve.wait_ge(step[b], base + 1)
                    nc.vector.tensor_scalar(mean[:], mean[:], 1.0 / 64, None, ALU.mult).then_inc(step[b], 1)
                    dve.wait_ge(step[b], base + 2)
                    nc.vector.tensor_tensor(yh, yh, per_head(mean[:]), ALU.subtract).then_inc(step[b], 1)
                    dve.wait_ge(step[b], base + 3)
                    dve.wait_ge(squared[b], i + 1)
                    nc.vector.tensor_tensor(sq[:, b, :], y[:, b, :], y[:, b, :], ALU.mult).then_inc(step[b], 1)
                    dve.wait_ge(step[b], base + 4)
                    nc.vector.tensor_reduce(var[:, b, :], heads(sq[:, b, :]), AX_X, ALU.add).then_inc(var_done[b], 1)
                    dve.wait_ge(o_root[b], i + 1)
                    dve.wait_ge(y_root[b], i + 1)
                    nc.vector.reciprocal(rstd[:, b, :], root[:, b, :]).then_inc(step[b], 1)
                    dve.wait_ge(step[b], base + 5)
                    dve.wait_ge(turned[b], i)
                    nc.vector.scalar_tensor_tensor(out=mixed[:, b, 0:RW], in0=o[:, b, :], scalar=rstd[:, b, 0:1],
                                                   in1=rows[:, 0, :], op0=ALU.mult, op1=ALU.mult).then_inc(step[b], 1)
                    nc.vector.tensor_tensor(yh, yh, per_head(rstd[:, b, 1:1 + H]), ALU.mult).then_inc(step[b], 1)
                    dve.wait_ge(step[b], base + 7)
                    nc.vector.tensor_tensor(y[:, b, :], y[:, b, :], rows[:, 1, :], ALU.mult).then_inc(step[b], 1)
                    dve.wait_ge(step[b], base + 8)
                    nc.vector.tensor_tensor(y[:, b, :], y[:, b, :], rows[:, 2, :], ALU.add).then_inc(step[b], 1)
                    dve.wait_ge(step[b], base + 9)
                    dve.wait_ge(v_scaled[b], i + 1)
                    nc.vector.tensor_tensor(y[:, b, :], y[:, b, :], v[:, b, :], ALU.add).then_inc(step[b], 1)
                    dve.wait_ge(step[b], base + 10)
                    nc.vector.tensor_tensor(mixed[:, b, RW:D], y[:, b, :],
                                            g_tok[:, bass.ds(i * 2 + b, 1), :].rearrange("p o c -> p (o c)"),
                                            ALU.mult).then_inc(step[b], 1)
                for b in range(2):
                    for k in range(2):
                        dve.wait_ge(hi_done[b], i * 2 + k + 1)
                        at = (slice(None), slice(4 * k, 4 * k + 4), bass.ds((i * 2 + b) * P, P))
                        nc.vector.tensor_tensor(lo[at], tp[:, 2 * b + k], hi[at].bitcast(F32),
                                                ALU.subtract).then_inc(lo_done[b], 1)

        @block.tensor
        def _(pe):
            with pe.Fori(0, TT // 2) as i:
                for b in range(2):
                    pe.wait_ge(step[b], i * STEPS + STEPS)
                    pe.wait_ge(lo_done[b], i * 2)
                    for k in range(KD):
                        last = nc.tensor.transpose(tp[:, 2 * b + k // 4, k % 4, :], mixed[:, b, k * P:(k + 1) * P], ident[:])
                    last.then_inc(turned[b], 1)


def token_product(core, tag, w, hi, lo, tiles, y):
    nc = core.nc
    STEP = 4
    with ExitStack() as ctx:
        raw = sbuf(nc, ctx, f"{tag}_raw", [P, 2, D])
        w_hi = sbuf(nc, ctx, f"{tag}_wh", [P, KD, D], F32R)
        w_lo = sbuf(nc, ctx, f"{tag}_wl", [P, KD, D], F32R)
        ps = psum(nc, ctx, f"{tag}_ps", [P, 8, HALF])
        loaded = core.sems(f"{tag}_loaded", 2)
        hi_done = core.sem(f"{tag}_hi_done")
        lo_done = core.sem(f"{tag}_lo_done")
        multiplied = core.sem(f"{tag}_multiplied")
        copied = core.sems(f"{tag}_copied", 2)
        block = ctx.enter_context(nc.Block())
        groups = [range(t, min(t + STEP, tiles)) for t in range(0, tiles, STEP)]

        @block.sync
        def _(sp):
            for k in range(KD):
                if k >= 2:
                    sp.wait_ge(lo_done, k - 1)
                sp.dma_start(raw[:, k % 2, :], w[k * P:(k + 1) * P, :]).then_inc(loaded[k % 2], 16)

        @block.scalar
        def _(act):
            for k in range(KD):
                act.wait_ge(loaded[k % 2], 16 * (k // 2 + 1))
                nc.scalar.copy(w_hi[:, k, :], raw[:, k % 2, :]).then_inc(hi_done, 1)
            done = 0
            for g in groups:
                for n in range(2 * len(g)):
                    if n % 2 == 0:
                        act.wait_ge(multiplied, done + n + 1)
                        nc.scalar.copy(y[:, g[0] + n // 2, 0:HALF], ps[:, n, :]).then_inc(copied[0], 1)
                done += 2 * len(g)

        @block.vector
        def _(dve):
            for k in range(KD):
                dve.wait_ge(hi_done, k + 1)
                nc.vector.tensor_tensor(w_lo[:, k, :], raw[:, k % 2, :], w_hi[:, k, :].bitcast(F32),
                                        ALU.subtract).then_inc(lo_done, 1)
            done = 0
            for g in groups:
                for n in range(2 * len(g)):
                    if n % 2 == 1:
                        dve.wait_ge(multiplied, done + n + 1)
                        nc.vector.tensor_copy(y[:, g[0] + n // 2, HALF:D], ps[:, n, :]).then_inc(copied[1], 1)
                done += 2 * len(g)

        @block.tensor
        def _(pe):
            done = 0
            for g in groups:
                for k in range(KD):
                    pe.wait_ge(lo_done, k + 1)
                    for n in range(2 * len(g)):
                        rows = slice((g[0] + n // 2) * P, (g[0] + n // 2 + 1) * P)
                        cols = slice(n % 2 * HALF, (n % 2 + 1) * HALF)
                        if k == 0 and done:
                            pe.wait_ge(copied[n % 2], done // 2 - len(g) + n // 2 + 1)
                        nc.tensor.matmul(ps[:, n, :], hi[:, k, rows], w_hi[:, k, cols], start=(k == 0), stop=False)
                        nc.tensor.matmul(ps[:, n, :], hi[:, k, rows], w_lo[:, k, cols], start=False, stop=False)
                        mm = nc.tensor.matmul(ps[:, n, :], lo[:, k, rows], w_hi[:, k, cols], start=False, stop=(k == KD - 1))
                        if k == KD - 1:
                            mm.then_inc(multiplied, 1)
                done += 2 * len(g)


def memory_attention(core, tag, qT_dram, kT_dram, v, consts, hi, lo):
    nc = core.nc
    ident = consts["ident"]
    MH, MD, MT = 4, 256, 256
    SCALE = MD ** -0.5
    with ExitStack() as ctx:
        q = sbuf(nc, ctx, f"{tag}_q", [P, 2, 2, T])
        kT = sbuf(nc, ctx, f"{tag}_k", [P, 2, 2, MT])
        vh = sbuf(nc, ctx, f"{tag}_v", [P, 2, 2, MD])
        prob = sbuf(nc, ctx, f"{tag}_prob", [P, 2, MT])
        top = sbuf(nc, ctx, f"{tag}_top", [P, 2])
        bias = sbuf(nc, ctx, f"{tag}_bias", [P, 2])
        den = sbuf(nc, ctx, f"{tag}_den", [P, 2])
        rden = sbuf(nc, ctx, f"{tag}_rden", [P, 2])
        probT = sbuf(nc, ctx, f"{tag}_probT", [P, 2, 2, HALF])
        s_ps = psum(nc, ctx, f"{tag}_s_ps", [P, 2, HALF])
        t_ps = psum(nc, ctx, f"{tag}_t_ps", [P, 2, HALF])
        o_ps = psum(nc, ctx, f"{tag}_o_ps", [P, 4, HALF])
        loaded = core.sems(f"{tag}_loaded", 2)
        v_copied = core.sems(f"{tag}_v_copied", 2)
        scored = core.sem(f"{tag}_scored")
        maxed = core.sem(f"{tag}_maxed")
        biased = core.sem(f"{tag}_biased")
        exped = core.sem(f"{tag}_exped")
        inverted = core.sem(f"{tag}_inverted")
        scaled = core.sem(f"{tag}_scaled")
        flipped = core.sem(f"{tag}_flipped")
        copied = core.sem(f"{tag}_copied")
        summed = core.sem(f"{tag}_summed")
        hi_done = core.sem(f"{tag}_hi_done")
        lo_done = core.sem(f"{tag}_lo_done")
        block = ctx.enter_context(nc.Block())
        TILES = 2 * TT

        @block.sync
        def _(sp):
            with sp.Fori(0, MH // 2) as n:
                for b in range(2):
                    row = sp.snap((n * 2 + b) * MD)
                    sp.wait_ge(summed, n * 8)
                    sp.dma_start(q[:, b], qT_dram[bass.ds(row, MD), :].rearrange("(c p) t -> p c t", p=P)).then_inc(loaded[b], 16)
                    sp.dma_start(kT[:, b], kT_dram[bass.ds(row, MD), :].rearrange("(c p) t -> p c t", p=P)).then_inc(loaded[b], 16)

        @block.gpsimd
        def _(pool):
            with pool.Fori(0, MH // 2) as n:
                for b in range(2):
                    pool.wait_ge(summed, n * 8)
                    nc.gpsimd.tensor_copy(vh[:, b], v[:, :, bass.ds((n * 2 + b) * MD, MD)]).then_inc(v_copied[b], 1)

        @block.tensor
        def _(pe):
            def score(n, s):
                b, i = s // TT, s % TT
                if i == 0:
                    pe.wait_ge(loaded[b], n * 32 + 32)
                pe.wait_ge(exped, n * TILES + max(s - 1, 0))
                for c in range(2):
                    mm = nc.tensor.matmul(s_ps[:, s % 2, 0:MT], q[:, b, c, i * P:(i + 1) * P], kT[:, b, c, :],
                                          start=(c == 0), stop=(c == 1))
                mm.then_inc(scored, 1)

            def turn(n, s):
                pe.wait_ge(scaled, n * TILES + s + 1)
                pe.wait_ge(copied, n * TILES + max(s - 1, 0))
                for c in range(2):
                    mm = nc.tensor.transpose(t_ps[:, s % 2, c * P:(c + 1) * P], prob[:, s % 2, c * P:(c + 1) * P], ident[:])
                mm.then_inc(flipped, 1)

            def values(n, s):
                b, half = s // TT, s % TT // 4
                pe.wait_ge(copied, n * TILES + s + 1)
                if s == 3:
                    pe.wait_ge(v_copied[0], n + 1)
                if s == TT + 3:
                    pe.wait_ge(v_copied[1], n + 1)
                for c in range(2):
                    m = s // 4 * 2 + c
                    pe.wait_ge(lo_done, n * 8 + max(m - 3, 0))
                    for kt in range(2):
                        mm = nc.tensor.matmul(o_ps[:, m % 4, :], vh[:, b, kt, c * P:(c + 1) * P], probT[:, half, kt, :],
                                              start=(kt == 0), stop=(kt == 1))
                    mm.then_inc(summed, 1)

            with pe.Fori(0, MH // 2) as n:
                score(n, 0)
                for s in range(TILES):
                    if s + 1 < TILES:
                        score(n, s + 1)
                    turn(n, s)
                    if s % 4 == 0 and s:
                        values(n, s - 1)
                values(n, TILES - 1)

        @block.scalar
        def _(act):
            def exps(n, s):
                act.wait_ge(biased, n * TILES + s + 1)
                act.wait_ge(flipped, n * TILES + max(s - 1, 0))
                nc.scalar.activation(prob[:, s % 2, :], s_ps[:, s % 2, 0:MT], ACT.Exp, bias=bias[:, s % 2:s % 2 + 1],
                                     scale=SCALE, accum_out=den[:, s % 2:s % 2 + 1]).then_inc(exped, 1)

            def out(n, m):
                b, half, c = m // 4, m // 2 % 2, m % 2
                act.wait_ge(summed, n * 8 + m + 1)
                nc.scalar.copy(hi[:, bass.ds((n * 2 + b) * 2 + c, 1), half * HALF:(half + 1) * HALF].rearrange("p o c -> p (o c)"),
                               o_ps[:, m % 4, :]).then_inc(hi_done, 1)

            with act.Fori(0, MH // 2) as n:
                exps(n, 0)
                for s in range(TILES):
                    if s + 1 < TILES:
                        exps(n, s + 1)
                    act.wait_ge(flipped, n * TILES + s + 1)
                    act.wait_ge(summed, n * 8 + (max(s // 4 - 1, 0)) * 2)
                    nc.scalar.copy(probT[:, s // 4 % 2, :, s % 4 * P:(s % 4 + 1) * P],
                                   t_ps[:, s % 2, 0:MT].rearrange("p (c t) -> p c t", c=2)).then_inc(copied, 1)
                    if s % 4 == 1 and s > 4:
                        out(n, s // 4 * 2 - 2)
                        out(n, s // 4 * 2 - 1)
                out(n, 6)
                out(n, 7)

        @block.vector
        def _(dve):
            def bias_of(n, s):
                dve.wait_ge(scored, n * TILES + s + 1)
                nc.vector.tensor_reduce(top[:, s % 2:s % 2 + 1], s_ps[:, s % 2, 0:MT], AX_X, ALU.max).then_inc(maxed, 1)
                dve.wait_ge(maxed, n * TILES + s + 1)
                nc.vector.tensor_scalar(bias[:, s % 2:s % 2 + 1], top[:, s % 2:s % 2 + 1], -SCALE, None,
                                        ALU.mult).then_inc(biased, 1)

            def out(n, m):
                b, half, c = m // 4, m // 2 % 2, m % 2
                dve.wait_ge(hi_done, n * 8 + m + 1)
                at = (slice(None), bass.ds((n * 2 + b) * 2 + c, 1), slice(half * HALF, (half + 1) * HALF))
                nc.vector.tensor_tensor(lo[at].rearrange("p o c -> p (o c)"), o_ps[:, m % 4, :],
                                        hi[at].bitcast(F32).rearrange("p o c -> p (o c)"),
                                        ALU.subtract).then_inc(lo_done, 1)

            with dve.Fori(0, MH // 2) as n:
                bias_of(n, 0)
                for s in range(TILES):
                    if s + 1 < TILES:
                        bias_of(n, s + 1)
                    dve.wait_ge(exped, n * TILES + s + 1)
                    nc.vector.reciprocal(rden[:, s % 2:s % 2 + 1], den[:, s % 2:s % 2 + 1]).then_inc(inverted, 1)
                    dve.wait_ge(inverted, n * TILES + s + 1)
                    nc.vector.tensor_scalar(prob[:, s % 2, :], prob[:, s % 2, :], rden[:, s % 2:s % 2 + 1], None,
                                            ALU.mult).then_inc(scaled, 1)
                    if s % 4 == 2 and s > 4:
                        out(n, s // 4 * 2 - 2)
                        out(n, s // 4 * 2 - 1)
                out(n, 6)
                out(n, 7)


def block_kernel(nc, a, out):
    f = {n: (v[0] if len(v.shape) > 1 and v.shape[0] == 1 and n not in ("ones_row",) else v) for n, v in a.items()}

    def scratch(name, shape):
        return nc.dram_tensor(name, shape, F32, kind="Internal").ap()

    x0, mem, dst = f["x"], f["mem"], out[0]
    x1, x2, x3 = scratch("x1", (T, D)), scratch("x2", (T, D)), scratch("x3", (T, D))
    projT = scratch("projT", (10 * P, T))
    z = scratch("z", (14 * P, T))
    rot_hi = nc.dram_tensor("rot_hi", (6 * P, T), F32, kind="Internal").ap()
    rot_lo = nc.dram_tensor("rot_lo", (6 * P, T), F32, kind="Internal").ap()
    v_tok = [scratch("v_slc", (T, P)), scratch("v_win", (T, P))]
    rv_tok = scratch("rv_tok", (T, RW))
    kc_hi = nc.dram_tensor("kc_hi", (64, 126), F32, kind="Internal").ap()
    kc_lo = nc.dram_tensor("kc_lo", (64, 126), F32, kind="Internal").ap()
    vc = scratch("vc", (63, P))
    o_nsa, y_rwkv = scratch("o_nsa", (T, RW)), scratch("y_rwkv", (T, RW))
    ops_dram = scratch("ops", (4, RW, T))
    qm, km = scratch("qm", (D, T)), scratch("km", (D, 256))

    core = Core(nc)

    def hidden_pair(ctx, name):
        return [sbuf(nc, ctx, f"{name}_{part}", [P, KD, T], F32R) for part in ("hi", "lo")]

    with ExitStack() as ctx:
        consts = make_consts(core, ctx, f["ident_"])

        def ffn(n, x_in, x_out):
            with ExitStack() as inner:
                hi, lo = hidden_pair(inner, f"ffn{n}")
                y = sbuf(nc, inner, f"ffn{n}_y", [P, TT, D])
                norm_transpose(core, f"n{n}", x_in, f[f"ffn{n}_pre_g"], TT, consts, hi, lo)
                ffn_products(core, f"f{n}", f[f"ffn{n}_w_gate"], f[f"ffn{n}_w_up"], f[f"ffn{n}_w_down"], hi, lo, y)
                residual(core, f"r{n}", x_in, y, f[f"ffn{n}_post_g"], 0.5, consts, x_out)
            core.clear()

        ffn(1, x0, x1)
        with ExitStack() as mixer:
            gates = sbuf(nc, mixer, "gates", [P, TT, 24])
            bonus = sbuf(nc, mixer, "bonus", [P, TT, 8])
            g_tok = sbuf(nc, mixer, "g_tok", [P, TT, RW])
            with ExitStack() as inner:
                hi, lo = hidden_pair(inner, "proj")
                norm_transpose(core, "nm", x1, f["mix_pre_g"], TT, consts, hi, lo)
                gate_product(core, "gp", f["w_in"], 10 * P, 24, hi, lo, gates)
                feature_product(core, "pn", f["w_in"], 0, 10, hi, lo, T, projT, 0)
                feature_product(core, "pr", f["w_in"], 10 * P + 24, 14, hi, lo, T, z, 0, mix=f["rwkv_mu"])
            core.clear()
            compress(core, "cp", projT, 4 * P, 5 * P, [f[f"cmp_{n}_k"] for n in ("pe", "w1", "w2")],
                     [f[f"cmp_{n}_v"] for n in ("pe", "w1", "w2")], f["ccos"], f["csin"], kc_hi, kc_lo, vc)
            rotate_and_turn(core, "rt", projT, f["cos_t"], f["sin_t"], [0, P, 2 * P, 3 * P, 6 * P, 8 * P],
                            rot_hi, rot_lo, [(projT, 7 * P), (projT, 9 * P)] + [(z, (8 + n) * P) for n in range(PAIRS)],
                            v_tok + [rv_tok[:, n * P:(n + 1) * P] for n in range(PAIRS)], consts)
            with ExitStack() as inner:
                end_decay = sbuf(nc, inner, "end_decay", [P, PAIRS, NCH])
                par = [f[f"rwkv_{n}"] for n in ("w0", "w2", "a0", "a2", "g2", "k_k", "k_a", "r_k")]
                rwkv_prepare(core, "rp", z, par, consts, f, ops_dram, end_decay, bonus, g_tok)
                core.clear()
                masks = load_masks(core, inner, f)
                attend_and_recur(core, "ar", rot_hi, rot_lo, kc_hi, kc_lo, v_tok, vc, gates, masks, o_nsa,
                                 ops_dram, rv_tok, end_decay, consts, f, y_rwkv)
            core.clear()
            with ExitStack() as inner:
                hi, lo = hidden_pair(inner, "mix")
                mix_transpose(core, "mt", o_nsa, y_rwkv, rv_tok, bonus, g_tok,
                              [f["nsa_out_g"], f["rwkv_gn_g"], f["rwkv_gn_b"]], consts, hi, lo)
                y = sbuf(nc, inner, "mix_y", [P, TT, D])
                token_product(core, "wo", f["w_out"], hi, lo, TT, y)
                residual(core, "rm", x1, y, f["mix_post_g"], 1.0, consts, x2)
            core.clear()

        with ExitStack() as outer:
            hi, lo = hidden_pair(outer, "mem")
            with ExitStack() as inner:
                v = sbuf(nc, inner, "mem_v", [P, 2, D])
                norm_transpose(core, "nk", mem, f["mem_kv_g"], 2, consts, hi, lo)
                feature_product(core, "pk", f["mem_wk"], 0, KD, hi, lo, 256, km, 0)
                token_product(core, "pv", f["mem_wv"], hi, lo, 2, v)
                norm_transpose(core, "nq", x2, f["mem_pre_g"], TT, consts, hi, lo)
                feature_product(core, "pq", f["mem_wq"], 0, KD, hi, lo, T, qm, 0)
                core.clear()
                memory_attention(core, "ma", qm, km, v, consts, hi, lo)
            y = sbuf(nc, outer, "mem_y", [P, TT, D])
            token_product(core, "mo", f["mem_wo"], hi, lo, TT, y)
            residual(core, "rq", x2, y, f["mem_post_g"], 1.0, consts, x3)
        core.clear()
        ffn(2, x3, dst)


_INS = ['x', 'mem',
        'ffn1_pre_g', 'ffn1_w_gate', 'ffn1_w_up', 'ffn1_w_down', 'ffn1_post_g',
        'mix_pre_g', 'w_in', 'cmp_pe_k', 'cmp_w1_k', 'cmp_w2_k', 'cmp_pe_v', 'cmp_w1_v', 'cmp_w2_v', 'nsa_out_g',
        'rwkv_mu', 'rwkv_w0', 'rwkv_w2', 'rwkv_a0', 'rwkv_a2', 'rwkv_g2', 'rwkv_k_k', 'rwkv_k_a', 'rwkv_r_k',
        'rwkv_gn_g', 'rwkv_gn_b', 'w_out', 'mix_post_g',
        'mem_pre_g', 'mem_kv_g', 'mem_wq', 'mem_wk', 'mem_wv', 'mem_wo', 'mem_post_g',
        'ffn2_pre_g', 'ffn2_w_gate', 'ffn2_w_up', 'ffn2_w_down', 'ffn2_post_g']


def kernel(**inputs):
    import numpy as _np
    import concourse.bacc as _bacc
    from concourse import mybir as _mybir
    from concourse.bass_utils import run_bass_kernel_spmd as _run

    nc = _bacc.Bacc("TRN2", target_bir_lowering=False, num_devices=1)
    arrays = {f"in_{n}": _np.ascontiguousarray(inputs[n]) for n in _INS}
    arrays.update({f"in_{n}": _np.ascontiguousarray(v) for n, v in shape_tables().items()})
    a = {n[3:]: nc.dram_tensor(n, v.shape, _mybir.dt.from_np(v.dtype), kind="ExternalInput").ap()
         for n, v in arrays.items()}
    out = nc.dram_tensor("out_0", (1, T, D), F32, kind="ExternalOutput").ap()
    block_kernel(nc, a, out)
    r = _run(nc, [arrays], core_ids=[0])
    return r.results[0]["out_0"]
```
